# Optimizing a Trainium2 kernel written in Bass

```python
import jax, jax.numpy as jnp
from jax import lax
import numpy as np
import math

D_MODEL = 1024
BATCH = 1
SEQ = 256
DEPTH = 2

GRID_W = 64
CTX_LEN = 256
Q_BLOCK = 128
ROPE_THETA = 10000.0
EPS = 1e-6
N_MOD = 6
MLA_HEADS = 8
MLA_NOPE = 64
MLA_ROPE = 32
MLA_V = 64
MLA_Q_RANK = 384
MLA_KV_RANK = 256
POOL_WINDOWS = (2, 4, 8, 16)
POOL_WIDTH = 512
POOL_GROUP = POOL_WIDTH // len(POOL_WINDOWS)
MIX0_IN = MLA_Q_RANK + MLA_KV_RANK + MLA_ROPE + POOL_WIDTH
MIX0_OUT = MLA_HEADS * MLA_V + POOL_WIDTH
GQA_HEADS = 8
GQA_KV_HEADS = 2
GQA_HEAD_DIM = 128
GQA_GROUP = GQA_HEADS // GQA_KV_HEADS
GQA_Q_W = GQA_HEADS * GQA_HEAD_DIM
GQA_KV_W = GQA_KV_HEADS * GQA_HEAD_DIM
D_FF = 2816
CONV_W = 3
N_EVEN = (DEPTH + 1) // 2
N_ODD = DEPTH // 2


def rms_norm(x, gain=None):
    xf = x.astype(jnp.float32)
    y = (xf * lax.rsqrt(jnp.mean(xf * xf, axis=-1, keepdims=True) + EPS)).astype(x.dtype)
    return y if gain is None else y * gain

def modulate(x, shift, scale):
    return rms_norm(x) * (1.0 + scale) + shift

def axial_rope_tables(n_tokens, rope_dim):
    rows = n_tokens // GRID_W
    row = jnp.repeat(jnp.arange(rows, dtype=jnp.float32), GRID_W)
    col = jnp.tile(jnp.arange(GRID_W, dtype=jnp.float32), rows)
    n_freq = rope_dim // 4
    freq = ROPE_THETA ** (-jnp.arange(n_freq, dtype=jnp.float32) / n_freq)
    ang = jnp.concatenate([row[:, None] * freq, col[:, None] * freq], axis=-1)
    return jnp.cos(ang), jnp.sin(ang)

def apply_rope(x, cos, sin):
    xr = x.reshape(x.shape[:-1] + (x.shape[-1] // 2, 2))
    x0, x1 = xr[..., 0], xr[..., 1]
    c = cos[None, :, None, :].astype(x.dtype)
    s = sin[None, :, None, :].astype(x.dtype)
    return jnp.stack([x0 * c - x1 * s, x0 * s + x1 * c], axis=-1).reshape(x.shape)

def attention(q, k, v):
    B, Nq, KV, G, Dh = q.shape
    blk = min(Q_BLOCK, Nq)
    qb = jnp.moveaxis(q.reshape(B, Nq // blk, blk, KV, G, Dh), 1, 0)
    scale = Dh ** -0.5

    def one_block(qi):
        s = jnp.einsum('bqhgd,bkhd->bhgqk', qi, k).astype(jnp.float32) * scale
        p = jax.nn.softmax(s, axis=-1).astype(v.dtype)
        return jnp.einsum('bhgqk,bkhd->bqhgd', p, v)

    o = lax.map(one_block, qb)
    return jnp.moveaxis(o, 0, 1).reshape(B, Nq, KV * G * v.shape[-1])

def multiscale_pool(p, w_pool, s_pool):
    B, T, C = p.shape
    cs = jnp.cumsum(p.astype(jnp.float32), axis=1)
    cs = jnp.concatenate([jnp.zeros((B, 1, C), jnp.float32), cs], axis=1)
    t = jnp.arange(T)
    outs = []
    for g, w in enumerate(POOL_WINDOWS):
        lo = jnp.clip(t - w // 2, 0, T)
        hi = jnp.clip(t - w // 2 + w, 0, T)
        csg = cs[:, :, g * POOL_GROUP:(g + 1) * POOL_GROUP]
        mean = (csg[:, hi] - csg[:, lo]) / (hi - lo).astype(jnp.float32)[None, :, None]
        d = mean.astype(p.dtype) - p[:, :, g * POOL_GROUP:(g + 1) * POOL_GROUP]
        outs.append(d @ w_pool[g])
    return jnp.concatenate(outs, axis=-1) * s_pool

def mla_q(cq, g_q, w_uq, cos, sin, rope):
    B, T, _ = cq.shape
    q = (rms_norm(cq, g_q) @ w_uq).reshape(B, T, MLA_HEADS, MLA_NOPE + MLA_ROPE)
    if rope:
        q = jnp.concatenate([q[..., :MLA_NOPE], apply_rope(q[..., MLA_NOPE:], cos, sin)], axis=-1)
    return q[:, :, :, None, :]

def mla_kv(ckv, kr, g_kv, w_uk, w_uv, cos, sin, rope):
    B, T, _ = ckv.shape
    ckv = rms_norm(ckv, g_kv)
    k_nope = (ckv @ w_uk).reshape(B, T, MLA_HEADS, MLA_NOPE)
    v = (ckv @ w_uv).reshape(B, T, MLA_HEADS, MLA_V)
    kr = kr[:, :, None, :]
    if rope:
        kr = apply_rope(kr, cos, sin)
    k = jnp.concatenate([k_nope, jnp.broadcast_to(kr, (B, T, MLA_HEADS, MLA_ROPE))], axis=-1)
    return k, v

def mla_pool_mixer(hc, hl, w_in, g_q, w_uq, g_kv, w_uk, w_uv, w_pool, s_pool, w_out, cos, sin, need_ctx):
    i_kv = MLA_Q_RANK
    i_kr = i_kv + MLA_KV_RANK
    i_p = i_kr + MLA_ROPE
    pl = hl @ w_in
    ql = mla_q(pl[..., :i_kv], g_q, w_uq, cos, sin, True)
    kl, vl = mla_kv(pl[..., i_kv:i_kr], pl[..., i_kr:i_p], g_kv, w_uk, w_uv, cos, sin, True)
    if need_ctx:
        pc = hc @ w_in
        qc = mla_q(pc[..., :i_kv], g_q, w_uq, cos, sin, False)
        kc, vc = mla_kv(pc[..., i_kv:i_kr], pc[..., i_kr:i_p], g_kv, w_uk, w_uv, cos, sin, False)
    else:
        pkv = hc @ w_in[:, i_kv:i_p]
        kc, vc = mla_kv(pkv[..., :MLA_KV_RANK], pkv[..., MLA_KV_RANK:], g_kv, w_uk, w_uv, cos, sin, False)
    al = attention(ql, jnp.concatenate([kc, kl], axis=1), jnp.concatenate([vc, vl], axis=1))
    ol = jnp.concatenate([al, multiscale_pool(pl[..., i_p:], w_pool, s_pool)], axis=-1) @ w_out
    oc = None
    if need_ctx:
        ac = attention(qc, kc, vc)
        oc = jnp.concatenate([ac, multiscale_pool(pc[..., i_p:], w_pool, s_pool)], axis=-1) @ w_out
    return oc, ol

def gqa_q(a, g_q, cos, sin, rope):
    B, T, _ = a.shape
    q = rms_norm(a.reshape(B, T, GQA_HEADS, GQA_HEAD_DIM), g_q)
    if rope:
        q = apply_rope(q, cos, sin)
    return q.reshape(B, T, GQA_KV_HEADS, GQA_GROUP, GQA_HEAD_DIM)

def gqa_kv(a, g_k, cos, sin, rope):
    B, T, _ = a.shape
    k = rms_norm(a[..., :GQA_KV_W].reshape(B, T, GQA_KV_HEADS, GQA_HEAD_DIM), g_k)
    v = a[..., GQA_KV_W:].reshape(B, T, GQA_KV_HEADS, GQA_HEAD_DIM)
    if rope:
        k = apply_rope(k, cos, sin)
    return k, v

def gqa_mixer(hc, hl, w_in, g_q, g_k, w_out, cos, sin, need_ctx):
    pl = hl @ w_in
    ql = gqa_q(pl[..., :GQA_Q_W], g_q, cos, sin, True)
    kl, vl = gqa_kv(pl[..., GQA_Q_W:], g_k, cos, sin, True)
    if need_ctx:
        pc = hc @ w_in
        qc = gqa_q(pc[..., :GQA_Q_W], g_q, cos, sin, False)
        kc, vc = gqa_kv(pc[..., GQA_Q_W:], g_k, cos, sin, False)
    else:
        kc, vc = gqa_kv(hc @ w_in[:, GQA_Q_W:], g_k, cos, sin, False)
    ol = attention(ql, jnp.concatenate([kc, kl], axis=1), jnp.concatenate([vc, vl], axis=1)) @ w_out
    oc = attention(qc, kc, vc) @ w_out if need_ctx else None
    return oc, ol

def conv_ffn(h, w_up, conv_w, conv_b, w_down):
    a = h @ w_up
    g, u = a[..., :D_FF], a[..., D_FF:]
    T = g.shape[1]
    half = CONV_W // 2
    gp = jnp.pad(g, ((0, 0), (half, half), (0, 0)))
    acc = conv_b + gp[:, 0:T] * conv_w[0]
    for j in range(1, CONV_W):
        acc = acc + gp[:, j:j + T] * conv_w[j]
    return (jax.nn.silu(acc) * u) @ w_down

def first_inputs(seed: int = 0) -> dict:
    key = jax.random.key(seed)
    ks = iter(jax.random.split(key, 32))
    D = D_MODEL

    def normal(shape, scale=1.0):
        return jax.random.normal(next(ks), shape, jnp.float32) * scale

    def gain(shape):
        return 1.0 + 0.05 * normal(shape)

    return {
        'x': normal((BATCH, SEQ, D)),
        'c': normal((BATCH, D)),
        'ctx': normal((BATCH, CTX_LEN, D)),
        'c_ctx': normal((D,)),
        'w_mod': normal((DEPTH, D, N_MOD * D), D ** -0.5),
        'b_mod': normal((DEPTH, N_MOD * D), 0.02),
        'mix0_w_in': normal((N_EVEN, D, MIX0_IN), D ** -0.5),
        'mla_g_q': gain((N_EVEN, MLA_Q_RANK)),
        'mla_w_uq': normal((N_EVEN, MLA_Q_RANK, MLA_HEADS * (MLA_NOPE + MLA_ROPE)), MLA_Q_RANK ** -0.5),
        'mla_g_kv': gain((N_EVEN, MLA_KV_RANK)),
        'mla_w_uk': normal((N_EVEN, MLA_KV_RANK, MLA_HEADS * MLA_NOPE), MLA_KV_RANK ** -0.5),
        'mla_w_uv': normal((N_EVEN, MLA_KV_RANK, MLA_HEADS * MLA_V), MLA_KV_RANK ** -0.5),
        'pool_w': normal((N_EVEN, len(POOL_WINDOWS), POOL_GROUP, POOL_GROUP), POOL_GROUP ** -0.5),
        'pool_scale': gain((N_EVEN, POOL_WIDTH)),
        'mix0_w_out': normal((N_EVEN, MIX0_OUT, D), MIX0_OUT ** -0.5),
        'gqa_w_in': normal((N_ODD, D, GQA_Q_W + 2 * GQA_KV_W), D ** -0.5),
        'gqa_g_q': gain((N_ODD, GQA_HEAD_DIM)),
        'gqa_g_k': gain((N_ODD, GQA_HEAD_DIM)),
        'gqa_w_out': normal((N_ODD, GQA_Q_W, D), GQA_Q_W ** -0.5),
        'ffn_w_up': normal((DEPTH, D, 2 * D_FF), D ** -0.5),
        'ffn_conv_w': normal((DEPTH, CONV_W, D_FF), CONV_W ** -0.5),
        'ffn_conv_b': normal((DEPTH, D_FF), 0.02),
        'ffn_w_down': normal((DEPTH, D_FF, D), D_FF ** -0.5),
        'g_final': gain((D,)),
    }

def first_block(x, c, ctx, c_ctx, w_mod, b_mod, mix0_w_in, mla_g_q, mla_w_uq, mla_g_kv, mla_w_uk, mla_w_uv,
              pool_w, pool_scale, mix0_w_out, gqa_w_in, gqa_g_q, gqa_g_k, gqa_w_out,
              ffn_w_up, ffn_conv_w, ffn_conv_b, ffn_w_down, g_final):
    B, N, D = x.shape
    cos_a, sin_a = axial_rope_tables(N, MLA_ROPE)
    cos_c, sin_c = axial_rope_tables(N, GQA_HEAD_DIM)
    xl, xc = x, ctx
    for i in range(DEPTH):
        last = i == DEPTH - 1
        j = i // 2
        ml = (jax.nn.silu(c) @ w_mod[i] + b_mod[i]).reshape(B, N_MOD, 1, D)
        mc = (jax.nn.silu(c_ctx) @ w_mod[i] + b_mod[i]).reshape(N_MOD, D)
        hl = modulate(xl, ml[:, 0], ml[:, 1])
        hc = modulate(xc, mc[0], mc[1])
        if i % 2 == 0:
            oc, ol = mla_pool_mixer(hc, hl, mix0_w_in[j], mla_g_q[j], mla_w_uq[j], mla_g_kv[j], mla_w_uk[j],
                                    mla_w_uv[j], pool_w[j], pool_scale[j], mix0_w_out[j], cos_a, sin_a, not last)
        else:
            oc, ol = gqa_mixer(hc, hl, gqa_w_in[j], gqa_g_q[j], gqa_g_k[j], gqa_w_out[j], cos_c, sin_c, not last)
        xl = xl + ml[:, 2] * ol
        xl = xl + ml[:, 5] * conv_ffn(modulate(xl, ml[:, 3], ml[:, 4]),
                                      ffn_w_up[i], ffn_conv_w[i], ffn_conv_b[i], ffn_w_down[i])
        if not last:
            xc = xc + mc[2] * oc
            xc = xc + mc[5] * conv_ffn(modulate(xc, mc[3], mc[4]),
                                       ffn_w_up[i], ffn_conv_w[i], ffn_conv_b[i], ffn_w_down[i])
    return rms_norm(xl, g_final)


DEPTH_2 = 1

DA_HEADS = 8
DA_HEAD_DIM = 64
DA_V_DIM = 2 * DA_HEAD_DIM
DA_QK_W = DA_HEADS * 2 * DA_HEAD_DIM
DA_V_W = DA_HEADS * DA_V_DIM
DIL_PAIRS = ((128, 1), (512, 4), (2048, 16))
DIL_HEADS_PER_GROUP = 4
DIL_HEADS = DIL_HEADS_PER_GROUP * len(DIL_PAIRS)
DIL_HEAD_DIM = 64
DIL_W = DIL_HEADS * DIL_HEAD_DIM
DIL_OUT_W = DIL_HEADS_PER_GROUP * DIL_HEAD_DIM
N_BRANCH = 2
IN_COLS = 2 * DA_QK_W + DA_V_W + 3 * DIL_W + N_BRANCH * D_MODEL
ROPE_THETA_2 = 500000.0
ROT_DIM = 16
NEG = -1e30


def rmsnorm(x, g):
    xf = x.astype(jnp.float32)
    y = xf * lax.rsqrt(jnp.mean(xf * xf, axis=-1, keepdims=True) + EPS)
    return (y * g.astype(jnp.float32)).astype(x.dtype)

def rope_tables(positions, dtype):
    inv = ROPE_THETA_2 ** (-(jnp.arange(0, ROT_DIM, 2, dtype=jnp.float32) / ROT_DIM))
    ang = positions.astype(jnp.float32)[..., None] * inv
    return jnp.cos(ang)[:, :, None, :].astype(dtype), jnp.sin(ang)[:, :, None, :].astype(dtype)

def partial_rope(t, cos, sin):
    half = ROT_DIM // 2
    t1, t2, tp = t[..., :half], t[..., half:ROT_DIM], t[..., ROT_DIM:]
    return jnp.concatenate([t1 * cos - t2 * sin, t2 * cos + t1 * sin, tp], axis=-1)

def swiglu(h, w_gu, w_down):
    g, u = jnp.split(h @ w_gu, 2, axis=-1)
    return (jax.nn.silu(g) * u) @ w_down

def diff_attention(q, k, v, lam):
    B, S, H, _, dh = q.shape
    nblk = S // Q_BLOCK
    scale = 1.0 / math.sqrt(dh)
    qb = q.reshape(B, nblk, Q_BLOCK, H, 2, dh).transpose(1, 0, 2, 3, 4, 5)

    def block(qblk):
        s = jnp.einsum('bqhcd,bkhcd->bhcqk', qblk, k, preferred_element_type=jnp.float32) * scale
        p = jax.nn.softmax(s, axis=-1)
        a = p[:, :, 0] - lam * p[:, :, 1]
        return jnp.einsum('bhqk,bkhe->bqhe', a.astype(v.dtype), v,
                          preferred_element_type=jnp.float32).astype(v.dtype)

    o = lax.map(block, qb)
    return o.transpose(1, 0, 2, 3, 4).reshape(B, S, H, 2 * dh)

def dilated_window_attention(q, k, v, dil, half):
    B, S, Hg, dh = q.shape
    L = S // dil
    N = B * dil
    blk = half
    nb = -(-L // blk)
    Lp = nb * blk
    scale = 1.0 / math.sqrt(dh)

    def fold(t):
        return t.reshape(B, L, dil, Hg, dh).transpose(0, 2, 1, 3, 4).reshape(N, L, Hg, dh)

    qf, kf, vf = fold(q), fold(k), fold(v)
    qb = jnp.pad(qf, ((0, 0), (0, Lp - L), (0, 0), (0, 0))).reshape(N, nb, blk, Hg, dh)

    def ctx(t):
        tp = jnp.pad(t, ((0, 0), (blk, Lp - L + blk), (0, 0), (0, 0))).reshape(N, nb + 2, blk, Hg, dh)
        return jnp.concatenate([tp[:, :-2], tp[:, 1:-1], tp[:, 2:]], axis=2)

    kc, vc = ctx(kf), ctx(vf)
    s = jnp.einsum('nbqhd,nbkhd->nbhqk', qb, kc, preferred_element_type=jnp.float32) * scale
    qpos = jnp.arange(nb)[:, None] * blk + jnp.arange(blk)[None, :]
    kpos = (jnp.arange(nb)[:, None] - 1) * blk + jnp.arange(3 * blk)[None, :]
    valid = ((jnp.abs(kpos[:, None, :] - qpos[:, :, None]) <= half)
             & (kpos >= 0)[:, None, :] & (kpos < L)[:, None, :])
    s = jnp.where(valid[None, :, None], s, NEG)
    m = jnp.max(s, axis=-1, keepdims=True)
    e = jnp.exp(s - m)
    l = jnp.sum(e, axis=-1)
    o = jnp.einsum('nbhqk,nbkhd->nbqhd', e.astype(v.dtype), vc, preferred_element_type=jnp.float32)
    o = o / l.transpose(0, 1, 3, 2)[..., None]
    lse = (m[..., 0] + jnp.log(l)).transpose(0, 1, 3, 2)

    def unfold(t):
        t = t.reshape((N, Lp) + t.shape[3:])[:, :L]
        t = t.reshape((B, dil, L) + t.shape[2:])
        return jnp.swapaxes(t, 1, 2).reshape((B, S) + t.shape[3:])

    return unfold(o).astype(q.dtype), unfold(lse)

def second_inputs(seed: int = 0) -> dict:
    key = jax.random.key(seed)
    ks = jax.random.split(key, 24)
    f32 = jnp.float32

    def w(k, shape, fan_in):
        return jax.random.normal(k, shape, f32) * fan_in ** -0.5

    def gain(k, shape):
        return 1.0 + 0.05 * jax.random.normal(k, shape, f32)

    return {
        "x": jax.random.normal(ks[0], (BATCH, SEQ, D_MODEL), f32),
        "positions": jnp.broadcast_to(jnp.arange(SEQ, dtype=jnp.int32), (BATCH, SEQ)),
        "w_in": w(ks[1], (DEPTH_2, D_MODEL, IN_COLS), D_MODEL),
        "lambda_q1": 0.1 * jax.random.normal(ks[2], (DEPTH_2, DA_HEAD_DIM), f32),
        "lambda_k1": 0.1 * jax.random.normal(ks[3], (DEPTH_2, DA_HEAD_DIM), f32),
        "lambda_q2": 0.1 * jax.random.normal(ks[4], (DEPTH_2, DA_HEAD_DIM), f32),
        "lambda_k2": 0.1 * jax.random.normal(ks[5], (DEPTH_2, DA_HEAD_DIM), f32),
        "g_subln": gain(ks[6], (DEPTH_2, DA_V_DIM)),
        "w_proj_a": w(ks[7], (DEPTH_2, DA_V_W, D_MODEL), DA_V_W),
        "w_proj_b": w(ks[8], (DEPTH_2, DIL_OUT_W, D_MODEL), DIL_OUT_W),
        "w_out": w(ks[9], (DEPTH_2, D_MODEL, D_MODEL), D_MODEL),
        "w_gu1": w(ks[10], (DEPTH_2, D_MODEL, 2 * D_FF), D_MODEL),
        "w_down1": w(ks[11], (DEPTH_2, D_FF, D_MODEL), D_FF),
        "w_gu2": w(ks[12], (DEPTH_2, D_MODEL, 2 * D_FF), D_MODEL),
        "w_down2": w(ks[13], (DEPTH_2, D_FF, D_MODEL), D_FF),
        "g_pre_ffn1": gain(ks[14], (DEPTH_2, D_MODEL)),
        "g_post_ffn1": gain(ks[15], (DEPTH_2, D_MODEL)),
        "g_pre_mix": gain(ks[16], (DEPTH_2, D_MODEL)),
        "g_post_mix": gain(ks[17], (DEPTH_2, D_MODEL)),
        "g_pre_ffn2": gain(ks[18], (DEPTH_2, D_MODEL)),
        "g_post_ffn2": gain(ks[19], (DEPTH_2, D_MODEL)),
    }

def second_block(x, positions, w_in, lambda_q1, lambda_k1, lambda_q2, lambda_k2, g_subln,
              w_proj_a, w_proj_b, w_out, w_gu1, w_down1, w_gu2, w_down2,
              g_pre_ffn1, g_post_ffn1, g_pre_mix, g_post_mix, g_pre_ffn2, g_post_ffn2):
    B, S, D = x.shape
    cos, sin = rope_tables(positions, x.dtype)
    cuts = [int(c) for c in np.cumsum([DA_QK_W, DA_QK_W, DA_V_W, DIL_W, DIL_W, DIL_W, D_MODEL])]

    for l in range(DEPTH_2):
        lambda_init = 0.8 - 0.6 * math.exp(-0.3 * l)

        h = rmsnorm(x, g_pre_ffn1[l])
        x = x + 0.5 * rmsnorm(swiglu(h, w_gu1[l], w_down1[l]), g_post_ffn1[l])

        h = rmsnorm(x, g_pre_mix[l])
        z = h @ w_in[l]
        qa, ka, va, qd, kd, vd, ga, gb = jnp.split(z, cuts, axis=-1)

        qa = partial_rope(qa.reshape(B, S, 2 * DA_HEADS, DA_HEAD_DIM), cos, sin)
        ka = partial_rope(ka.reshape(B, S, 2 * DA_HEADS, DA_HEAD_DIM), cos, sin)
        qa = qa.reshape(B, S, DA_HEADS, 2, DA_HEAD_DIM)
        ka = ka.reshape(B, S, DA_HEADS, 2, DA_HEAD_DIM)
        va = va.reshape(B, S, DA_HEADS, DA_V_DIM)
        lam = (jnp.exp(jnp.dot(lambda_q1[l], lambda_k1[l]).astype(jnp.float32))
               - jnp.exp(jnp.dot(lambda_q2[l], lambda_k2[l]).astype(jnp.float32)) + lambda_init)
        oa = diff_attention(qa, ka, va, lam)
        oa = (rmsnorm(oa, g_subln[l]) * (1.0 - lambda_init)).reshape(B, S, DA_V_W)

        qd = partial_rope(qd.reshape(B, S, DIL_HEADS, DIL_HEAD_DIM), cos, sin)
        kd = partial_rope(kd.reshape(B, S, DIL_HEADS, DIL_HEAD_DIM), cos, sin)
        vd = vd.reshape(B, S, DIL_HEADS, DIL_HEAD_DIM)
        outs, lses = [], []
        for gi, (win, dil) in enumerate(DIL_PAIRS):
            hs = slice(gi * DIL_HEADS_PER_GROUP, (gi + 1) * DIL_HEADS_PER_GROUP)
            o_g, lse_g = dilated_window_attention(qd[:, :, hs], kd[:, :, hs], vd[:, :, hs],
                                                  dil, win // (2 * dil))
            outs.append(o_g)
            lses.append(lse_g)
        wts = jax.nn.softmax(jnp.stack(lses, axis=0), axis=0)
        od = jnp.sum(wts[..., None].astype(x.dtype) * jnp.stack(outs, axis=0), axis=0)
        od = od.reshape(B, S, DIL_OUT_W)

        merged = jax.nn.sigmoid(ga) * (oa @ w_proj_a[l]) + jax.nn.sigmoid(gb) * (od @ w_proj_b[l])
        x = x + rmsnorm(merged @ w_out[l], g_post_mix[l])

        h = rmsnorm(x, g_pre_ffn2[l])
        x = x + 0.5 * rmsnorm(swiglu(h, w_gu2[l], w_down2[l]), g_post_ffn2[l])

    return x


def setup_inputs(seed=0):
    out = dict(first_inputs(seed))
    for name, value in second_inputs(seed + 1).items():
        if name != "x":
            out[name + "_2"] = value
    return out


def reference(
    x, c, ctx, c_ctx, w_mod, b_mod, mix0_w_in, mla_g_q, mla_w_uq, mla_g_kv, mla_w_uk, mla_w_uv,
    pool_w, pool_scale, mix0_w_out, gqa_w_in, gqa_g_q, gqa_g_k, gqa_w_out, ffn_w_up, ffn_conv_w,
    ffn_conv_b, ffn_w_down, g_final, positions_2, w_in_2, lambda_q1_2, lambda_k1_2, lambda_q2_2,
    lambda_k2_2, g_subln_2, w_proj_a_2, w_proj_b_2, w_out_2, w_gu1_2, w_down1_2, w_gu2_2,
    w_down2_2, g_pre_ffn1_2, g_post_ffn1_2, g_pre_mix_2, g_post_mix_2, g_pre_ffn2_2,
    g_post_ffn2_2,
):
    x = first_block(
        x, c, ctx, c_ctx, w_mod, b_mod, mix0_w_in, mla_g_q, mla_w_uq, mla_g_kv, mla_w_uk,
        mla_w_uv, pool_w, pool_scale, mix0_w_out, gqa_w_in, gqa_g_q, gqa_g_k, gqa_w_out,
        ffn_w_up, ffn_conv_w, ffn_conv_b, ffn_w_down, g_final,
    )
    return second_block(
        x, positions_2, w_in_2, lambda_q1_2, lambda_k1_2, lambda_q2_2, lambda_k2_2, g_subln_2,
        w_proj_a_2, w_proj_b_2, w_out_2, w_gu1_2, w_down1_2, w_gu2_2, w_down2_2, g_pre_ffn1_2,
        g_post_ffn1_2, g_pre_mix_2, g_post_mix_2, g_pre_ffn2_2, g_post_ffn2_2,
    )


_drawn_inputs = setup_inputs


def setup_inputs(seed=0):
    import zlib

    import numpy as np

    out = dict(_drawn_inputs(seed))
    spreads = {}
    factors = {'mla_g_q': 8.0,
     'mla_g_kv': 2.669,
     'gqa_g_q': 8.0,
     'gqa_g_k': 8.0,
     'ffn_conv_b': 3.477,
     'lambda_q1_2': 29.016,
     'lambda_k1_2': 56.424,
     'lambda_q2_2': 200.0,
     'lambda_k2_2': 3.51,
     'g_post_ffn2_2': 3.256}
    for name, (base, spread) in spreads.items():
        noise = np.random.default_rng([zlib.crc32(name.encode()), seed]).standard_normal(out[name].shape)
        drawn = base * np.exp(spread * noise) if base else spread * noise
        out[name] = __import__('jax').numpy.asarray(drawn.astype(out[name].dtype))
    for name, factor in factors.items():
        out[name] = (out[name] * factor).astype(out[name].dtype)
    return out
```

```python
from contextlib import ExitStack

import numpy as np
import concourse.bass as bass
from concourse import mybir

F32 = mybir.dt.float32
F32R = mybir.dt.float32r
I32 = mybir.dt.int32
ALU = mybir.AluOpType
ACT = mybir.ActivationFunctionType
AX = mybir.AxisListType

P = 128
D = 1024
KD = D // P
T = 256
TT = 2 * T
EPS = 1e-6
FF = 2816
NFF = FF // P
PAIRS = NFF // 2
STRIPE = 2048
RING = 3

MLA_H, NOPE, ROPE, MLA_QK = 8, 64, 32, 96
QR, KVR = 384, 256
MLA_SCALE = float(MLA_QK) ** -0.5
GQA_SCALE = 128.0 ** -0.5
B2_SCALE = 0.125
LAMBDA_INIT = 0.2
DIL_OUT = 4
WINDOWS = (2, 4, 8, 16)
PAD = 8
NEG = -1e30


def stripes():
    out, at = [], {}

    def add(stage, items):
        at[stage] = len(out)
        out.extend(items)

    def columns(name, layer, starts):
        return [(name, layer, "cols", c) for c in starts]

    def ffn(up, down, layer):
        g = [(up, layer, "cols", 256 * j) for j in range(PAIRS)]
        u = [(up, layer, "cols", FF + 256 * j) for j in range(PAIRS)]
        d = [(down, layer, "rows", 256 * j) for j in range(PAIRS)]
        order = [g[0], u[0]]
        for j in range(1, PAIRS):
            order += [g[j], u[j], d[j - 1]]
        return order + [d[-1]]

    add("mix_in", columns("mix0_w_in", 0, (0, 256, 512, 672, 928)))
    add("mix_out", columns("mix0_w_out", 0, range(0, D, 256)))
    add("ffn0", ffn("ffn_w_up", "ffn_w_down", 0))
    add("gqa_in", columns("gqa_w_in", 0, range(0, 1536, 256)))
    add("gqa_out", columns("gqa_w_out", 0, range(0, D, 256)))
    add("ffn1", ffn("ffn_w_up", "ffn_w_down", 1))
    add("ffn2", ffn("w_gu1_2", "w_down1_2", 0))
    qk = [*range(0, 2048, 256), *range(3072, 3840, 256), *range(3840, 4608, 256)]
    v = [*range(2048, 3072, 256), *range(4608, 5376, 256)]
    add("qkv", columns("w_in_2", 0, qk + v))
    add("proj", [x for s in range(4) for x in
                 (("w_proj_a_2", 0, "cols", 256 * s), ("w_in_2", 0, "cols", 5376 + 256 * s))]
        + [("w_proj_b_2", 0, "rows", 0)] + columns("w_in_2", 0, range(6400, 7424, 256)))
    add("w_out", columns("w_out_2", 0, range(0, D, 256)))
    add("ffn3", ffn("w_gu2_2", "w_down2_2", 0))
    return out, at


STRIPES, AT = stripes()


def need(eng, sem, value):
    if isinstance(value, int) and value <= 0:
        return
    eng.wait_ge(sem, value)


def build(nc, a, out):
    ctx = ExitStack()
    with ctx:
        def sem(name):
            return ctx.enter_context(nc.semaphore(name))

        def sb(name, shape, dt=F32):
            return ctx.enter_context(nc.sbuf_tensor(name, shape, dt))

        w_raw = sb("w_raw", [P, RING, STRIPE])
        w_hi = sb("w_hi", [P, RING, STRIPE], F32R)
        w_lo = sb("w_lo", [P, RING, STRIPE], F32R)
        X = sb("X", [P, KD, TT])
        h_at = nc.sbuf_base
        h_hi = sb("h_hi", [P, KD, TT], F32R)
        h_lo = sb("h_lo", [P, KD, TT], F32R)
        mod_early_ring = nc.alloc_sbuf_tensor_at("mod_early_ring", [P, 4, STRIPE], F32, offset=h_at)
        scr = sb("scr", [P, 6, TT])
        std = sb("std", [P, TT])
        rinv = sb("rinv", [P, TT])
        const = sb("const", [P, 5 * P + 8])
        par = sb("par", [P, 4, P])
        mod = sb("mod", [P, 2, 48, 2])
        mod1 = sb("mod1", [P, 2, 2, 8, 2])
        silu_all = sb("silu_all", [P, 2 * KD + 30])
        silu_c = silu_all[:, 0:2 * KD].rearrange("p (k s) -> p k s", s=2)
        small = sb("small", [P, 64])
        small_w = sb("small_w", [P, 8])
        ident, ones = const[:, 0:P], const[:, P:2 * P]
        rot_mla, rot_gqa, rot_b2 = (const[:, i * P:(i + 1) * P] for i in (2, 3, 4))
        inv_freq = const[:, 5 * P:5 * P + 1]
        eps, eps_down = small_w[:, 0:1], small_w[:, 1:2]

        U = sb("U", [P, 14720])
        u2_at = nc.sbuf_base
        U2 = sb("U2", [P, 2112])
        a_hi = nc.alloc_sbuf_tensor_at("a_hi", [P, 2, TT], F32R, offset=u2_at)
        a_lo = nc.alloc_sbuf_tensor_at("a_lo", [P, 2, TT], F32R, offset=u2_at + 8 * TT)

        def view(at, *shape):
            n = int(np.prod(shape))
            v = U[:, at:at + n]
            names = "abcd"[:len(shape)]
            if len(shape) == 1:
                return v
            return v.rearrange(f"p ({' '.join(names)}) -> p {' '.join(names)}",
                               **{names[i]: shape[i] for i in range(1, len(shape))})

        ctx_rows = view(5632, 2, D)
        lat_rows = U2[:, 0:2 * D].rearrange("p (t n) -> p t n", t=2)
        mod_ring = view(0, 2, STRIPE)
        mod_rows = view(5120, TT)
        q_mla = view(0, 2, TT)
        k_mla = view(1024, 2, TT)
        v_mla = view(2048, 4, 512)
        pt_mla = view(4096, 1536)
        w_uv = view(4096, 2, 512)
        cq = view(5632, 3, TT)
        ckv = view(7168, 2, TT)
        w_uq = view(8192, 3, 768)
        w_uk = view(10496, 2, 512)
        w_pool = view(11520, 4, P)
        pool_p = view(12032, 4, 2, T + 2 * PAD)
        tab_mla = view(14208, 2, T)
        pool_inv = U2[:, 0:1024].rearrange("p (g t) -> p g t", g=4)
        pool_a = U2[:, 1024:1568].rearrange("p (s t) -> p s t", s=2)
        pool_b = U2[:, 1568:2112].rearrange("p (s t) -> p s t", s=2)
        f_act = view(4096, 2, TT)
        q_gqa = view(5632, 8, T)
        k_gqa = view(7680, 2, TT)
        v_gqa = view(8704, 4, T)
        g_tmp = view(9728, 2, TT)
        tab_gqa = view(10752, 2, T)
        pt_gqa = view(4096, 1024)
        pt_b2 = view(0, 1536)
        t_rope = view(0, 2, TT)
        qa = view(1536, 8, T)
        ka = view(5120, 8, T)
        yb = ka
        qd = view(3584, 6, T)
        kd = view(7168, 6, T)
        va = view(8704, 2, D)
        vd = view(10752, 2, 768)
        tab_b2 = view(12288, 2, T)
        dil_mask = view(12800, 4, T)
        pos_i = view(13824, T)
        sgate = view(0, 2, TT)
        out_rows = view(8704, 2, D)
        par_rows = std[:, :].rearrange("p (n c) -> p n c", c=P)
        lam_rows = view(14080, 4, 64)
        row_max, row_neg, row_sum, row_inv = (
            small[:, 8 * i:8 * i + 8].rearrange("p (h r) -> p h r", h=2) for i in range(4))
        lam, g_sub = small[:, 32:40], small[:, 40:41]

        psum = ctx.enter_context(nc.psum_tensor("psum", [P, 8, TT], F32))

        def bank2(b):
            return psum[:, b, :].rearrange("p (s t) -> p s t", s=2)

        raw_in = [sem(f"raw_in{i}") for i in range(RING)]
        hi_made, lo_made = sem("hi_made"), sem("lo_made")
        stripe_started = sem("stripe_started")
        base_in, rows_in, par_in, small_in = (sem(n) for n in ("base_in", "rows_in", "par_in", "small_in"))
        tab_in, inv_in, b2_in, fill = (sem(n) for n in ("tab_in", "inv_in", "b2_in", "fill"))
        x_turned, x_in, par_turned, par_ready = (sem(n) for n in ("x_turned", "x_in", "par_turned", "par_ready"))
        c_ready = sem("c_ready")
        mod_in = [sem(f"mod_in{i}") for i in range(2)]
        mod_early = [sem(f"mod_early{i}") for i in range(4)]
        mod_stripes, mod_rows_in, mod_turned, mod_ready, mod1_ready = (
            sem(n) for n in ("mod_stripes", "mod_rows_in", "mod_turned", "mod_ready", "mod1_ready"))
        n_sq, n_ss, n_std, n_rinv, n_t, n_hi, n_lo, n_x = (
            sem(n) for n in ("n_sq", "n_ss", "n_std", "n_rinv", "n_t", "n_hi", "n_lo", "n_x"))
        mi_sums, mi_sq, mi_ss, mi_evac, mi_std, mi_fix, mi_rot = (
            sem(n) for n in ("mi_sums", "mi_sq", "mi_ss", "mi_evac", "mi_std", "mi_fix", "mi_rot"))
        v_sums, v_evac = sem("v_sums"), sem("v_evac")
        q_sums, k_sums, q_rot, q_copied, k_copied, q_roped = (
            sem(n) for n in ("q_sums", "k_sums", "q_rot", "q_copied", "k_copied", "q_roped"))
        at_s, at_mx, at_e, at_rs, at_pn, at_t, at_pt, at_o, at_hi, at_lo = (
            sem(n) for n in ("at_s", "at_mx", "at_e", "at_rs", "at_pn", "at_t", "at_pt", "at_o", "at_hi", "at_lo"))
        pool_pads, pool_seq, pool_d, pool_sums, pool_hi, pool_lo = (
            sem(n) for n in ("pool_pads", "pool_seq", "pool_d", "pool_sums", "pool_hi", "pool_lo"))
        o_sums, o_evac = sem("o_sums"), sem("o_evac")
        f_g, f_u, f_d, f_mid, f_left, f_conv, f_silu, f_prod, f_ahi, f_alo, f_x = (
            sem(n) for n in ("f_g", "f_u", "f_d", "f_mid", "f_left", "f_conv", "f_silu", "f_prod",
                             "f_ahi", "f_alo", "f_x"))
        gi_sums, gi_evac, gi_sq, gi_rot, gi_std, gi_fix = (
            sem(n) for n in ("gi_sums", "gi_evac", "gi_sq", "gi_rot", "gi_std", "gi_fix"))
        tb_seq, tb_ang, tb_sin = sem("tb_seq"), sem("tb_ang"), sem("tb_sin")
        r_sums, r_evac, r_rot, r_fix = (sem(n) for n in ("r_sums", "r_evac", "r_rot", "r_fix"))
        d_clip, d_copied, d_sq, d_ss, d_std, d_t, d_rinv, d_hi, d_lo = (
            sem(n) for n in ("d_clip", "d_copied", "d_sq", "d_ss", "d_std", "d_t", "d_rinv", "d_hi", "d_lo"))
        p_sums, p_sig, p_m, p_hi, p_lo = (sem(n) for n in ("p_sums", "p_sig", "p_m", "p_hi", "p_lo"))
        y_turned, y_rows, stored = sem("y_turned"), sem("y_rows"), sem("stored")

        NORMS = [(TT, "mod", 0, 1, 0), (TT, "mod", 0, 4, 3), (TT, "mod", 1, 1, 0), (T, "mod", 1, 4, 3),
                 (T, "final", 0, 0, 0), (T, "gain", 8, 0, 0), (T, "post", 16, 0, 0), (T, "gain", 24, 0, 0),
                 (T, "post", 32, 0, 0), (T, "gain", 40, 0, 0), (T, "post", 48, 0, 0)]

        def chunks(n):
            return KD if NORMS[n][0] == TT else KD // 2

        def chunks_before(n, kinds=("mod", "final", "gain", "post")):
            return sum(chunks(i) for i in range(n) if NORMS[i][1] in kinds)

        def h_count(n, tile):
            per = KD // chunks(n)
            return chunks_before(n, ("mod", "gain")) + tile // per + 1

        def blocks(n, c):
            return [(c, 0), (c, 1)] if NORMS[n][0] == TT else [(2 * c, 1), (2 * c + 1, 1)]

        def chunk_of(t, n, c):
            if NORMS[n][0] == TT:
                return t[:, c, :].rearrange("p (s t) -> p s t", s=2)
            return t[:, 2 * c:2 * c + 2, T:TT]

        def block_cols(s):
            return slice(s * T, (s + 1) * T)

        def load(sp, i, src, n=0):
            if i >= RING:
                sp.wait_ge(lo_made, i - RING + 1 + 3 * n)
            parts = 2 if src.shape[2] == D else 8
            sp.dma_start(w_raw[:, i % RING, :].rearrange("p (k n) -> p k n", k=parts),
                         src).then_inc(raw_in[i % RING], 16)

        def stripe_source(i):
            name, layer, kind, start = STRIPES[i]
            if kind == "cols":
                return a[name][layer].rearrange("(k p) n -> p k n", p=P)[:, :, start:start + 256]
            return a[name][layer].rearrange("(k p) n -> p k n", p=P)[:, start // P:start // P + 2, :]

        def split_hi(act, i, n=0):
            act.wait_ge(raw_in[i % RING], 16 * (i // RING + 1) + 16 * n)
            if i >= RING:
                act.wait_ge(stripe_started, i - RING + 2 + 3 * n)
            nc.scalar.activation(w_hi[:, i % RING, :], w_raw[:, i % RING, :], ACT.Copy).then_inc(hi_made, 1)

        def split_lo(dve, i, n=0):
            dve.wait_ge(hi_made, i + 1 + 3 * n)
            nc.vector.tensor_tensor(w_lo[:, i % RING, :], w_raw[:, i % RING, :],
                                    w_hi[:, i % RING, :].bitcast(F32), ALU.subtract).then_inc(lo_made, 1)

        def ahead_hi(act, i, n=0):
            if not isinstance(n, int) or i + 2 + 3 * n < len(STRIPES):
                split_hi(act, i + 2, n)

        def ahead_lo(dve, i, n=0):
            if not isinstance(n, int) or i + 2 + 3 * n < len(STRIPES):
                split_lo(dve, i + 2, n)

        def begin_stripe(pe, i, n=0):
            pe.wait_ge(lo_made, i + 1 + 3 * n)

        def three(dst, weight, moving, start, stop, swap=False):
            (wh, wl), (mh, ml) = weight, moving
            pairs = ((mh, wh), (ml, wh), (mh, wl)) if swap else ((wh, mh), (wh, ml), (wl, mh))
            return [nc.tensor.matmul(dst, x, y, start=start and q == 0, stop=stop and q == 2,
                                     skip_group_check=True) for q, (x, y) in enumerate(pairs)]

        def product(pe, dst, i, col, acts, first, done=None, tiles=KD, pitch=256, ready=None):
            slot = i % RING
            for k in range(tiles):
                if ready is not None:
                    ready(k)
                c = k * pitch + col
                made = three(dst, (w_hi[:, slot, c:c + P], w_lo[:, slot, c:c + P]), acts(k),
                             k == 0, k == tiles - 1)
                if first and k == 0:
                    made[0].then_inc(stripe_started, 1)
            if done is not None:
                made[-1].then_inc(done, 1)

        def product_rows(pe, dst, i, acts, first, start, done=None):
            slot = i % RING
            for k in range(KD):
                made = three(dst, (w_hi[:, slot, k * 256:(k + 1) * 256], w_lo[:, slot, k * 256:(k + 1) * 256]),
                             acts(k), start and k == 0, k == KD - 1, swap=True)
                if first and k == 0:
                    made[0].then_inc(stripe_started, 1)
            if done is not None:
                made[-1].then_inc(done, 1)

        def h_cols(lo, hi):
            return lambda k: (h_hi[:, k, lo:hi], h_lo[:, k, lo:hi])

        def h_ready(pe, n):
            return lambda k: pe.wait_ge(n_lo, h_count(n, k))

        def norm_bank(n):
            return 0 if n in (2, 4, 6, 10) else 6

        def norm_scalar(act, n, src, ready):
            tokens, kind, layer, _, shift = NORMS[n]
            sq0, h0 = chunks_before(n), chunks_before(n, ("mod", "gain"))
            for c in range(chunks(n)):
                need(act, *ready(c))
                need(act, n_ss, sq0 + c - 2)
                nc.scalar.activation(scr[:, 3 + c % 3, :].rearrange("p (s t) -> p s t", s=2), src(c),
                                     ACT.Square).then_inc(n_sq, 1)
            act.wait_ge(n_ss, sq0 + chunks(n))
            if n:
                act.wait_ge(n_rinv, n)
            nc.scalar.activation(std[:, 0:tokens], psum[:, norm_bank(n), 0:tokens], ACT.Sqrt, bias=eps,
                                 scale=1.0 / D).then_inc(n_std, 1)
            if kind in ("mod", "gain"):
                for c in range(chunks(n)):
                    act.wait_ge(n_t, sq0 + c + 1)
                    t = scr[:, c % 3, :].rearrange("p (s t) -> p s t", s=2)
                    if kind == "gain":
                        nc.scalar.activation(chunk_of(h_hi, n, c), t, ACT.Copy).then_inc(n_hi, 1)
                        continue
                    for b, (m, s) in enumerate(blocks(n, c)):
                        made = nc.scalar.activation(h_hi[:, m, block_cols(s)], t[:, b, :], ACT.Identity,
                                                    bias=mod[:, layer, 8 * shift + m, s:s + 1])
                    made.then_inc(n_hi, 1)

        def norm_tensor(pe, n):
            tokens = NORMS[n][0]
            sq0 = chunks_before(n)
            for c in range(chunks(n)):
                pe.wait_ge(n_sq, sq0 + c + 1)
                sq = scr[:, 3 + c % 3, :]
                for b in range(1 if tokens == TT else 2):
                    made = nc.tensor.matmul(psum[:, norm_bank(n), 0:tokens], ones, sq[:, b * T:b * T + tokens],
                                            start=c == 0 and b == 0,
                                            stop=c == chunks(n) - 1 and (tokens == TT or b == 1))
                made.then_inc(n_ss, 1)

        def norm_vector(dve, n, src, factor=1.0):
            tokens, kind, first, scale, shift = NORMS[n]
            sq0, h0 = chunks_before(n), chunks_before(n, ("mod", "gain"))
            dve.wait_ge(n_std, n + 1)
            nc.vector.reciprocal(rinv[:, 0:tokens], std[:, 0:tokens]).then_inc(n_rinv, 1)
            dve.wait_ge(n_rinv, n + 1)

            def scaled(c):
                t = scr[:, c % 3, :].rearrange("p (s t) -> p s t", s=2)
                for b, (m, s) in enumerate(blocks(n, c)):
                    if kind == "mod":
                        g = mod1[:, first, scale // 4, m, s:s + 1]
                    else:
                        g = par[:, 3, first + m:first + m + 1]
                    x = src(c)[:, b, :]
                    dst = t[:, b, :] if kind in ("mod", "gain") else x
                    r = rinv[:, block_cols(s)] if tokens == TT else rinv[:, 0:T]
                    made = nc.vector.scalar_tensor_tensor(out=dst, in0=x, scalar=g, in1=r,
                                                          op0=ALU.mult, op1=ALU.mult)
                made.then_inc(n_t, 1)

            def remainder(c):
                dve.wait_ge(n_hi, h0 + c + 1)
                t = scr[:, c % 3, :].rearrange("p (s t) -> p s t", s=2)
                if kind == "gain":
                    nc.vector.tensor_tensor(chunk_of(h_lo, n, c), t, chunk_of(h_hi, n, c).bitcast(F32),
                                            ALU.subtract).then_inc(n_lo, 1)
                    return
                for b, (m, s) in enumerate(blocks(n, c)):
                    cols = block_cols(s)
                    made = nc.vector.scalar_tensor_tensor(
                        out=h_lo[:, m, cols], in0=t[:, b, :], scalar=mod[:, first, 8 * shift + m, s:s + 1],
                        in1=h_hi[:, m, cols].bitcast(F32), op0=ALU.add, op1=ALU.subtract)
                made.then_inc(n_lo, 1)

            for c in range(chunks(n)):
                if kind in ("mod", "gain") and c >= 3:
                    dve.wait_ge(n_lo, h0 + c - 2)
                scaled(c)
                if kind in ("mod", "gain") and c >= 1:
                    remainder(c - 1)
                if kind == "post" and c >= 1:
                    residual(dve, n, src, c - 1, factor, sq0)
            if kind in ("mod", "gain"):
                remainder(chunks(n) - 1)
            if kind == "post":
                residual(dve, n, src, chunks(n) - 1, factor, sq0)

        def residual(dve, n, src, c, factor, sq0):
            dve.wait_ge(n_t, sq0 + c + 1)
            x = chunk_of(X, n, c)
            nc.vector.scalar_tensor_tensor(out=x, in0=src(c), scalar=factor, in1=x, op0=ALU.mult,
                                           op1=ALU.add).then_inc(n_x, 1)

        def x_chunk(n):
            return lambda c: chunk_of(X, n, c)

        def y_chunk(c):
            return yb[:, 2 * c:2 * c + 2, :]

        def mod_stripe(pe, batch, k):
            slot = k % 2
            if k == 0:
                need(pe, mod_ready, batch)
            w = mod_ring[:, slot, :]
            if isinstance(batch, int) and batch == 0:
                if 2 <= k < 6:
                    pe.wait_ge(mod_early[k - 2], 16)
                    w = mod_early_ring[:, k - 2, :]
                else:
                    pe.wait_ge(mod_in[slot], 16 if k < 2 else 32)
            else:
                pe.wait_ge(mod_in[slot], 64 * batch + 16 * (k // 2 - 1))
            for j in range(4):
                made = nc.tensor.matmul(psum[32 * j:32 * j + 32, 7, :], silu_all[:, 2 * k:2 * k + 32], w[:, TT * j:TT * (j + 1)],
                                        start=k == 0, stop=k == KD - 1, skip_group_check=True)
            made.then_inc(mod_stripes, 1)

        def mod_turn(pe, batch):
            pe.wait_ge(mod_rows_in, batch + 1)
            for q in range(4):
                made = nc.tensor.transpose(psum[:, 7, q * P:(q + 1) * P], mod_rows[:, q * P:(q + 1) * P], ident)
            made.then_inc(mod_turned, 1)

        def mod_copy(dve, batch):
            dve.wait_ge(mod_stripes, 8 * batch + 8)
            nc.vector.tensor_copy(mod_rows, psum[:, 7, :]).then_inc(mod_rows_in, 1)

        def mod_store(dve, layer, batch, at):
            dve.wait_ge(mod_turned, batch + 1)
            turned = psum[:, 7, :].rearrange("p (q j n) -> p j q n", q=4, j=4)
            b = par[:, 0, bass.ds(16 + 48 * layer + 16 * at, 16)].rearrange("p (j q) -> p j q", q=4)
            dst = mod[:, layer, bass.ds(16 * at, 16), :].rearrange("p (j q) s -> p j q s", q=4)
            for s in range(2):
                made = nc.vector.tensor_tensor(dst[:, :, :, s], turned[:, :, :, s], b, ALU.add)
            made.then_inc(mod_ready, 1)

        def mod_plus_one(dve, layer, which):
            at = 8 * (1, 4)[which]
            nc.vector.tensor_scalar(mod1[:, layer, which, :, :], mod[:, layer, at:at + 8, :], 1.0, None,
                                    ALU.add).then_inc(mod1_ready, 1)

        def mod_step(pe, batch, i):
            if i < KD:
                mod_stripe(pe, batch, i)
            else:
                mod_turn(pe, batch)

        MI = AT["mix_in"]
        MOD_AFTER = ([(1, 0), (1, 1)], [(1, 2)], [(1, 3), (1, 4)], [(1, 5)], [(1, 6), (1, 7)], [(1, 8)],
                     [(2, 0), (2, 1)], [(2, 2), (2, 3)], [(2, 4), (2, 5)], [(2, 6), (2, 7)])
        kr_raw = scr[64:96, 2, :]

        def mix_in_tensor(pe):
            for s in range(5):
                begin_stripe(pe, MI + s)
                for t in range(2):
                    n = 2 * s + t
                    need(pe, mi_evac, n - 3)
                    product(pe, psum[:, n % 4, :], MI + s, 64 if n == 5 else t * P, h_cols(0, TT), t == 0,
                            mi_sums, ready=h_ready(pe, 0) if n == 0 else None)
                    for batch, k in MOD_AFTER[n]:
                        mod_step(pe, batch, k)
                if s == 1:
                    for k in range(3):
                        pe.wait_ge(mi_sq, k + 1)
                        nc.tensor.matmul(psum[:, 4, :], ones, scr[:, 3 + k, :], start=k == 0,
                                         stop=k == 2).then_inc(mi_ss, 1)
                if s == 2:
                    for k in range(2):
                        pe.wait_ge(mi_sq, k + 4)
                        nc.tensor.matmul(psum[:, 5, :], ones, scr[:, 3 + k, :], start=k == 0,
                                         stop=k == 1).then_inc(mi_ss, 1)
                    pe.wait_ge(mi_evac, 6)
                    nc.tensor.matmul(psum[64:96, 6, 0:T], rot_mla[64:96, 64:96], kr_raw[:, T:TT],
                                     start=True, stop=True).then_inc(mi_rot, 1)

        def mix_in_scalar(act):
            for s in range(5):
                ahead_hi(act, MI + s)
                for n in (2 * s, 2 * s + 1):
                    act.wait_ge(mi_sums, n + 1)
                    bank = psum[:, n % 4, :]
                    if n < 5:
                        need(act, mi_ss, n - 2)
                        nc.scalar.activation(scr[:, 3 + n % 3, :], bank, ACT.Square).then_inc(mi_sq, 1)
                        dst = cq[:, n, :] if n < 3 else ckv[:, n - 3, :]
                        nc.scalar.activation(dst, bank, ACT.Copy,
                                             scale=par[:, 1, 88 + n:89 + n]).then_inc(mi_evac, 1)
                    elif n == 5:
                        nc.scalar.activation(kr_raw, psum[64:96, n % 4, :], ACT.Copy).then_inc(mi_evac, 1)
                    else:
                        nc.scalar.activation(pool_p[:, n - 6, :, PAD:PAD + T], bank2(n % 4),
                                             ACT.Copy).then_inc(mi_evac, 1)
                if s == 1:
                    act.wait_ge(mi_ss, 3)
                    act.wait_ge(n_rinv, 1)
                    nc.scalar.activation(std[:, :], psum[:, 4, :], ACT.Sqrt, bias=eps,
                                         scale=1.0 / QR).then_inc(mi_std, 1)
                if s == 2:
                    act.wait_ge(mi_ss, 5)
                    nc.scalar.activation(scr[:, 0, :], psum[:, 5, :], ACT.Sqrt, bias=eps,
                                         scale=1.0 / KVR).then_inc(mi_std, 1)
            for t in range(4):
                act.wait_ge(v_sums, t + 1)
                nc.scalar.activation(v_mla[:, t, :], psum[:, t, :], ACT.Copy).then_inc(v_evac, 1)

        def mix_in_vector(dve):
            def fix(inst, count):
                inst.then_inc(mi_fix, 1)
                dve.wait_ge(mi_fix, count)

            for s in range(5):
                ahead_lo(dve, MI + s)
                if s == 2:
                    dve.wait_ge(mi_std, 1)
                    fix(nc.vector.reciprocal(rinv[:, :], std[:, :]), 1)
                    for k in range(3):
                        dve.wait_ge(mi_evac, k + 1)
                        nc.vector.tensor_tensor(cq[:, k, :], cq[:, k, :], rinv[:, :], ALU.mult).then_inc(mi_fix, 1)
                if s == 3:
                    mod_store(dve, 0, 1, 1)
                    dve.wait_ge(mi_std, 2)
                    fix(nc.vector.reciprocal(scr[:, 1, :], scr[:, 0, :]), 5)
                    for k in range(2):
                        dve.wait_ge(mi_evac, k + 4)
                        nc.vector.tensor_tensor(ckv[:, k, :], ckv[:, k, :], scr[:, 1, :],
                                                ALU.mult).then_inc(mi_fix, 1)
                if s == 2:
                    mod_copy(dve, 1)
            mod_copy(dve, 2)
            mod_store(dve, 0, 2, 2)
            dve.wait_ge(mod_ready, 3)
            mod_plus_one(dve, 0, 1)
            dve.wait_ge(mi_rot, 1)
            dve.wait_ge(small_in, 80)
            k0, tmp = k_mla[64:96, 0, :], scr[64:96, 0, 0:T]
            nc.vector.tensor_copy(k0[:, 0:T], kr_raw[:, 0:T]).then_inc(mi_fix, 1)
            nc.vector.tensor_tensor(k0[:, T:TT], kr_raw[:, T:TT], tab_mla[64:96, 0, :], ALU.mult).then_inc(mi_fix, 1)
            fix(nc.vector.tensor_tensor(tmp, psum[64:96, 6, 0:T], tab_mla[64:96, 1, :], ALU.mult), 10)
            fix(nc.vector.tensor_tensor(k0[:, T:TT], k0[:, T:TT], tmp, ALU.add), 11)
            fix(nc.vector.tensor_copy(k_mla[64:96, 1, :], k0), 12)

        def values_tensor(pe):
            pe.wait_ge(small_in, 80)
            pe.wait_ge(mi_fix, 7)
            pe.wait_ge(mi_evac, 10)
            for t in range(4):
                for k in range(2):
                    made = nc.tensor.matmul(psum[:, t, :], ckv[:, k, t * P:(t + 1) * P], w_uv[:, k, :],
                                            start=k == 0, stop=k == 1)
                made.then_inc(v_sums, 1)

        def qk_tensor(pe, h):
            if h == 0:
                pe.wait_ge(v_evac, 4)
                pe.wait_ge(mi_fix, 12)
            need(pe, q_roped, 3 * h)
            for k in range(3):
                made = nc.tensor.matmul(psum[0:MLA_QK, 0, :], w_uq[:, k, MLA_QK * h:MLA_QK * (h + 1)], cq[:, k, :],
                                        start=k == 0, stop=k == 2)
            made.then_inc(q_sums, 1)
            need(pe, k_copied, h)
            for k in range(2):
                made = nc.tensor.matmul(psum[0:NOPE, 1, :], w_uk[:, k, NOPE * h:NOPE * (h + 1)], ckv[:, k, :],
                                        start=k == 0, stop=k == 1)
            made.then_inc(k_sums, 1)

        def q_rotate_tensor(pe, h):
            pe.wait_ge(q_copied, h + 1)
            nc.tensor.matmul(psum[0:MLA_QK, 0, 0:T], rot_mla[0:MLA_QK, 0:MLA_QK], q_mla[0:MLA_QK, h % 2, T:TT],
                             start=True, stop=True).then_inc(q_rot, 1)

        def q_copy_scalar(act, h):
            act.wait_ge(q_sums, h + 1)
            need(act, at_s, 3 * (h - 1))
            nc.scalar.activation(q_mla[0:MLA_QK, h % 2, :], psum[0:MLA_QK, 0, :], ACT.Copy).then_inc(q_copied, 1)

        def k_copy_vector(dve, h):
            dve.wait_ge(k_sums, h + 1)
            need(dve, at_s, 3 * (h - 1))
            nc.vector.tensor_copy(k_mla[0:NOPE, h % 2, :], psum[0:NOPE, 1, :]).then_inc(k_copied, 1)

        def q_rope_vector(dve, h):
            dve.wait_ge(q_rot, h + 1)
            q, tmp = q_mla[0:MLA_QK, h % 2, T:TT], rinv[0:MLA_QK, 0:T]
            nc.vector.tensor_tensor(tmp, psum[0:MLA_QK, 0, 0:T], tab_mla[0:MLA_QK, 1, :], ALU.mult).then_inc(q_roped, 1)
            nc.vector.tensor_tensor(q, q, tab_mla[0:MLA_QK, 0, :], ALU.mult).then_inc(q_roped, 1)
            dve.wait_ge(q_roped, 3 * h + 2)
            nc.vector.tensor_tensor(q, q, tmp, ALU.add).then_inc(q_roped, 1)

        pt_l = pt_mla[:, 0:1024].rearrange("p (k q) -> p k q", k=4)
        pt_c = pt_mla[:, 1024:1536].rearrange("p (k q) -> p k q", k=2)
        pt_g = pt_gqa.rearrange("p (k q) -> p k q", k=4)
        MLA = dict(
            heads=8, scale=MLA_SCALE, base=0, score_banks=((2, 1), (3, 1), (4, 2)),
            rows=((2, 0, 512, 0), (3, 0, 512, 1), (4, 0, 256, 2), (4, 256, 256, 2)),
            turns=((5, [(0, 128 * k, 128 * k) for k in range(4)], pt_l[:, :, 0:P], 1),
                   (6, [(1, 128 * k, 128 * k) for k in range(4)], pt_l[:, :, P:T], 2),
                   (5, [(2, 256 * q + 128 * k, 256 * k + 128 * q) for q in range(2) for k in range(2)],
                    pt_c[:, :, :], 4)))
        GQA = dict(
            heads=8, scale=GQA_SCALE, base=1, score_banks=((0, 1), (1, 1)),
            rows=((0, 0, 512, 0), (1, 0, 512, 1)),
            turns=((2, [(0, 128 * k, 128 * k) for k in range(4)], pt_g[:, :, 0:P], 1),
                   (3, [(1, 128 * k, 128 * k) for k in range(4)], pt_g[:, :, P:T], 2)))

        def at_base(cfg, per):
            return cfg["base"] * MLA["heads"] * per(MLA)

        def n_rows(cfg):
            return len(cfg["rows"])

        def n_banks(cfg):
            return len(cfg["score_banks"])

        def n_turns(cfg):
            return len(cfg["turns"])

        def mla_scores(pe, h, b):
            q, k = q_mla[0:MLA_QK, h % 2, :], k_mla[0:MLA_QK, h % 2, :]
            if b < 2:
                return nc.tensor.matmul(psum[:, 2 + b, :], q[:, T + b * P:T + (b + 1) * P], k, start=True, stop=True)
            for t in range(2):
                made = nc.tensor.matmul(psum[:, 4, t * T:(t + 1) * T], q[:, t * P:(t + 1) * P], k[:, 0:T],
                                        start=True, stop=True)
            return made

        def gqa_scores(pe, h, b):
            return nc.tensor.matmul(psum[:, b, :], q_gqa[:, h, b * P:(b + 1) * P], k_gqa[:, h // 4, :],
                                    start=True, stop=True)

        def scores_tensor(pe, cfg, h, scores):
            need(pe, at_e, at_base(cfg, n_rows) + n_rows(cfg) * h)
            for b in range(n_banks(cfg)):
                scores(pe, h, b).then_inc(at_s, 1)

        def turns_tensor(pe, cfg, h):
            done, turned = at_base(cfg, n_rows) + n_rows(cfg) * h, at_base(cfg, n_turns) + n_turns(cfg) * h
            banks = [b for b, *_ in cfg["turns"]]
            for g, (bank, pieces, _, rows) in enumerate(cfg["turns"]):
                pe.wait_ge(at_pn, done + rows)
                before = [x for x in range(g) if banks[x] == bank]
                last = max(x for x in range(len(banks)) if banks[x] == bank)
                need(pe, at_pt, turned + before[-1] + 1 if before else turned - n_turns(cfg) + last + 1)
                for slot, col, to in pieces:
                    made = nc.tensor.transpose(psum[:, bank, to:to + P], scr[:, 3 * (h % 2) + slot, col:col + P], ident)
                made.then_inc(at_t, 1)

        def mla_out_tensor(pe, h):
            pe.wait_ge(at_pt, 3 * (h + 1))
            need(pe, at_lo, h)
            r = slice(NOPE * (h % 2), NOPE * (h % 2) + NOPE)
            for t in range(2):
                nc.tensor.matmul(psum[r, 7, 0:T], v_mla[:, t, 64 * h:64 * (h + 1)], pt_c[:, t, :],
                                 start=t == 0, stop=t == 1)
            for t in range(4):
                made = nc.tensor.matmul(psum[r, 7, T:TT], v_mla[:, t, 64 * h:64 * (h + 1)], pt_l[:, t, :],
                                        start=t == 0, stop=t == 3)
            made.then_inc(at_o, 1)

        def gqa_out_tensor(pe, h):
            pe.wait_ge(at_pt, at_base(GQA, n_turns) + 2 * (h + 1))
            need(pe, at_lo, 8 + h - 1)
            for t in range(4):
                made = nc.tensor.matmul(psum[:, 4 + h % 2, 0:T], v_gqa[:, t, P * (h // 4):P * (h // 4 + 1)],
                                        pt_g[:, t, :], start=t == 0, stop=t == 3)
            made.then_inc(at_o, 1)

        def exp_scalar(act, cfg, h):
            n = at_base(cfg, lambda c: n_banks(c) + 1) + (n_banks(cfg) + 1) * (h + 1)
            act.wait_ge(at_mx, n)
            need(act, at_t, at_base(cfg, n_turns) + n_turns(cfg) * (h - 1))
            for r, (bank, lo, cols, slot) in enumerate(cfg["rows"]):
                nc.scalar.activation(scr[:, 3 * (h % 2) + slot, lo:lo + cols], psum[:, bank, lo:lo + cols], ACT.Exp,
                                     bias=row_neg[:, h % 2, r:r + 1], scale=cfg["scale"],
                                     accum_out=row_sum[:, h % 2, r:r + 1]).then_inc(at_e, 1)

        def turned_scalar(act, cfg, h):
            turned = at_base(cfg, n_turns) + n_turns(cfg) * h
            need(act, at_o, 8 * cfg["base"] + h)
            for g, (bank, _, dst, _) in enumerate(cfg["turns"]):
                act.wait_ge(at_t, turned + g + 1)
                k = dst.shape[1]
                nc.scalar.activation(dst, psum[:, bank, :].rearrange("p (k q) -> p k q", k=k),
                                     ACT.Copy).then_inc(at_pt, 1)

        def head_out(cfg, h):
            if cfg is MLA:
                r = slice(NOPE * (h % 2), NOPE * (h % 2) + NOPE)
                return psum[r, 7, :], h_hi[r, h // 2, :], h_lo[r, h // 2, :]
            return psum[:, 4 + h % 2, 0:T], h_hi[:, h, 0:T], h_lo[:, h, 0:T]

        def out_hi_scalar(act, cfg, h):
            act.wait_ge(at_o, 8 * cfg["base"] + h + 1)
            src, hi, _ = head_out(cfg, h)
            nc.scalar.activation(hi, src, ACT.Copy).then_inc(at_hi, 1)

        def out_lo_vector(dve, cfg, h):
            dve.wait_ge(at_hi, 8 * cfg["base"] + h + 1)
            src, hi, lo = head_out(cfg, h)
            nc.vector.tensor_tensor(lo, src, hi.bitcast(F32), ALU.subtract).then_inc(at_lo, 1)

        def max_vector(dve, cfg, h):
            scored = at_base(cfg, n_banks) + n_banks(cfg) * h
            n = at_base(cfg, lambda c: n_banks(c) + 1) + (n_banks(cfg) + 1) * h
            r = 0
            for b, (bank, blocks_) in enumerate(cfg["score_banks"]):
                dve.wait_ge(at_s, scored + b + 1)
                src = psum[:, bank, :].rearrange("p (r k) -> p r k", r=blocks_)
                nc.vector.tensor_reduce(row_max[:, h % 2, r:r + blocks_], src, AX.X, ALU.max).then_inc(at_mx, 1)
                r += blocks_
            dve.wait_ge(at_mx, n + n_banks(cfg))
            nc.vector.tensor_scalar(row_neg[:, h % 2, 0:r], row_max[:, h % 2, 0:r], -cfg["scale"], None,
                                    ALU.mult).then_inc(at_mx, 1)

        def norm_rows_vector(dve, cfg, h):
            made = at_base(cfg, n_rows) + n_rows(cfg) * h
            R = n_rows(cfg)
            dve.wait_ge(at_e, made + R)
            nc.vector.reciprocal(row_inv[:, h % 2, 0:R], row_sum[:, h % 2, 0:R]).then_inc(at_rs, 1)
            dve.wait_ge(at_rs, 8 * cfg["base"] + h + 1)
            for r, (_, lo, cols, slot) in enumerate(cfg["rows"]):
                p = scr[:, 3 * (h % 2) + slot, lo:lo + cols]
                nc.vector.tensor_scalar(p, p, row_inv[:, h % 2, r:r + 1], None, ALU.mult).then_inc(at_pn, 1)

        def mla_tensor(pe):
            qk_tensor(pe, 0)
            q_rotate_tensor(pe, 0)
            for h in range(MLA_H):
                if h + 1 < MLA_H:
                    qk_tensor(pe, h + 1)
                pe.wait_ge(q_roped, 3 * (h + 1))
                pe.wait_ge(k_copied, h + 1)
                scores_tensor(pe, MLA, h, mla_scores)
                if h + 1 < MLA_H:
                    q_rotate_tensor(pe, h + 1)
                if h:
                    turns_tensor(pe, MLA, h - 1)
                    mla_out_tensor(pe, h - 1)
            turns_tensor(pe, MLA, MLA_H - 1)
            mla_out_tensor(pe, MLA_H - 1)

        def mla_scalar(act):
            q_copy_scalar(act, 0)
            for h in range(MLA_H):
                if h + 1 < MLA_H:
                    q_copy_scalar(act, h + 1)
                exp_scalar(act, MLA, h)
                if h:
                    turned_scalar(act, MLA, h - 1)
                    out_hi_scalar(act, MLA, h - 1)
            turned_scalar(act, MLA, MLA_H - 1)
            out_hi_scalar(act, MLA, MLA_H - 1)

        def mla_vector(dve):
            k_copy_vector(dve, 0)
            q_rope_vector(dve, 0)
            for h in range(MLA_H):
                if h + 1 < MLA_H:
                    k_copy_vector(dve, h + 1)
                max_vector(dve, MLA, h)
                if h + 1 < MLA_H:
                    q_rope_vector(dve, h + 1)
                norm_rows_vector(dve, MLA, h)
                if h:
                    out_lo_vector(dve, MLA, h - 1)
            out_lo_vector(dve, MLA, MLA_H - 1)

        def pool_gpsimd(pool):
            seq = 0

            def then(inst):
                nonlocal seq
                seq += 1
                inst.then_inc(pool_seq, 1)
                pool.wait_ge(pool_seq, seq)

            pool.wait_ge(inv_in, 16)
            for g, w in enumerate(WINDOWS):
                pool.wait_ge(mi_evac, 7 + g)
                src, length, step = pool_p[:, g, :, :], T + 2 * PAD, 1
                while step < w:
                    dst = pool_b if src is pool_a else pool_a
                    length -= step
                    then(nc.gpsimd.tensor_tensor(dst[:, :, 0:length], src[:, :, 0:length],
                                                 src[:, :, step:step + length], ALU.add))
                    src, step = dst, 2 * step
                dst = pool_b if src is pool_a else pool_a
                inv = pool_inv[:, g, :]
                for s in range(2):
                    made = nc.gpsimd.tensor_tensor(dst[:, s, 0:T], src[:, s, PAD - w // 2:PAD - w // 2 + T], inv, ALU.mult)
                then(made)
                p = pool_p[:, g, :, PAD:PAD + T]
                nc.gpsimd.tensor_tensor(p, dst[:, :, 0:T], p, ALU.subtract).then_inc(pool_d, 1)
                pool.wait_ge(pool_d, g + 1)

        def pool_tensor(pe):
            for g in range(4):
                pe.wait_ge(pool_d, g + 1)
                if g == 0:
                    pe.wait_ge(at_e, 8 * n_rows(MLA))
                nc.tensor.matmul(psum[:, g, :], w_pool[:, g, :], pool_p[:, g, :, PAD:PAD + T], start=True,
                                 stop=True).then_inc(pool_sums, 1)

        def pool_scalar(act):
            for g in range(4):
                act.wait_ge(pool_sums, g + 1)
                nc.scalar.activation(h_hi[:, 4 + g, :], psum[:, g, :], ACT.Copy,
                                     scale=par[:, 1, 93 + g:94 + g]).then_inc(pool_hi, 1)

        def pool_vector(dve):
            for g in range(4):
                dve.wait_ge(pool_hi, g + 1)
                nc.vector.scalar_tensor_tensor(out=h_lo[:, 4 + g, :], in0=psum[:, g, :],
                                               scalar=par[:, 1, 93 + g:94 + g],
                                               in1=h_hi[:, 4 + g, :].bitcast(F32), op0=ALU.mult,
                                               op1=ALU.subtract).then_inc(pool_lo, 1)

        def double(x, n=2):
            return x.unsqueeze(1).broadcast_to([x.shape[0], n, x.shape[1]])

        MO, GO, WO = AT["mix_out"], AT["gqa_out"], AT["w_out"]

        def mix_out_tensor(pe):
            pe.wait_ge(at_lo, MLA_H)
            pe.wait_ge(pool_lo, 4)
            for m in range(KD):
                if m % 2 == 0:
                    begin_stripe(pe, MO + m // 2)
                need(pe, o_evac, m - 3)
                product(pe, psum[:, m % 4, :], MO + m // 2, m % 2 * P, h_cols(0, TT), m % 2 == 0, o_sums)

        def mix_out_vector(dve):
            for m in range(KD):
                if m % 2 == 0:
                    ahead_lo(dve, MO + m // 2)
                dve.wait_ge(o_sums, m + 1)
                for s in range(2):
                    x = X[:, m, block_cols(s)]
                    made = nc.vector.scalar_tensor_tensor(out=x, in0=psum[:, m % 4, block_cols(s)],
                                                          scalar=mod[:, 0, 16 + m, s:s + 1], in1=x,
                                                          op0=ALU.mult, op1=ALU.add)
                made.then_inc(o_evac, 1)

        def out_tensor(pe, i0, ready):
            for s in range(4):
                begin_stripe(pe, i0 + s)
                product(pe, psum[:, s, 0:T], i0 + s, 0, h_cols(0, T), True, ready=ready if s == 0 else None)
                product(pe, psum[:, s, T:TT], i0 + s, P, h_cols(0, T), False, o_sums)

        def ahead_scalar(act, i0, n):
            for i in range(i0, i0 + n):
                ahead_hi(act, i)

        def gqa_out_vector(dve):
            for s in range(4):
                ahead_lo(dve, GO + s)
                dve.wait_ge(o_sums, 8 + s + 1)
                for t in range(2):
                    x = X[:, 2 * s + t, T:TT]
                    made = nc.vector.scalar_tensor_tensor(out=x, in0=psum[:, s, block_cols(t)],
                                                          scalar=mod[:, 1, 16 + 2 * s + t, 1:2], in1=x,
                                                          op0=ALU.mult, op1=ALU.add)
                made.then_inc(o_evac, 1)

        def w_out_vector(dve):
            for s in range(4):
                ahead_lo(dve, WO + s)
                dve.wait_ge(o_sums, 12 + s + 1)
                dve.wait_ge(p_hi, s + 1)
                nc.vector.tensor_copy(yb[:, 2 * s:2 * s + 2, :], bank2(s)).then_inc(o_evac, 1)

        FFNS = [dict(wide=True, layer=0, norm=1), dict(wide=False, layer=1, norm=3),
                dict(wide=False, layer=None, norm=5), dict(wide=False, layer=None, norm=9)]

        def units(f):
            return 2 if FFNS[f]["wide"] else 1

        def unit_base(f):
            return sum(units(g) * PAIRS for g in range(f))

        def down_per(f):
            return KD if FFNS[f]["wide"] else 1

        def down_base(f):
            return sum(down_per(g) * PAIRS for g in range(f))

        def x_base(f):
            return (0, KD * PAIRS, KD * PAIRS + KD, KD * PAIRS + KD + 4)[f]

        def ffn_stripe(f, what, first):
            i0 = AT[f"ffn{f}"]
            return i0 + {"g": 0, "u": 1}[what] if first else i0 + {"g": 2, "u": 3, "d": 4}[what]

        def up_tensor(pe, f, what, i, n, j):
            U_, base = units(f), unit_base(f)
            begin_stripe(pe, i, n)
            conv = FFNS[f]["layer"] is not None
            freed = f_prod if what == "u" else f_conv if conv else f_silu
            need(pe, freed, base + U_ * j)
            done = f_g if what == "g" else f_u
            ready = None
            if what == "g" and isinstance(j, int) and j == 0:
                ready = h_ready(pe, FFNS[f]["norm"])
            for t in range(2):
                if FFNS[f]["wide"]:
                    product(pe, psum[:, t + (2 if what == "u" else 0), :], i, t * P, h_cols(0, TT), t == 0, done,
                            ready=ready if t == 0 else None)
                else:
                    product(pe, psum[:, 1 if what == "u" else 0, block_cols(t)], i, t * P, h_cols(T, TT),
                            t == 0, done if t == 1 else None, ready=ready if t == 0 else None)

        def down_tensor(pe, f, i, n, j, last=False):
            begin_stripe(pe, i, n)
            pe.wait_ge(f_alo, unit_base(f) + units(f) * (j + 1))
            slot = i % RING
            started = False
            if FFNS[f]["wide"]:
                for m in range(KD):
                    need(pe, f_x, x_base(f) + KD * j + (m - 2 if m >= 3 else 0))
                    for k in range(2):
                        c = k * D + m * P
                        made = three(psum[:, 4 + m % 3, :], (w_hi[:, slot, c:c + P], w_lo[:, slot, c:c + P]),
                                     (a_hi[:, k, :], a_lo[:, k, :]), k == 0, k == 1)
                        if not started:
                            made[0].then_inc(stripe_started, 1)
                            started = True
                    made[-1].then_inc(f_d, 1)
                return
            for k in range(2):
                for m in range(KD):
                    c = k * D + m * P
                    begins = isinstance(j, int) and j == 0 and k == 0 and m % 2 == 0
                    made = three(psum[:, 4 + m // 2, block_cols(m % 2)],
                                 (w_hi[:, slot, c:c + P], w_lo[:, slot, c:c + P]),
                                 (a_hi[:, 0, block_cols(k)], a_lo[:, 0, block_cols(k)]), begins, last and k == 1)
                    if not started:
                        made[0].then_inc(stripe_started, 1)
                        started = True
            made[-1].then_inc(f_d, 1)

        def ffn_tensor(pe, f):
            i0 = AT[f"ffn{f}"]
            G, U_, D_ = (ffn_stripe(f, w, False) for w in "gud")
            up_tensor(pe, f, "g", i0, 0, 0)
            up_tensor(pe, f, "u", i0 + 1, 0, 0)

            def pair(n, between=lambda i: None):
                up_tensor(pe, f, "g", G, n, n + 1)
                between(0)
                up_tensor(pe, f, "u", U_, n, n + 1)
                between(1)
                down_tensor(pe, f, D_, n, n)
                between(2)

            pair(0)
            if f == 0:
                with pe.Fori(0, (PAIRS - 2) // 3) as r:
                    for c in range(3):
                        pair(3 * r + (c + 1), lambda i, c=c: mod_step(pe, r + 3, 3 * c + i))
            else:
                with pe.Fori(1, PAIRS - 1) as n:
                    pair(n)
            down_tensor(pe, f, i0 + 3 * PAIRS - 1, 0, PAIRS - 1, last=True)

        def g_bank(f, t):
            return psum[:, t, :] if FFNS[f]["wide"] else psum[:, 0, :]

        def u_bank(f, t):
            return psum[:, 2 + t, :] if FFNS[f]["wide"] else psum[:, 1, :]

        def ffn_act_hi(act, f, j):
            base = unit_base(f) + units(f) * j
            for t in range(units(f)):
                act.wait_ge(f_prod, base + t + 1)
                if not (isinstance(j, int) and j == 0):
                    act.wait_ge(f_d, down_base(f) + down_per(f) * j)
                nc.scalar.activation(a_hi[:, t, :], f_act[:, t, :], ACT.Copy).then_inc(f_ahi, 1)

        def conv_blocks(f, t, j):
            if FFNS[f]["wide"]:
                return [(bank2(t), f_act[:, t, :].rearrange("p (s t) -> p s t", s=2), 2 * j + t)]
            act2 = f_act[:, 0, :].rearrange("p (s t) -> p s t", s=2)
            return [(bank2(0)[:, q:q + 1, :], act2[:, q:q + 1, :], 2 * j + q) for q in range(2)]

        def ffn_mid_scalar(act, f, j):
            layer = FFNS[f]["layer"]
            base = unit_base(f) + units(f) * j
            for t in range(units(f)):
                act.wait_ge(f_g, base + t + 1)
                need(act, f_alo, unit_base(f) + units(f) * j)
                for src, dst, tile in conv_blocks(f, t, j):
                    made = nc.scalar.activation(dst, src, ACT.Identity,
                                                bias=par[:, 1 + layer, bass.ds(66 + tile, 1)],
                                                scale=par[:, 1 + layer, bass.ds(NFF + tile, 1)])
                made.then_inc(f_mid, 1)

        def ffn_silu_scalar(act, f, j):
            base = unit_base(f) + units(f) * j
            for t in range(units(f)):
                if FFNS[f]["layer"] is not None:
                    act.wait_ge(f_conv, base + t + 1)
                    src = f_act[:, t, :]
                else:
                    act.wait_ge(f_g, base + t + 1)
                    need(act, f_alo, unit_base(f) + units(f) * j)
                    src = g_bank(f, t)
                nc.scalar.activation(f_act[:, t, :], src, ACT.Silu).then_inc(f_silu, 1)

        def ffn_scalar(act, f):
            i0 = AT[f"ffn{f}"]
            G, U_, D_ = (ffn_stripe(f, w, False) for w in "gud")

            def gate(i, n, j):
                if FFNS[f]["layer"] is not None:
                    ffn_mid_scalar(act, f, j)
                ahead_hi(act, i, n)
                ffn_silu_scalar(act, f, j)

            ahead_hi(act, i0)
            gate(i0 + 1, 0, 0)

            def pair(n):
                ffn_act_hi(act, f, n)
                ahead_hi(act, G, n)
                gate(U_, n, n + 1)
                ahead_hi(act, D_, n)

            pair(0)
            last = PAIRS - 2 if f == 3 else PAIRS - 1
            with act.Fori(1, last) as n:
                pair(n)
            for n in range(last, PAIRS - 1):
                pair(n)
            ffn_act_hi(act, f, PAIRS - 1)
            ahead_hi(act, i0 + 3 * PAIRS - 1)

        def ffn_act_lo(dve, f, j):
            base = unit_base(f) + units(f) * j
            for t in range(units(f)):
                dve.wait_ge(f_ahi, base + t + 1)
                nc.vector.tensor_tensor(a_lo[:, t, :], f_act[:, t, :], a_hi[:, t, :].bitcast(F32),
                                        ALU.subtract).then_inc(f_alo, 1)

        def ffn_conv_vector(dve, f, j):
            layer = FFNS[f]["layer"]
            base = unit_base(f) + units(f) * j
            for t in range(units(f)):
                dve.wait_ge(f_mid, base + t + 1)
                for tap, src_at, dst_at, done in ((0, 0, 1, f_left), (2, 1, 0, f_conv)):
                    for src, dst, tile in conv_blocks(f, t, j):
                        made = nc.vector.scalar_tensor_tensor(
                            out=dst[:, :, dst_at:dst_at + T - 1], in0=src[:, :, src_at:src_at + T - 1],
                            scalar=par[:, 1 + layer, bass.ds(NFF * tap + tile, 1)],
                            in1=dst[:, :, dst_at:dst_at + T - 1], op0=ALU.mult, op1=ALU.add)
                    made.then_inc(done, 1)
                    if tap == 0:
                        dve.wait_ge(f_left, base + t + 1)

        def ffn_prod_vector(dve, f, j):
            base = unit_base(f) + units(f) * j
            for t in range(units(f)):
                dve.wait_ge(f_u, base + t + 1)
                dve.wait_ge(f_silu, base + t + 1)
                nc.vector.tensor_tensor(f_act[:, t, :], f_act[:, t, :], u_bank(f, t), ALU.mult).then_inc(f_prod, 1)

        def ffn_down_vector(dve, f, j, tiles):
            for m in tiles:
                dve.wait_ge(f_d, down_base(f) + KD * j + m + 1)
                for s in range(2):
                    x = X[:, m, block_cols(s)]
                    made = nc.vector.scalar_tensor_tensor(out=x, in0=psum[:, 4 + m % 3, block_cols(s)],
                                                          scalar=mod[:, 0, 40 + m, s:s + 1], in1=x,
                                                          op0=ALU.mult, op1=ALU.add)
                made.then_inc(f_x, 1)

        def ffn_vector(dve, f):
            i0 = AT[f"ffn{f}"]
            wide = FFNS[f]["wide"]
            G, U_, D_ = (ffn_stripe(f, w, False) for w in "gud")

            def gate(i, n, j):
                if FFNS[f]["layer"] is not None:
                    ffn_conv_vector(dve, f, j)
                ahead_lo(dve, i, n)

            def store(i, n, j):
                if wide:
                    ffn_down_vector(dve, f, j, range(3))
                ahead_lo(dve, i, n)
                if wide:
                    ffn_down_vector(dve, f, j, range(3, KD))

            ahead_lo(dve, i0)
            gate(i0 + 1, 0, 0)
            ffn_prod_vector(dve, f, 0)

            def pair(n, batch=None):
                ffn_act_lo(dve, f, n)
                ahead_lo(dve, G, n)
                gate(U_, n, n + 1)
                ffn_prod_vector(dve, f, n + 1)
                if batch is not None:
                    mod_copy(dve, batch + 3)
                if wide:
                    dve.wait_ge(f_x, x_base(f) + KD * n) if not isinstance(n, int) else None
                store(D_, n, n)
                if batch is not None:
                    mod_store(dve, 1, batch + 3, batch)

            pair(0)
            if f == 0:
                with dve.Fori(0, (PAIRS - 2) // 3) as r:
                    for c in range(3):
                        pair(3 * r + (c + 1), r if c == 2 else None)
            else:
                last = PAIRS - 2 if f == 3 else PAIRS - 1
                with dve.Fori(1, last) as n:
                    pair(n)
                for n in range(last, PAIRS - 1):
                    pair(n)
            ffn_act_lo(dve, f, PAIRS - 1)
            if wide:
                dve.wait_ge(f_x, x_base(f) + KD * (PAIRS - 1))
            store(i0 + 3 * PAIRS - 1, 0, PAIRS - 1)
            if f == 0:
                dve.wait_ge(mod_ready, 6)
                mod_plus_one(dve, 1, 0)
                mod_plus_one(dve, 1, 1)
                dve.wait_ge(mod1_ready, 4)
            if not wide:
                dve.wait_ge(f_d, down_base(f) + PAIRS)
                for b in range(4):
                    if FFNS[f]["layer"] is None:
                        nc.vector.tensor_copy(yb[:, 2 * b:2 * b + 2, :], bank2(4 + b)).then_inc(f_x, 1)
                        continue
                    for t in range(2):
                        m = 2 * b + t
                        x = X[:, m, T:TT]
                        nc.vector.scalar_tensor_tensor(out=x, in0=bank2(4 + b)[:, t, :],
                                                       scalar=mod[:, 1, 40 + m, 1:2], in1=x, op0=ALU.mult,
                                                       op1=ALU.add).then_inc(f_x, 1)

        GI = AT["gqa_in"]

        def gqa_in_tensor(pe):
            def turn(v):
                pe.wait_ge(gi_evac, v + 1)
                need(pe, gi_fix, 5 * (v - 1))
                nc.tensor.matmul(psum[:, 4 + v % 2, :], rot_gqa, g_tmp[:, v % 2, :], start=True,
                                 stop=True).then_inc(gi_rot, 1)
                nc.tensor.matmul(psum[:, 6 + v % 2, :], ones, scr[:, 3 + v % 3, :], start=True,
                                 stop=True).then_inc(gi_rot, 1)

            for s in range(6):
                begin_stripe(pe, GI + s)
                for t in range(2):
                    u = s if s < 4 else 2 * s - 4 + t
                    if s >= 4 or t == 0:
                        need(pe, gi_evac, u - 3)
                    ready = h_ready(pe, 2) if s == t == 0 else None
                    if s < 4:
                        product(pe, psum[:, u, block_cols(t)], GI + s, t * P, h_cols(T, TT), t == 0,
                                gi_sums if t else None, ready=ready)
                    elif s == 4:
                        product(pe, psum[:, u % 4, :], GI + s, t * P, h_cols(0, TT), t == 0, gi_sums)
                    else:
                        for q in range(2):
                            c = (2 * t + q) * P
                            product_rows(pe, psum[:, u % 4, block_cols(q)], GI + s, h_cols(c, c + P),
                                         t == q == 0, True, gi_sums if q else None)
                    if (s < 4 and t == 0) or s == 5:
                        continue
                    if u >= 1:
                        turn(u - 1)
                if s == 4:
                    turn(5)

        def gqa_in_scalar(act):
            def deviation(v):
                act.wait_ge(gi_rot, 2 * v + 2)
                need(act, gi_fix, 5 * (v - 1) + 1)
                nc.scalar.activation(std[:, :], psum[:, 6 + v % 2, :], ACT.Sqrt, bias=eps,
                                     scale=1.0 / P).then_inc(gi_std, 1)

            act.wait_ge(n_rinv, 3)
            for s in range(6):
                ahead_hi(act, GI + s)
                if s == 5:
                    deviation(5)
                for u in ((s,) if s < 4 else (2 * s - 4, 2 * s - 3)):
                    act.wait_ge(gi_sums, u + 1)
                    if u < 6:
                        need(act, gi_rot, 2 * (u - 2))
                        nc.scalar.activation(scr[:, 3 + u % 3, :], psum[:, u % 4, :], ACT.Square)
                        need(act, gi_fix, 5 * (u - 1))
                        nc.scalar.activation(g_tmp[:, u % 2, :], psum[:, u % 4, :], ACT.Copy,
                                             scale=par[:, 1, 97:98] if u < 4 else par[:, 1, 98:99]).then_inc(gi_evac, 1)
                        if u >= 1:
                            deviation(u - 1)
                    else:
                        nc.scalar.activation(v_gqa[:, 2 * (u - 6):2 * (u - 6) + 2, :], bank2(u % 4),
                                             ACT.Copy).then_inc(gi_evac, 1)

        def gqa_in_vector(dve):
            def rope(v):
                f0 = 5 * v
                dve.wait_ge(gi_std, v + 1)
                need(dve, gi_fix, f0)
                nc.vector.reciprocal(rinv[:, :], std[:, :]).then_inc(gi_fix, 1)
                g = g_tmp[:, v % 2, :].rearrange("p (s t) -> p s t", s=2)
                r = bank2(4 + v % 2)
                tmp = scr[:, v % 2, :].rearrange("p (s t) -> p s t", s=2)
                if v < 4:
                    cos, sin = double(tab_gqa[:, 0, :]), double(tab_gqa[:, 1, :])
                    dst = q_gqa[:, 2 * v:2 * v + 2, :]
                    gr = g
                else:
                    cos, sin = tab_gqa[:, 0:1, :], tab_gqa[:, 1:2, :]
                    dst = k_gqa[:, v - 4, :].rearrange("p (s t) -> p s t", s=2)
                    gr, r, tmp = g[:, 1:2, :], r[:, 1:2, :], tmp[:, 1:2, :]
                nc.vector.tensor_tensor(tmp, r, sin, ALU.mult).then_inc(gi_fix, 1)
                nc.vector.tensor_tensor(gr, gr, cos, ALU.mult).then_inc(gi_fix, 1)
                dve.wait_ge(gi_fix, f0 + 3)
                nc.vector.tensor_tensor(gr, gr, tmp, ALU.add).then_inc(gi_fix, 1)
                dve.wait_ge(gi_fix, f0 + 4)
                nc.vector.tensor_tensor(dst, g, rinv[:, :].rearrange("p (s t) -> p s t", s=2),
                                        ALU.mult).then_inc(gi_fix, 1)

            dve.wait_ge(tab_in, 16)
            for s in range(6):
                ahead_lo(dve, GI + s)
                if 1 <= s < 5:
                    rope(s - 1)
            rope(4)
            rope(5)

        def gqa_tensor(pe):
            pe.wait_ge(gi_fix, 30)
            pe.wait_ge(gi_evac, 8)
            for h in range(8):
                scores_tensor(pe, GQA, h, gqa_scores)
                if h:
                    turns_tensor(pe, GQA, h - 1)
                    gqa_out_tensor(pe, h - 1)
            turns_tensor(pe, GQA, 7)
            gqa_out_tensor(pe, 7)

        def gqa_scalar(act):
            for h in range(8):
                exp_scalar(act, GQA, h)
                if h:
                    turned_scalar(act, GQA, h - 1)
                    out_hi_scalar(act, GQA, h - 1)
            turned_scalar(act, GQA, 7)
            out_hi_scalar(act, GQA, 7)

        def gqa_vector(dve):
            for h in range(8):
                max_vector(dve, GQA, h)
                norm_rows_vector(dve, GQA, h)
                if h:
                    out_lo_vector(dve, GQA, h - 1)
            out_lo_vector(dve, GQA, 7)

        TWO_PI = 6.283185307179586
        PI_1, PI_2, PI_3 = 6.28125, 0.0019350051879882812, 3.0199159819e-07
        ROUND = 12582912.0
        PI_TOP = 3.1415925

        def tables_vector(dve):
            seq = 0

            def then(inst):
                nonlocal seq
                seq += 1
                inst.then_inc(tb_seq, 1)
                dve.wait_ge(tb_seq, seq)

            ang, turns, red = scr[:, 3, 0:T], scr[:, 3, T:TT], scr[:, 4, :]
            dve.wait_ge(b2_in, 80)
            then(nc.vector.tensor_copy(turns, pos_i.bitcast(I32)))
            then(nc.vector.tensor_scalar(ang, turns, inv_freq, None, ALU.mult))
            then(nc.vector.tensor_scalar(turns, ang, 1.0 / TWO_PI, ROUND, ALU.mult, ALU.add))
            then(nc.vector.tensor_scalar(turns, turns, ROUND, None, ALU.subtract))
            for part in (PI_1, PI_2, PI_3):
                then(nc.vector.scalar_tensor_tensor(out=ang, in0=turns, scalar=-part, in1=ang, op0=ALU.mult,
                                                    op1=ALU.add))
            then(nc.vector.tensor_scalar(red[:, 0:T], ang, TWO_PI / 4, None, ALU.add))
            then(nc.vector.tensor_scalar(turns, red[:, 0:T], TWO_PI / 2, -TWO_PI, ALU.is_gt, ALU.mult))
            then(nc.vector.tensor_tensor(red[:, 0:T], red[:, 0:T], turns, ALU.add))
            then(nc.vector.tensor_copy(red[:, T:TT], ang))
            then(nc.vector.tensor_scalar(red, red, PI_TOP, -PI_TOP, ALU.min, ALU.max))
            pairs = scr[:, 5, 0:P].rearrange("p (i n) -> p i n", i=2)
            then(nc.vector.tensor_tensor(pairs, lam_rows[:, 0:4:2, :], lam_rows[:, 1:4:2, :], ALU.mult))
            nc.vector.tensor_reduce(lam[:, 0:2], pairs, AX.X, ALU.add).then_inc(tb_ang, 1)
            dve.wait_ge(tb_sin, 2)
            then(nc.vector.tensor_tensor(lam[:, 4:5], lam[:, 2:3], lam[:, 3:4], ALU.subtract))
            then(nc.vector.tensor_scalar(lam[:, 5:6], lam[:, 4:5], LAMBDA_INIT, None, ALU.add))
            then(nc.vector.tensor_scalar(g_sub, par[:, 2, 88:89], 1.0 - LAMBDA_INIT, None, ALU.mult))

        def tables_scalar(act):
            act.wait_ge(tb_ang, 1)
            nc.scalar.activation(tab_b2, scr[:, 4, :].rearrange("p (s t) -> p s t", s=2),
                                 ACT.Sin).then_inc(tb_sin, 1)
            nc.scalar.activation(lam[:, 2:4], lam[:, 0:2], ACT.Exp).then_inc(tb_sin, 1)

        QK = AT["qkv"]
        N_ROT = 14

        def qkv_dst(u):
            if u < 4:
                return qa[:, 2 * u:2 * u + 2, :]
            if u < 8:
                return ka[:, 2 * (u - 4):2 * (u - 4) + 2, :]
            if u < 11:
                return qd[:, 2 * (u - 8):2 * (u - 8) + 2, :]
            if u < N_ROT:
                return kd[:, 2 * (u - 11):2 * (u - 11) + 2, :]
            if u < 18:
                return va[:, :, 256 * (u - 14):256 * (u - 13)]
            return vd[:, :, 256 * (u - 18):256 * (u - 17)]

        def qkv_tensor(pe):
            def turn(v):
                pe.wait_ge(r_evac, v + 1)
                need(pe, r_fix, 3 * (v - 1))
                nc.tensor.matmul(psum[:, 4 + v % 2, :], rot_b2, t_rope[:, v % 2, :], start=True,
                                 stop=True).then_inc(r_rot, 1)

            for u in range(21):
                begin_stripe(pe, QK + u)
                need(pe, r_evac, u - 3)
                for t in range(2):
                    dst, done = psum[:, u % 4, block_cols(t)], r_sums if t else None
                    if u < N_ROT:
                        product(pe, dst, QK + u, t * P, h_cols(T, TT), t == 0, done,
                                ready=h_ready(pe, 7) if u == t == 0 else None)
                    else:
                        product_rows(pe, dst, QK + u, h_cols(T + t * P, T + (t + 1) * P), t == 0, True, done)
                if 1 <= u <= N_ROT:
                    turn(u - 1)

        def qkv_scalar(act):
            for u in range(21):
                ahead_hi(act, QK + u)
                act.wait_ge(r_sums, u + 1)
                if u < N_ROT:
                    need(act, r_fix, 3 * (u - 1))
                    nc.scalar.activation(t_rope[:, u % 2, :], psum[:, u % 4, :], ACT.Copy).then_inc(r_evac, 1)
                else:
                    nc.scalar.activation(qkv_dst(u), bank2(u % 4), ACT.Copy).then_inc(r_evac, 1)

        def qkv_vector(dve):
            for u in range(21):
                ahead_lo(dve, QK + u)
                if not 1 <= u <= N_ROT:
                    continue
                v = u - 1
                dve.wait_ge(r_rot, v + 1)
                need(dve, r_fix, 3 * v - 3)
                x = t_rope[:, v % 2, :].rearrange("p (s t) -> p s t", s=2)
                tmp = scr[:, v % 2, :].rearrange("p (s t) -> p s t", s=2)
                nc.vector.tensor_tensor(tmp, bank2(4 + v % 2), double(tab_b2[:, 1, :]), ALU.mult).then_inc(r_fix, 1)
                nc.vector.tensor_tensor(x, x, double(tab_b2[:, 0, :]), ALU.mult).then_inc(r_fix, 1)
                dve.wait_ge(r_fix, 3 * v + 2)
                nc.vector.tensor_tensor(qkv_dst(v), x, tmp, ALU.add).then_inc(r_fix, 1)

        B_S, B_MX, B_E, B_RS, B_PN, B_T, B_PT, B_O = 40, 56, 48, 16, 48, 40, 40, 16
        C_S, C_MX, C_E, C_RS, C_PN, C_T, C_PT, C_O = 56, 80, 80, 32, 80, 48, 48, 24

        DOWN, CLIP, OVERFLOW = 2.0 ** -20, 2.0 ** 78, 2.0 ** 88

        def diff_probs(h, c):
            return scr[:, 3 * (h % 2) + c, :].rearrange("p (q k) -> p q k", q=2)

        def diff_tensor(pe):
            pe.wait_ge(r_fix, 3 * N_ROT)
            pe.wait_ge(r_evac, 21)

            def turns(h):
                pe.wait_ge(at_pn, B_PN + 4 * (h + 1))
                need(pe, at_pt, B_PT + h)
                for q in range(2):
                    for k in range(2):
                        made = nc.tensor.transpose(psum[:, 4, k * T + q * P:k * T + (q + 1) * P],
                                                   diff_probs(h, 0)[:, q, k * P:(k + 1) * P], ident)
                made.then_inc(at_t, 1)

            def outputs(h):
                pe.wait_ge(at_pt, B_PT + h + 1)
                need(pe, d_copied, h - 1)
                for k in range(2):
                    made = nc.tensor.matmul(psum[:, 5 + h % 2, 0:T], va[:, k, h * P:(h + 1) * P],
                                            pt_b2[:, k * T:(k + 1) * T], start=k == 0, stop=k == 1)
                made.then_inc(at_o, 1)

            for h in range(8):
                need(pe, at_e, B_E + 4 * (h - 1))
                for c in range(2):
                    r = slice(64 * c, 64 * (c + 1))
                    for q in range(2):
                        made = nc.tensor.matmul(psum[:, 2 * (h % 2) + c, block_cols(q)],
                                                qa[r, h, q * P:(q + 1) * P], ka[r, h, :], start=True, stop=True)
                    made.then_inc(at_s, 1)
                if h:
                    turns(h - 1)
                    outputs(h - 1)
            turns(7)
            outputs(7)
            for p in range(4):
                pe.wait_ge(d_sq, p + 1)
                nc.tensor.matmul(psum[:, 4 + p, :], ones, scr[:, 3 + p % 3, :], start=True,
                                 stop=True).then_inc(d_ss, 1)

        def diff_scalar(act):
            def finish(h):
                act.wait_ge(at_t, B_T + h + 1)
                act.wait_ge(at_o, B_O + h)
                nc.scalar.activation(pt_b2[:, 0:TT], psum[:, 4, :], ACT.Copy).then_inc(at_pt, 1)
                act.wait_ge(at_o, B_O + h + 1)
                nc.scalar.activation(qa[:, h, :], psum[:, 5 + h % 2, 0:T], ACT.Copy).then_inc(d_copied, 1)

            for h in range(8):
                act.wait_ge(at_mx, B_MX + 3 * (h + 1))
                need(act, at_t, B_T + h - 1)
                for c in range(2):
                    for q in range(2):
                        nc.scalar.activation(diff_probs(h, c)[:, q, :], psum[:, 2 * (h % 2) + c, block_cols(q)],
                                             ACT.Exp, bias=row_neg[:, h % 2, 2 * c + q:2 * c + q + 1], scale=B2_SCALE,
                                             accum_out=row_sum[:, h % 2, 2 * c + q:2 * c + q + 1]).then_inc(at_e, 1)
                if h:
                    finish(h - 1)
            finish(7)
            for p in range(4):
                act.wait_ge(d_clip, p + 1)
                nc.scalar.activation(scr[:, 3 + p % 3, :], scr[:, 3 + p % 3, :], ACT.Square,
                                     scale=DOWN).then_inc(d_sq, 1)
            for p in range(4):
                act.wait_ge(d_ss, p + 1)
                need(act, d_rinv, 3 * p - 2)
                nc.scalar.activation(std[:, :], psum[:, 4 + p, :], ACT.Sqrt, bias=eps_down, scale=1.0 / P).then_inc(d_std, 1)
                if p:
                    diff_hi(act, p - 1)
            diff_hi(act, 3)

        def diff_hi(act, p):
            act.wait_ge(d_t, p + 1)
            nc.scalar.activation(h_hi[:, 2 * p:2 * p + 2, 0:T], scr[:, p % 3, :].rearrange("p (s t) -> p s t", s=2),
                                 ACT.Copy).then_inc(d_hi, 1)

        def diff_lo(dve, p):
            dve.wait_ge(d_hi, p + 1)
            nc.vector.tensor_tensor(h_lo[:, 2 * p:2 * p + 2, 0:T],
                                    scr[:, p % 3, :].rearrange("p (s t) -> p s t", s=2),
                                    h_hi[:, 2 * p:2 * p + 2, 0:T].bitcast(F32), ALU.subtract).then_inc(d_lo, 1)

        def diff_vector(dve):
            for h in range(8):
                par_ = h % 2
                for c in range(2):
                    dve.wait_ge(at_s, B_S + 2 * h + c + 1)
                    nc.vector.tensor_reduce(row_max[:, par_, 2 * c:2 * c + 2], bank2(2 * par_ + c), AX.X,
                                            ALU.max).then_inc(at_mx, 1)
                dve.wait_ge(at_mx, B_MX + 3 * h + 2)
                nc.vector.tensor_scalar(row_neg[:, par_, :], row_max[:, par_, :], -B2_SCALE, None,
                                        ALU.mult).then_inc(at_mx, 1)
                dve.wait_ge(at_e, B_E + 4 * (h + 1))
                nc.vector.reciprocal(row_inv[:, par_, :], row_sum[:, par_, :]).then_inc(at_rs, 1)
                dve.wait_ge(at_rs, B_RS + 2 * h + 1)
                nc.vector.tensor_scalar(row_inv[:, par_, 2:4], row_inv[:, par_, 2:4], lam[:, 5:6], None,
                                        ALU.mult).then_inc(at_rs, 1)
                dve.wait_ge(at_rs, B_RS + 2 * h + 2)
                p0, p1 = diff_probs(h, 0), diff_probs(h, 1)
                for q in range(2):
                    nc.vector.tensor_scalar(p1[:, q, :], p1[:, q, :], row_inv[:, par_, 2 + q:3 + q], None,
                                            ALU.mult).then_inc(at_pn, 1)
                for q in range(2):
                    dve.wait_ge(at_pn, B_PN + 4 * h + q + 1)
                    nc.vector.scalar_tensor_tensor(out=p0[:, q, :], in0=p0[:, q, :], scalar=row_inv[:, par_, q:q + 1],
                                                   in1=p1[:, q, :], op0=ALU.mult, op1=ALU.subtract).then_inc(at_pn, 1)
            for p in range(4):
                dve.wait_ge(d_copied, 8)
                need(dve, d_ss, p - 2)
                nc.vector.tensor_scalar(scr[:, 3 + p % 3, :].rearrange("p (s t) -> p s t", s=2),
                                        qa[:, 2 * p:2 * p + 2, :], CLIP, -CLIP, ALU.min,
                                        ALU.max).then_inc(d_clip, 1)
            for p in range(4):
                dve.wait_ge(d_std, p + 1)
                if p >= 3:
                    dve.wait_ge(d_lo, p - 2)
                need(dve, d_t, p)
                nc.vector.reciprocal(rinv[:, :], std[:, :]).then_inc(d_rinv, 1)
                nc.vector.tensor_scalar(scr[:, p % 3, :], psum[:, 4 + p, :], OVERFLOW, DOWN, ALU.is_lt,
                                        ALU.mult).then_inc(d_rinv, 1)
                dve.wait_ge(d_rinv, 3 * p + 2)
                nc.vector.tensor_tensor(rinv[:, :], rinv[:, :], scr[:, p % 3, :], ALU.mult).then_inc(d_rinv, 1)
                dve.wait_ge(d_rinv, 3 * p + 3)
                nc.vector.scalar_tensor_tensor(out=scr[:, p % 3, :], in0=qa[:, 2 * p:2 * p + 2, :].rearrange("p s t -> p (s t)"),
                                               scalar=g_sub, in1=rinv[:, :], op0=ALU.mult,
                                               op1=ALU.mult).then_inc(d_t, 1)
                if p:
                    diff_lo(dve, p - 1)
            diff_lo(dve, 3)

        def dil_tensor(pe):
            def turns(j):
                pe.wait_ge(at_pn, C_PN + 2 * (j + 1))
                need(pe, at_pt, C_PT + 3 * j)
                for g in range(3):
                    for q in range(2):
                        for k in range(2):
                            made = nc.tensor.transpose(psum[:, 3 + g, k * T + q * P:k * T + (q + 1) * P],
                                                       scr[:, 3 * (j % 2) + g, q * T + k * P:q * T + (k + 1) * P], ident)
                    made.then_inc(at_t, 1)

            def outputs(j):
                pe.wait_ge(at_pt, C_PT + 3 * (j + 1))
                r = slice(64 * (j % 2), 64 * (j % 2) + 64)
                for g in range(3):
                    for k in range(2):
                        c = 64 * (4 * g + j)
                        made = nc.tensor.matmul(psum[r, 6 + j // 2, 0:T], vd[:, k, c:c + 64],
                                                pt_b2[:, g * TT + k * T:g * TT + (k + 1) * T],
                                                start=g == k == 0, stop=g == 2 and k == 1)
                made.then_inc(at_o, 1)

            for j in range(DIL_OUT):
                need(pe, at_mx, C_MX + 5 * (j - 1) + 3)
                if j == 0:
                    pe.wait_ge(d_t, 4)
                for g in range(3):
                    hd = 4 * g + j
                    r = slice(64 * (hd % 2), 64 * (hd % 2) + 64)
                    for q in range(2):
                        made = nc.tensor.matmul(psum[:, g, block_cols(q)], qd[r, hd // 2, q * P:(q + 1) * P],
                                                kd[r, hd // 2, :], start=True, stop=True)
                    made.then_inc(at_s, 1)
                if j:
                    turns(j - 1)
                    outputs(j - 1)
            turns(DIL_OUT - 1)
            outputs(DIL_OUT - 1)

        def dil_scalar(act):
            def finish(j):
                need(act, at_o, C_O + j)
                for g in range(3):
                    act.wait_ge(at_t, C_T + 3 * j + g + 1)
                    nc.scalar.activation(pt_b2[:, g * TT:(g + 1) * TT], psum[:, 3 + g, :], ACT.Copy).then_inc(at_pt, 1)
                if j % 2:
                    act.wait_ge(at_o, C_O + j + 1)
                    p = j // 2
                    nc.scalar.activation(a_hi[:, 0, block_cols(p)], psum[:, 6 + p, 0:T], ACT.Copy).then_inc(d_hi, 1)

            for j in range(DIL_OUT):
                act.wait_ge(at_mx, C_MX + 5 * (j + 1))
                for q in range(2):
                    rows = scr[:, 3 * (j % 2):3 * (j % 2) + 3, block_cols(q)]
                    nc.scalar.activation(rows, rows, ACT.Exp, bias=row_neg[:, j % 2, q:q + 1], scale=B2_SCALE,
                                         accum_out=row_sum[:, j % 2, q:q + 1]).then_inc(at_e, 1)
                if j:
                    finish(j - 1)
            finish(DIL_OUT - 1)

        def dil_vector(dve):
            def lo(p):
                dve.wait_ge(d_hi, 4 + p + 1)
                nc.vector.tensor_tensor(a_lo[:, 0, block_cols(p)], psum[:, 6 + p, 0:T],
                                        a_hi[:, 0, block_cols(p)].bitcast(F32), ALU.subtract).then_inc(d_lo, 1)

            dve.wait_ge(tab_in, 32)
            masks = (dil_mask[:, 0:2, :], double(dil_mask[:, 2, :]), double(dil_mask[:, 3, :]))
            for j in range(DIL_OUT):
                par_ = j % 2
                if j == 0:
                    dve.wait_ge(d_lo, 4)
                if j == 1:
                    dve.wait_ge(d_ss, 4)
                need(dve, at_t, C_T + 3 * (j - 1))
                for g in range(3):
                    dve.wait_ge(at_s, C_S + 3 * j + g + 1)
                    nc.vector.tensor_tensor(scr[:, 3 * par_ + g, :].rearrange("p (q k) -> p q k", q=2), bank2(g),
                                            masks[g], ALU.add).then_inc(at_mx, 1)
                dve.wait_ge(at_mx, C_MX + 5 * j + 3)
                for q in range(2):
                    made = nc.vector.tensor_reduce(row_max[:, par_, q:q + 1],
                                                   scr[:, 3 * par_:3 * par_ + 3, block_cols(q)], AX.XY, ALU.max)
                made.then_inc(at_mx, 1)
                dve.wait_ge(at_mx, C_MX + 5 * j + 4)
                nc.vector.tensor_scalar(row_neg[:, par_, 0:2], row_max[:, par_, 0:2], -B2_SCALE, None,
                                        ALU.mult).then_inc(at_mx, 1)
                dve.wait_ge(at_e, C_E + 2 * (j + 1))
                nc.vector.reciprocal(row_inv[:, par_, 0:2], row_sum[:, par_, 0:2]).then_inc(at_rs, 1)
                dve.wait_ge(at_rs, C_RS + j + 1)
                for q in range(2):
                    rows = scr[:, 3 * par_:3 * par_ + 3, block_cols(q)]
                    nc.vector.tensor_scalar(rows, rows, row_inv[:, par_, q:q + 1], None, ALU.mult).then_inc(at_pn, 1)
                if j == 2:
                    lo(0)
            lo(1)

        PJ = AT["proj"]

        def proj_tensor(pe):
            pe.wait_ge(d_lo, 4)
            for s in range(4):
                for which in range(2):
                    i, bank = PJ + 2 * s + which, 2 * (s % 2) + which
                    begin_stripe(pe, i)
                    if which == 0:
                        need(pe, p_m, s - 1)
                        if s == 0:
                            pe.wait_ge(at_mx, C_MX + 5 * DIL_OUT)
                    acts = h_cols(T, TT) if which else h_cols(0, T)
                    for t in range(2):
                        product(pe, psum[:, bank, block_cols(t)], i, t * P, acts, t == 0, p_sums if t else None)
            begin_stripe(pe, PJ + 8)
            pe.wait_ge(d_lo, 6)
            pe.wait_ge(at_pt, C_PT + 3 * DIL_OUT)
            for m in range(KD):
                product(pe, psum[:, 4 + m // 2, block_cols(m % 2)], PJ + 8, m * P,
                        lambda k: (a_hi[:, 0, block_cols(k)], a_lo[:, 0, block_cols(k)]), m == 0,
                        p_sums if m == KD - 1 else None, tiles=2, pitch=D)
            for s in range(4):
                begin_stripe(pe, PJ + 9 + s)
                need(pe, p_m, 4 if s == 0 else 0)
                need(pe, p_sig, 4 + s - 1)
                for t in range(2):
                    product(pe, psum[:, 2 + s % 2, block_cols(t)], PJ + 9 + s, t * P, h_cols(T, TT), t == 0,
                            p_sums if t else None)

        def proj_scalar(act):
            for s in range(4):
                ahead_hi(act, PJ + 2 * s)
                ahead_hi(act, PJ + 2 * s + 1)
                act.wait_ge(p_sums, 2 * s + 2)
                need(act, p_m, s - 1)
                nc.scalar.activation(sgate[:, s % 2, :], psum[:, 2 * (s % 2) + 1, :], ACT.Sigmoid).then_inc(p_sig, 1)
            ahead_hi(act, PJ + 8)
            for s in range(4):
                ahead_hi(act, PJ + 9 + s)
                act.wait_ge(p_sums, 9 + s + 1)
                need(act, p_m, 4 + 2 * (s - 1) if s else 3)
                nc.scalar.activation(sgate[:, s % 2, :], psum[:, 2 + s % 2, :], ACT.Sigmoid).then_inc(p_sig, 1)
                if s:
                    merged_hi(act, s - 1)
            merged_hi(act, 3)

        def merged_hi(act, s):
            act.wait_ge(p_m, 4 + 2 * (s + 1))
            nc.scalar.activation(h_hi[:, 2 * s:2 * s + 2, 0:T], yb[:, 2 * s:2 * s + 2, :], ACT.Copy).then_inc(p_hi, 1)

        def merged_lo(dve, s):
            dve.wait_ge(p_hi, s + 1)
            nc.vector.tensor_tensor(h_lo[:, 2 * s:2 * s + 2, 0:T], yb[:, 2 * s:2 * s + 2, :],
                                    h_hi[:, 2 * s:2 * s + 2, 0:T].bitcast(F32), ALU.subtract).then_inc(p_lo, 1)

        def proj_vector(dve):
            for s in range(4):
                ahead_lo(dve, PJ + 2 * s)
                ahead_lo(dve, PJ + 2 * s + 1)
                dve.wait_ge(p_sig, s + 1)
                nc.vector.tensor_tensor(yb[:, 2 * s:2 * s + 2, :], sgate[:, s % 2, :].rearrange("p (s t) -> p s t", s=2),
                                        bank2(2 * (s % 2)), ALU.mult).then_inc(p_m, 1)
            ahead_lo(dve, PJ + 8)
            for s in range(4):
                ahead_lo(dve, PJ + 9 + s)
                dve.wait_ge(p_sig, 4 + s + 1)
                dve.wait_ge(p_m, 4 + 2 * s)
                g = sgate[:, s % 2, :].rearrange("p (s t) -> p s t", s=2)
                y = yb[:, 2 * s:2 * s + 2, :]
                nc.vector.tensor_tensor(g, g, bank2(4 + s), ALU.mult).then_inc(p_m, 1)
                dve.wait_ge(p_m, 4 + 2 * s + 1)
                nc.vector.tensor_tensor(y, y, g, ALU.add).then_inc(p_m, 1)
                if s:
                    merged_lo(dve, s - 1)
            merged_lo(dve, 3)

        PAR_ROWS = (112, 99, 89, 56)

        block = ctx.enter_context(nc.Block())

        @block.sync
        def _(sp):
            sp.dma_start(const[:, 0:5 * P + 1], a["const_base"]).then_inc(base_in, 16)
            rows = par_rows
            packs = [
                (0, [(a["c"], 8), (a["c_ctx"].unsqueeze(0), 8), (a["b_mod"], 96)]),
                (1, [(a["ffn_conv_w"][0], 66), (a["ffn_conv_b"][0:1], 22), (a["mla_g_q"], 3), (a["mla_g_kv"], 2),
                     (a["pool_scale"], 4), (a["gqa_g_q"], 1), (a["gqa_g_k"], 1)]),
                (2, [(a["ffn_conv_w"][1], 66), (a["ffn_conv_b"][1:2], 22), (a["g_subln_2"], 1)]),
                (3, [(a["g_final"].unsqueeze(0), 8)] + [(a[n], 8) for n in (
                    "g_pre_ffn1_2", "g_post_ffn1_2", "g_pre_mix_2", "g_post_mix_2", "g_pre_ffn2_2", "g_post_ffn2_2")]),
            ]
            count = 0
            for p, parts in packs:
                at = 0
                for src, n in parts:
                    sp.dma_start(rows[at:at + n, p, :], src.rearrange("l (t q) -> (l t) q", q=P)).then_inc(par_in, 16)
                    at += n
                    count += 1
                assert at == PAR_ROWS[p]
            assert count == 20
            sp.dma_start(ctx_rows, a["ctx"][0].rearrange("(t p) n -> p t n", p=P)).then_inc(rows_in, 16)
            sp.dma_start(lat_rows, a["x"][0].rearrange("(t p) n -> p t n", p=P)).then_inc(rows_in, 16)
            for i in range(3):
                load(sp, i, stripe_source(i))
            for dst, src in ((w_uq, a["mla_w_uq"]), (w_uk, a["mla_w_uk"]), (w_uv, a["mla_w_uv"])):
                sp.dma_start(dst, src[0].rearrange("(k p) n -> p k n", p=P)).then_inc(small_in, 16)
            sp.dma_start(w_pool, a["pool_w"][0].rearrange("g p n -> p g n")).then_inc(small_in, 16)
            sp.dma_start(tab_mla, a["rope_mla"].rearrange("p (s t) -> p s t", s=2)).then_inc(small_in, 16)
            for i in range(3, AT["ffn0"]):
                load(sp, i, stripe_source(i))

            def ffn_loads(f):
                i0 = AT[f"ffn{f}"]
                up_name, layer, _, _ = STRIPES[i0]
                down_name = STRIPES[i0 + 4][0]
                up = a[up_name][layer].rearrange("(k p) n -> p k n", p=P)
                down = a[down_name][layer].rearrange("(k p) n -> p k n", p=P)
                load(sp, i0, stripe_source(i0))
                load(sp, i0 + 1, stripe_source(i0 + 1))
                if f == 0:
                    sp.wait_ge(pool_sums, 4)
                    sp.wait_ge(at_o, 8)
                    sp.dma_start(tab_gqa, a["rope_gqa"].rearrange("p (s t) -> p s t", s=2)).then_inc(tab_in, 16)
                if f == 2:
                    sp.dma_start(dil_mask, a["dil_mask"].rearrange("p (g t) -> p g t", g=4)).then_inc(tab_in, 16)
                with sp.Fori(0, PAIRS - 1) as n:
                    load(sp, i0 + 2, up[:, :, bass.ds(256 * n + 256, 256)], n)
                    load(sp, i0 + 3, up[:, :, bass.ds(256 * n + FF + 256, 256)], n)
                    load(sp, i0 + 4, down[:, bass.ds(2 * n, 2), :], n)
                load(sp, i0 + 3 * PAIRS - 1, stripe_source(i0 + 3 * PAIRS - 1))

            ffn_loads(0)
            for i in range(AT["gqa_in"], AT["ffn1"]):
                load(sp, i, stripe_source(i))
            ffn_loads(1)
            ffn_loads(2)
            for i in range(AT["qkv"], AT["ffn3"]):
                load(sp, i, stripe_source(i))
            ffn_loads(3)
            for t in range(2):
                sp.wait_ge(y_rows, 2 * t + 2)
                sp.dma_start(out[0, t * P:(t + 1) * P, :], out_rows[:, t, :]).then_inc(stored, 16)
            sp.wait_ge(stored, 32)

        @block.gpsimd
        def _(pool):
            nc.gpsimd.memset(small_w[:, 0:1], EPS)
            nc.gpsimd.memset(silu_all[:, 2 * KD:], 0.0)
            nc.gpsimd.memset(small_w[:, 1:2], EPS * 2.0 ** -40).then_inc(fill, 1)
            def mod_load(batch, k, layer, at):
                src = a["w_mod"][layer][k * P:(k + 1) * P, bass.ds(STRIPE * at, STRIPE)]
                slot = k % 2
                if isinstance(batch, int) and batch == 0:
                    if 2 <= k < 6:
                        pool.dma_start(mod_early_ring[:, k - 2, :], src).then_inc(mod_early[k - 2], 16)
                        return
                    if k >= 6:
                        pool.wait_ge(mod_stripes, k - 5)
                else:
                    pool.wait_ge(mod_stripes, 8 * batch + k - 1)
                pool.dma_start(mod_ring[:, slot, :], src).then_inc(mod_in[slot], 16)

            for k in range(KD):
                mod_load(0, k, 0, 0)
            pool.wait_ge(x_turned, KD)
            pool.dma_start(pool_inv, a["pool_inv"].rearrange("p (g t) -> p g t", g=4)).then_inc(inv_in, 16)
            for g in range(4):
                for s in range(2):
                    for c in (0, PAD + T):
                        made = nc.gpsimd.memset(pool_p[:, g, s, c:c + PAD], 0.0)
            made.then_inc(pool_pads, 1)
            with pool.Fori(1, 3) as batch:
                for k in range(KD):
                    mod_load(batch, k, 0, batch)
            pool.wait_ge(pool_pads, 1)
            pool_gpsimd(pool)
            pool.wait_ge(o_sums, 1)
            with pool.Fori(3, 6) as batch:
                for k in range(KD):
                    mod_load(batch, k, 1, batch - 3)
            pool.wait_ge(f_x, x_base(2))
            pool.dma_start(pos_i.bitcast(I32), a["positions_2"].broadcast_to([P, T])).then_inc(b2_in, 16)
            for i, name in enumerate(("lambda_q1_2", "lambda_k1_2", "lambda_q2_2", "lambda_k2_2")):
                pool.dma_start(lam_rows[:, i, :], a[name].broadcast_to([P, 64])).then_inc(b2_in, 16)

        @block.tensor
        def _(pe):
            pe.wait_ge(base_in, 16)
            pe.wait_ge(par_in, 320)
            for p, n in enumerate(PAR_ROWS):
                nc.tensor.transpose(psum[:, 4 + p, 0:n], par_rows[0:n, p, :], ident[0:n, 0:n]).then_inc(par_turned, 1)
            pe.wait_ge(rows_in, 32)
            for m in range(KD):
                need(pe, x_in, m - 3)
                for t in range(4):
                    src = (ctx_rows if t < 2 else lat_rows)[:, t % 2, m * P:(m + 1) * P]
                    made = nc.tensor.transpose(psum[:, m % 4, t * P:(t + 1) * P], src, ident)
                made.then_inc(x_turned, 1)
            norm_tensor(pe, 0)
            pe.wait_ge(c_ready, 1)
            pe.wait_ge(fill, 1)
            pe.wait_ge(par_ready, 4)
            for i in range(KD + 1):
                mod_step(pe, 0, i)
            pe.wait_ge(x_in, KD)
            mix_in_tensor(pe)
            values_tensor(pe)
            mod_turn(pe, 2)
            mla_tensor(pe)
            pool_tensor(pe)
            mix_out_tensor(pe)
            norm_tensor(pe, 1)
            ffn_tensor(pe, 0)
            norm_tensor(pe, 2)
            gqa_in_tensor(pe)
            gqa_tensor(pe)
            out_tensor(pe, GO, lambda k: pe.wait_ge(at_lo, 8 + k + 1))
            norm_tensor(pe, 3)
            ffn_tensor(pe, 1)
            norm_tensor(pe, 4)
            norm_tensor(pe, 5)
            ffn_tensor(pe, 2)
            norm_tensor(pe, 6)
            norm_tensor(pe, 7)
            qkv_tensor(pe)
            diff_tensor(pe)
            dil_tensor(pe)
            proj_tensor(pe)
            out_tensor(pe, WO, lambda k: pe.wait_ge(p_lo, k // 2 + 1))
            norm_tensor(pe, 8)
            norm_tensor(pe, 9)
            ffn_tensor(pe, 3)
            norm_tensor(pe, 10)
            for t in range(2):
                for m in range(KD):
                    pe.wait_ge(n_x, 8 + m // 2 + 1)
                    made = nc.tensor.transpose(psum[:, 2 * t + m // 4, (m % 4) * P:(m % 4 + 1) * P],
                                               X[:, m, T + t * P:T + (t + 1) * P], ident)
                    if m % 4 == 3:
                        made.then_inc(y_turned, 1)

        @block.scalar
        def _(act):
            act.wait_ge(par_ready, 1)
            nc.scalar.activation(silu_c[:, :, 1], par[:, 0, 0:8], ACT.Silu)
            nc.scalar.activation(silu_c[:, :, 0], par[:, 0, 8:16], ACT.Silu).then_inc(c_ready, 1)
            act.wait_ge(fill, 1)
            act.wait_ge(par_ready, 4)
            split_hi(act, 0)
            split_hi(act, 1)
            norm_scalar(act, 0, x_chunk(0), lambda c: (x_in, c + 1))
            mix_in_scalar(act)
            mla_scalar(act)
            pool_scalar(act)
            ahead_scalar(act, MO, 4)
            norm_scalar(act, 1, x_chunk(1), lambda c: (o_evac, c + 1))
            ffn_scalar(act, 0)
            norm_scalar(act, 2, x_chunk(2), lambda c: (f_x, x_base(1) - 7 + c))
            gqa_in_scalar(act)
            gqa_scalar(act)
            ahead_scalar(act, GO, 4)
            norm_scalar(act, 3, x_chunk(3), lambda c: (o_evac, 8 + c + 1))
            ffn_scalar(act, 1)
            norm_scalar(act, 4, x_chunk(4), lambda c: (f_x, x_base(1) + 2 * c + 2))
            norm_scalar(act, 5, x_chunk(5), lambda c: (n_t, chunks_before(4) + c + 1))
            tables_scalar(act)
            ffn_scalar(act, 2)
            norm_scalar(act, 6, y_chunk, lambda c: (f_x, x_base(2) + c + 1))
            norm_scalar(act, 7, x_chunk(7), lambda c: (n_x, c + 1))
            qkv_scalar(act)
            diff_scalar(act)
            dil_scalar(act)
            proj_scalar(act)
            ahead_scalar(act, WO, 4)
            norm_scalar(act, 8, y_chunk, lambda c: (o_evac, 12 + c + 1))
            norm_scalar(act, 9, x_chunk(9), lambda c: (n_x, 4 + c + 1))
            ffn_scalar(act, 3)
            norm_scalar(act, 10, y_chunk, lambda c: (f_x, x_base(3) + c + 1))

        @block.vector
        def _(dve):
            for p, n in enumerate(PAR_ROWS):
                dve.wait_ge(par_turned, p + 1)
                nc.vector.tensor_copy(par[:, p, 0:n], psum[:, 4 + p, 0:n]).then_inc(par_ready, 1)
            split_lo(dve, 0)
            split_lo(dve, 1)
            for m in range(KD):
                dve.wait_ge(x_turned, m + 1)
                nc.vector.tensor_copy(X[:, m, :], psum[:, m % 4, :]).then_inc(x_in, 1)
            dve.wait_ge(par_ready, 4)
            mod_copy(dve, 0)
            mod_store(dve, 0, 0, 0)
            dve.wait_ge(mod_ready, 1)
            mod_plus_one(dve, 0, 0)
            dve.wait_ge(mod1_ready, 1)
            norm_vector(dve, 0, x_chunk(0))
            mix_in_vector(dve)
            mla_vector(dve)
            pool_vector(dve)
            mix_out_vector(dve)
            norm_vector(dve, 1, x_chunk(1))
            ffn_vector(dve, 0)
            norm_vector(dve, 2, x_chunk(2))
            gqa_in_vector(dve)
            gqa_vector(dve)
            gqa_out_vector(dve)
            norm_vector(dve, 3, x_chunk(3))
            ffn_vector(dve, 1)
            norm_vector(dve, 4, x_chunk(4))
            norm_vector(dve, 5, x_chunk(5))
            tables_vector(dve)
            ffn_vector(dve, 2)
            norm_vector(dve, 6, y_chunk, 0.5)
            norm_vector(dve, 7, x_chunk(7))
            qkv_vector(dve)
            diff_vector(dve)
            dil_vector(dve)
            proj_vector(dve)
            w_out_vector(dve)
            norm_vector(dve, 8, y_chunk, 1.0)
            norm_vector(dve, 9, x_chunk(9))
            ffn_vector(dve, 3)
            norm_vector(dve, 10, y_chunk, 0.5)
            for b in range(4):
                dve.wait_ge(y_turned, b + 1)
                nc.vector.tensor_copy(out_rows[:, b // 2, (b % 2) * TT:(b % 2 + 1) * TT], psum[:, b, :]).then_inc(y_rows, 1)


def shape_constants():
    f = np.float32
    base = np.zeros((P, 5 * P + 1), f)
    base[:, 0:P] = np.eye(P)
    base[:, P:2 * P] = 1
    rot = np.zeros((3, P, P), f)
    for which, rows in ((0, range(NOPE, MLA_QK, 2)), (1, range(0, P, 2))):
        for r in rows:
            rot[which, r + 1, r], rot[which, r, r + 1] = -1, 1
    for r in range(P):
        if r % 64 < 8:
            rot[2, r + 8, r], rot[2, r, r + 8] = -1, 1
    base[:, 2 * P:5 * P] = rot.transpose(1, 0, 2).reshape(P, 3 * P)
    inv = f(500000.0) ** (-(np.arange(0, 16, 2, dtype=f) / f(16)))
    for r in range(P):
        if r % 64 < 16:
            base[r, 5 * P] = inv[r % 8]

    def tables(dim, first, rows):
        n = dim // 4
        freq = f(10000.0) ** (-np.arange(n, dtype=f) / f(n))
        row = np.repeat(np.arange(T // 64, dtype=f), 64)
        col = np.tile(np.arange(64, dtype=f), T // 64)
        ang = np.concatenate([row[:, None] * freq, col[:, None] * freq], -1)
        out = np.zeros((P, 2, T), f)
        out[:, 0] = 1
        for r in range(first, rows):
            out[r, 0], out[r, 1] = np.cos(ang[:, (r - first) // 2]), np.sin(ang[:, (r - first) // 2])
        return out.reshape(P, 2 * T)

    t = np.arange(T)
    inverse = np.stack([1 / (np.minimum(t - w // 2 + w, T) - np.maximum(t - w // 2, 0)).astype(f) for w in WINDOWS])
    i, j = np.arange(T)[:, None], np.arange(T)[None, :]
    near = np.where(abs(i - j) <= 64, 0, NEG).reshape(2, P, T).transpose(1, 0, 2)
    apart = [np.where((i[:P] - j) % d == 0, 0, NEG)[:, None] for d in (4, 16)]
    return {
        "const_base": base,
        "rope_mla": tables(ROPE, NOPE, MLA_QK),
        "rope_gqa": tables(P, 0, P),
        "pool_inv": np.broadcast_to(inverse.astype(f).reshape(1, -1), (P, 4 * T)).copy(),
        "dil_mask": np.concatenate([near, *apart], 1).astype(f).reshape(P, 4 * T),
    }


INPUTS = ["x", "c", "ctx", "c_ctx", "w_mod", "b_mod", "mix0_w_in", "mla_g_q", "mla_w_uq", "mla_g_kv", "mla_w_uk",
          "mla_w_uv", "pool_w", "pool_scale", "mix0_w_out", "gqa_w_in", "gqa_g_q", "gqa_g_k", "gqa_w_out",
          "ffn_w_up", "ffn_conv_w", "ffn_conv_b", "ffn_w_down", "g_final", "positions_2", "w_in_2",
          "lambda_q1_2", "lambda_k1_2", "lambda_q2_2", "lambda_k2_2", "g_subln_2", "w_proj_a_2", "w_proj_b_2",
          "w_out_2", "w_gu1_2", "w_down1_2", "w_gu2_2", "w_down2_2", "g_pre_ffn1_2", "g_post_ffn1_2",
          "g_pre_mix_2", "g_post_mix_2", "g_pre_ffn2_2", "g_post_ffn2_2"]


def kernel(**inputs):
    import concourse.bacc as bacc
    from concourse.bass_utils import run_bass_kernel_spmd

    nc = bacc.Bacc("TRN2", target_bir_lowering=False, num_devices=1)
    arrays, aps = {}, {}
    for name, value in [(n, inputs[n]) for n in INPUTS] + list(shape_constants().items()):
        value = np.ascontiguousarray(value)
        if name == "ffn_conv_w":
            value = value.reshape(value.shape[0], 1, -1)
        arrays[f"in_{name}"] = value
        aps[name] = nc.dram_tensor(f"in_{name}", value.shape, mybir.dt.from_np(value.dtype),
                                   kind="ExternalInput").ap()
    out = nc.dram_tensor("out", (1, T, D), F32, kind="ExternalOutput").ap()
    build(nc, aps, out)
    result = run_bass_kernel_spmd(nc, [arrays], core_ids=[0])
    return result.results[0]["out"]
```

```python
from contextlib import ExitStack

import numpy as np
import concourse.bass as bass
from concourse import mybir

F32 = mybir.dt.float32
F32R = mybir.dt.float32r
I32 = mybir.dt.int32
ALU = mybir.AluOpType
ACT = mybir.ActivationFunctionType
AX = mybir.AxisListType

P = 128
D = 1024
KD = D // P
T = 256
TT = 2 * T
EPS = 1e-6
FF = 2816
NFF = FF // P
PAIRS = NFF // 2
STRIPE = 2048
RING = 3

MLA_H, NOPE, ROPE, MLA_QK = 8, 64, 32, 96
QR, KVR = 384, 256
MLA_SCALE = float(MLA_QK) ** -0.5
GQA_SCALE = 128.0 ** -0.5
B2_SCALE = 0.125
LAMBDA_INIT = 0.2
DIL_OUT = 4
WINDOWS = (2, 4, 8, 16)
PAD = 8
NEG = -1e30


def stripes():
    out, at = [], {}

    def add(stage, items):
        at[stage] = len(out)
        out.extend(items)

    def columns(name, layer, starts):
        return [(name, layer, "cols", c) for c in starts]

    def ffn(up, down, layer):
        g = [(up, layer, "cols", 256 * j) for j in range(PAIRS)]
        u = [(up, layer, "cols", FF + 256 * j) for j in range(PAIRS)]
        d = [(down, layer, "rows", 256 * j) for j in range(PAIRS)]
        order = [g[0], u[0]]
        for j in range(1, PAIRS):
            order += [g[j], u[j], d[j - 1]]
        return order + [d[-1]]

    add("mix_in", columns("mix0_w_in", 0, (0, 256, 512, 672, 928)))
    add("mix_out", columns("mix0_w_out", 0, range(0, D, 256)))
    add("ffn0", ffn("ffn_w_up", "ffn_w_down", 0))
    add("gqa_in", columns("gqa_w_in", 0, range(0, 1536, 256)))
    add("gqa_out", columns("gqa_w_out", 0, range(0, D, 256)))
    add("ffn1", ffn("ffn_w_up", "ffn_w_down", 1))
    add("ffn2", ffn("w_gu1_2", "w_down1_2", 0))
    qk = [*range(0, 2048, 256), *range(3072, 3840, 256), *range(3840, 4608, 256)]
    v = [*range(2048, 3072, 256), *range(4608, 5376, 256)]
    add("qkv", columns("w_in_2", 0, qk + v))
    gate_b = columns("w_in_2", 0, range(6400, 7424, 256))
    add("gate_a", columns("w_in_2", 0, range(5376, 6400, 256)))
    add("gate_b01", gate_b[:2])
    add("proj_a", columns("w_proj_a_2", 0, range(0, D, 256)))
    add("gate_b2", gate_b[2:3])
    add("proj_b", [("w_proj_b_2", 0, "rows", 0)])
    add("gate_b3", gate_b[3:])
    add("w_out", columns("w_out_2", 0, range(0, D, 256)))
    add("ffn3", ffn("w_gu2_2", "w_down2_2", 0))
    return out, at


STRIPES, AT = stripes()


def need(eng, sem, value):
    if isinstance(value, int) and value <= 0:
        return
    eng.wait_ge(sem, value)


def build(nc, a, out):
    ctx = ExitStack()
    with ctx:
        def sem(name):
            return ctx.enter_context(nc.semaphore(name))

        def sb(name, shape, dt=F32):
            return ctx.enter_context(nc.sbuf_tensor(name, shape, dt))

        w_raw = sb("w_raw", [P, RING, STRIPE])
        w_hi = sb("w_hi", [P, RING, STRIPE], F32R)
        w_lo = sb("w_lo", [P, RING, STRIPE], F32R)
        X = sb("X", [P, KD, TT])
        h_at = nc.sbuf_base
        h_hi = sb("h_hi", [P, KD, TT], F32R)
        h_lo = sb("h_lo", [P, KD, TT], F32R)
        mod_early_ring = nc.alloc_sbuf_tensor_at("mod_early_ring", [P, 4, STRIPE], F32, offset=h_at)
        scr = sb("scr", [P, 6, TT])
        std = sb("std", [P, TT])
        rinv = sb("rinv", [P, TT])
        const = sb("const", [P, 5 * P + 8])
        par = sb("par", [P, 4, P])
        mod = sb("mod", [P, 2, 48, 2])
        mod1 = sb("mod1", [P, 2, 2, 8, 2])
        silu_all = sb("silu_all", [P, 2 * KD + 30])
        silu_c = silu_all[:, 0:2 * KD].rearrange("p (k s) -> p k s", s=2)
        small = sb("small", [P, 64])
        small_w = sb("small_w", [P, 8])
        ident, ones = const[:, 0:P], const[:, P:2 * P]
        rot_mla, rot_gqa, rot_b2 = (const[:, i * P:(i + 1) * P] for i in (2, 3, 4))
        inv_freq = const[:, 5 * P:5 * P + 1]
        eps, eps_down = small_w[:, 0:1], small_w[:, 1:2]

        U = sb("U", [P, 14720])
        u2_at = nc.sbuf_base
        U2 = sb("U2", [P, 2112])
        a_hi = nc.alloc_sbuf_tensor_at("a_hi", [P, 2, TT], F32R, offset=u2_at)
        a_lo = nc.alloc_sbuf_tensor_at("a_lo", [P, 2, TT], F32R, offset=u2_at + 8 * TT)

        def view(at, *shape):
            n = int(np.prod(shape))
            v = U[:, at:at + n]
            names = "abcd"[:len(shape)]
            if len(shape) == 1:
                return v
            return v.rearrange(f"p ({' '.join(names)}) -> p {' '.join(names)}",
                               **{names[i]: shape[i] for i in range(1, len(shape))})

        ctx_rows = view(5632, 2, D)
        lat_rows = U2[:, 0:2 * D].rearrange("p (t n) -> p t n", t=2)
        mod_ring = view(0, 2, STRIPE)
        mod_rows = view(5120, TT)
        q_mla = view(0, 2, TT)
        k_mla = view(1024, 2, TT)
        v_mla = view(2048, 4, 512)
        pt_mla = view(4096, 1536)
        w_uv = view(4096, 2, 512)
        cq = view(5632, 3, TT)
        ckv = view(7168, 2, TT)
        w_uq = view(8192, 3, 768)
        w_uk = view(10496, 2, 512)
        w_pool = view(11520, 4, P)
        pool_p = view(12032, 4, 2, T + 2 * PAD)
        tab_mla = view(14208, 2, T)
        pool_inv = U2[:, 0:1024].rearrange("p (g t) -> p g t", g=4)
        pool_a = U2[:, 1024:1568].rearrange("p (s t) -> p s t", s=2)
        pool_b = U2[:, 1568:2112].rearrange("p (s t) -> p s t", s=2)
        f_act = view(4096, 2, TT)
        q_gqa = view(5632, 8, T)
        k_gqa = view(7680, 2, TT)
        v_gqa = view(8704, 4, T)
        g_tmp = view(9728, 2, TT)
        tab_gqa = view(10752, 2, T)
        pt_gqa = view(4096, 1024)
        pt_b2 = view(0, 1536)
        t_rope = view(0, 2, TT)
        qa = view(1536, 8, T)
        ka = view(5120, 8, T)
        yb = ka
        qd = view(3584, 6, T)
        kd = view(7168, 6, T)
        va = view(8704, 2, D)
        vd = view(10752, 2, 768)
        tab_b2 = view(12288, 2, T)
        dil_mask = view(12800, 4, T)
        pos_i = view(13824, T)
        gate_a = [view(12288, TT), view(13824, TT), U2[:, TT:2 * TT], U2[:, 3 * TT:4 * TT]]
        gate_b = view(8704, 4, TT)
        out_rows = view(8704, 2, D)
        par_rows = std[:, :].rearrange("p (n c) -> p n c", c=P)
        lam_rows = view(14080, 4, 64)
        row_max, row_neg, row_sum, row_inv = (
            small[:, 8 * i:8 * i + 8].rearrange("p (h r) -> p h r", h=2) for i in range(4))
        lam, g_sub = small[:, 32:40], small[:, 40:41]

        psum = ctx.enter_context(nc.psum_tensor("psum", [P, 8, TT], F32))

        def bank2(b):
            return psum[:, b, :].rearrange("p (s t) -> p s t", s=2)

        raw_in = [sem(f"raw_in{i}") for i in range(RING)]
        hi_made, lo_made = sem("hi_made"), sem("lo_made")
        stripe_started = sem("stripe_started")
        base_in, rows_in, par_in, small_in = (sem(n) for n in ("base_in", "rows_in", "par_in", "small_in"))
        tab_in, inv_in, b2_in, fill = (sem(n) for n in ("tab_in", "inv_in", "b2_in", "fill"))
        x_turned, x_in, par_turned, par_ready = (sem(n) for n in ("x_turned", "x_in", "par_turned", "par_ready"))
        c_ready = sem("c_ready")
        mod_in = [sem(f"mod_in{i}") for i in range(2)]
        mod_early = [sem(f"mod_early{i}") for i in range(4)]
        mod_stripes, mod_rows_in, mod_turned, mod_ready, mod1_ready = (
            sem(n) for n in ("mod_stripes", "mod_rows_in", "mod_turned", "mod_ready", "mod1_ready"))
        n_sq, n_ss, n_std, n_rinv, n_t, n_hi, n_lo, n_x = (
            sem(n) for n in ("n_sq", "n_ss", "n_std", "n_rinv", "n_t", "n_hi", "n_lo", "n_x"))
        mi_sums, mi_sq, mi_ss, mi_evac, mi_std, mi_fix, mi_rot = (
            sem(n) for n in ("mi_sums", "mi_sq", "mi_ss", "mi_evac", "mi_std", "mi_fix", "mi_rot"))
        v_sums, v_evac = sem("v_sums"), sem("v_evac")
        q_sums, k_sums, q_rot, q_copied, k_copied, q_roped = (
            sem(n) for n in ("q_sums", "k_sums", "q_rot", "q_copied", "k_copied", "q_roped"))
        at_s, at_mx, at_e, at_rs, at_pn, at_t, at_pt, at_o, at_hi, at_lo = (
            sem(n) for n in ("at_s", "at_mx", "at_e", "at_rs", "at_pn", "at_t", "at_pt", "at_o", "at_hi", "at_lo"))
        pool_pads, pool_seq, pool_d, pool_sums, pool_hi, pool_lo = (
            sem(n) for n in ("pool_pads", "pool_seq", "pool_d", "pool_sums", "pool_hi", "pool_lo"))
        o_sums, o_evac = sem("o_sums"), sem("o_evac")
        f_g, f_u, f_d, f_mid, f_left, f_conv, f_silu, f_prod, f_ahi, f_alo, f_x = (
            sem(n) for n in ("f_g", "f_u", "f_d", "f_mid", "f_left", "f_conv", "f_silu", "f_prod",
                             "f_ahi", "f_alo", "f_x"))
        gi_sums, gi_evac, gi_sq, gi_rot, gi_std, gi_fix = (
            sem(n) for n in ("gi_sums", "gi_evac", "gi_sq", "gi_rot", "gi_std", "gi_fix"))
        tb_seq, tb_ang, tb_sin = sem("tb_seq"), sem("tb_ang"), sem("tb_sin")
        r_sums, r_evac, r_rot, r_fix = (sem(n) for n in ("r_sums", "r_evac", "r_rot", "r_fix"))
        d_clip, d_copied, d_sq, d_ss, d_std, d_wide, d_t, d_rinv, d_hi, d_lo = (
            sem(n) for n in ("d_clip", "d_copied", "d_sq", "d_ss", "d_std", "d_wide", "d_t", "d_rinv", "d_hi", "d_lo"))
        ga_sums, ga_kept, ga_sig, gb_sums, gb_sig, pa_sums, pb_sums, p_m, p_hi, p_lo = (
            sem(n) for n in ("ga_sums", "ga_kept", "ga_sig", "gb_sums", "gb_sig", "pa_sums", "pb_sums", "p_m", "p_hi",
                             "p_lo"))
        y_turned, y_rows, stored = sem("y_turned"), sem("y_rows"), sem("stored")

        NORMS = [(TT, "mod", 0, 1, 0), (TT, "mod", 0, 4, 3), (TT, "mod", 1, 1, 0), (T, "mod", 1, 4, 3),
                 (T, "final", 0, 0, 0), (T, "late", 8, 0, 0), (T, "post", 16, 0, 0), (T, "gain", 24, 0, 0),
                 (T, "post", 32, 0, 0), (T, "late", 40, 0, 0), (T, "post", 48, 0, 0)]


        def chunks(n):
            return KD if NORMS[n][0] == TT else KD // 2

        def chunks_before(n, kinds=("mod", "final", "gain", "post", "late")):
            return sum(chunks(i) for i in range(n) if NORMS[i][1] in kinds)

        def h_count(n, tile):
            per = KD // chunks(n)
            return chunks_before(n, ("mod", "gain", "late")) + tile // per + 1

        def blocks(n, c):
            return [(c, 0), (c, 1)] if NORMS[n][0] == TT else [(2 * c, 1), (2 * c + 1, 1)]

        def chunk_of(t, n, c):
            if NORMS[n][0] == TT:
                return t[:, c, :].rearrange("p (s t) -> p s t", s=2)
            return t[:, 2 * c:2 * c + 2, T:TT]

        def block_cols(s):
            return slice(s * T, (s + 1) * T)

        def load(sp, i, src, n=0):
            if i >= RING:
                sp.wait_ge(lo_made, i - RING + 1 + 3 * n)
            parts = 2 if src.shape[2] == D else 8
            sp.dma_start(w_raw[:, i % RING, :].rearrange("p (k n) -> p k n", k=parts),
                         src).then_inc(raw_in[i % RING], 16)

        def stripe_source(i):
            name, layer, kind, start = STRIPES[i]
            if kind == "cols":
                return a[name][layer].rearrange("(k p) n -> p k n", p=P)[:, :, start:start + 256]
            return a[name][layer].rearrange("(k p) n -> p k n", p=P)[:, start // P:start // P + 2, :]

        def split_hi(act, i, n=0):
            act.wait_ge(raw_in[i % RING], 16 * (i // RING + 1) + 16 * n)
            if i >= RING:
                act.wait_ge(stripe_started, i - RING + 2 + 3 * n)
            nc.scalar.activation(w_hi[:, i % RING, :], w_raw[:, i % RING, :], ACT.Copy).then_inc(hi_made, 1)

        def split_lo(dve, i, n=0):
            dve.wait_ge(hi_made, i + 1 + 3 * n)
            nc.vector.tensor_tensor(w_lo[:, i % RING, :], w_raw[:, i % RING, :],
                                    w_hi[:, i % RING, :].bitcast(F32), ALU.subtract).then_inc(lo_made, 1)

        def ahead_hi(act, i, n=0):
            if not isinstance(n, int) or i + 2 + 3 * n < len(STRIPES):
                split_hi(act, i + 2, n)

        def ahead_lo(dve, i, n=0):
            if not isinstance(n, int) or i + 2 + 3 * n < len(STRIPES):
                split_lo(dve, i + 2, n)

        def begin_stripe(pe, i, n=0):
            pe.wait_ge(lo_made, i + 1 + 3 * n)

        def three(dst, weight, moving, start, stop, swap=False):
            (wh, wl), (mh, ml) = weight, moving
            pairs = ((mh, wh), (ml, wh), (mh, wl)) if swap else ((wh, mh), (wh, ml), (wl, mh))
            return [nc.tensor.matmul(dst, x, y, start=start and q == 0, stop=stop and q == 2,
                                     skip_group_check=True) for q, (x, y) in enumerate(pairs)]

        def product(pe, dst, i, col, acts, first, done=None, tiles=KD, pitch=256, ready=None):
            slot = i % RING
            for k in range(tiles):
                if ready is not None:
                    ready(k)
                c = k * pitch + col
                made = three(dst, (w_hi[:, slot, c:c + P], w_lo[:, slot, c:c + P]), acts(k),
                             k == 0, k == tiles - 1)
                if first and k == 0:
                    made[0].then_inc(stripe_started, 1)
            if done is not None:
                made[-1].then_inc(done, 1)

        def product_rows(pe, dst, i, acts, first, start, done=None):
            slot = i % RING
            for k in range(KD):
                made = three(dst, (w_hi[:, slot, k * 256:(k + 1) * 256], w_lo[:, slot, k * 256:(k + 1) * 256]),
                             acts(k), start and k == 0, k == KD - 1, swap=True)
                if first and k == 0:
                    made[0].then_inc(stripe_started, 1)
            if done is not None:
                made[-1].then_inc(done, 1)

        def two_products(pe, dsts, i, acts, done, ready):
            slot = i % RING
            halves = len(done) == 1
            for k in range(KD):
                ready(k)
                for t in range(2):
                    c = 256 * k + t * P
                    made = three(dsts[t], (w_hi[:, slot, c:c + P], w_lo[:, slot, c:c + P]), acts(k),
                                 k == 0 and not (halves and t), k == KD - 1)
                    if k == t == 0:
                        made[0].then_inc(stripe_started, 1)
                    if k == KD - 1 and (t or not halves):
                        made[-1].then_inc(done[0], 1)

        def h_cols(lo, hi):
            return lambda k: (h_hi[:, k, lo:hi], h_lo[:, k, lo:hi])

        def h_ready(pe, n):
            return lambda k: pe.wait_ge(n_lo, h_count(n, k))

        def norm_bank(n):
            return 0 if n in (2, 4, 6, 10) else 6

        def norm_scalar(act, n, src, ready, between=lambda: None):
            tokens, kind, layer, _, shift = NORMS[n]
            sq0, h0 = chunks_before(n), chunks_before(n, ("mod", "gain", "late"))
            t0 = chunks_before(n, ("mod", "final", "gain", "post"))
            if kind == "late":
                for c in range(chunks(n)):
                    need(act, *ready(c))
                    for m, s in blocks(n, c):
                        made = nc.scalar.activation(h_hi[:, m, block_cols(s)], X[:, m, block_cols(s)], ACT.Copy,
                                                    scale=par[:, 3, layer + m:layer + m + 1])
                    made.then_inc(n_hi, 1)
            for c in range(chunks(n)):
                need(act, *ready(c))
                need(act, n_ss, sq0 + c - 2)
                nc.scalar.activation(scr[:, 3 + c % 3, :].rearrange("p (s t) -> p s t", s=2), src(c),
                                     ACT.Square).then_inc(n_sq, 1)
            act.wait_ge(n_ss, sq0 + chunks(n))
            if n:
                act.wait_ge(n_rinv, n)
            nc.scalar.activation(std[:, 0:tokens], psum[:, norm_bank(n), 0:tokens], ACT.Sqrt, bias=eps,
                                 scale=1.0 / D).then_inc(n_std, 1)
            between()
            if kind in ("mod", "gain"):
                for c in range(chunks(n)):
                    act.wait_ge(n_t, t0 + c + 1)
                    t = scr[:, c % 3, :].rearrange("p (s t) -> p s t", s=2)
                    if kind == "gain":
                        nc.scalar.activation(chunk_of(h_hi, n, c), t, ACT.Copy).then_inc(n_hi, 1)
                        continue
                    for b, (m, s) in enumerate(blocks(n, c)):
                        made = nc.scalar.activation(h_hi[:, m, block_cols(s)], t[:, b, :], ACT.Identity,
                                                    bias=mod[:, layer, 8 * shift + m, s:s + 1])
                    made.then_inc(n_hi, 1)

        def norm_tensor(pe, n):
            tokens = NORMS[n][0]
            sq0 = chunks_before(n)
            for c in range(chunks(n)):
                pe.wait_ge(n_sq, sq0 + c + 1)
                sq = scr[:, 3 + c % 3, :]
                for b in range(1 if tokens == TT else 2):
                    made = nc.tensor.matmul(psum[:, norm_bank(n), 0:tokens], ones, sq[:, b * T:b * T + tokens],
                                            start=c == 0 and b == 0,
                                            stop=c == chunks(n) - 1 and (tokens == TT or b == 1))
                made.then_inc(n_ss, 1)

        def norm_vector(dve, n, src, factor=1.0, between=lambda: None):
            tokens, kind, first, scale, shift = NORMS[n]
            h0 = chunks_before(n, ("mod", "gain", "late"))
            t0 = chunks_before(n, ("mod", "final", "gain", "post"))
            if kind == "late":
                for c in range(chunks(n)):
                    dve.wait_ge(n_hi, h0 + c + 1)
                    for m, s in blocks(n, c):
                        cols = block_cols(s)
                        made = nc.vector.scalar_tensor_tensor(
                            out=h_lo[:, m, cols], in0=X[:, m, cols], scalar=par[:, 3, first + m:first + m + 1],
                            in1=h_hi[:, m, cols].bitcast(F32), op0=ALU.mult, op1=ALU.subtract)
                    made.then_inc(n_lo, 1)
            dve.wait_ge(n_std, n + 1)
            nc.vector.reciprocal(rinv[:, 0:tokens], std[:, 0:tokens]).then_inc(n_rinv, 1)
            between()
            dve.wait_ge(n_rinv, n + 1)
            if kind == "late":
                return

            def scaled(c):
                t = scr[:, c % 3, :].rearrange("p (s t) -> p s t", s=2)
                for b, (m, s) in enumerate(blocks(n, c)):
                    if kind == "mod":
                        g = mod1[:, first, scale // 4, m, s:s + 1]
                    else:
                        g = par[:, 3, first + m:first + m + 1]
                    x = src(c)[:, b, :]
                    dst = t[:, b, :] if kind in ("mod", "gain") else x
                    r = rinv[:, block_cols(s)] if tokens == TT else rinv[:, 0:T]
                    made = nc.vector.scalar_tensor_tensor(out=dst, in0=x, scalar=g, in1=r,
                                                          op0=ALU.mult, op1=ALU.mult)
                made.then_inc(n_t, 1)

            def remainder(c):
                dve.wait_ge(n_hi, h0 + c + 1)
                t = scr[:, c % 3, :].rearrange("p (s t) -> p s t", s=2)
                if kind == "gain":
                    nc.vector.tensor_tensor(chunk_of(h_lo, n, c), t, chunk_of(h_hi, n, c).bitcast(F32),
                                            ALU.subtract).then_inc(n_lo, 1)
                    return
                for b, (m, s) in enumerate(blocks(n, c)):
                    cols = block_cols(s)
                    made = nc.vector.scalar_tensor_tensor(
                        out=h_lo[:, m, cols], in0=t[:, b, :], scalar=mod[:, first, 8 * shift + m, s:s + 1],
                        in1=h_hi[:, m, cols].bitcast(F32), op0=ALU.add, op1=ALU.subtract)
                made.then_inc(n_lo, 1)

            for c in range(chunks(n)):
                if kind in ("mod", "gain") and c >= 3:
                    dve.wait_ge(n_lo, h0 + c - 2)
                scaled(c)
                if kind in ("mod", "gain") and c >= 1:
                    remainder(c - 1)
                if kind == "post" and c >= 1:
                    residual(dve, n, src, c - 1, factor, t0)
            if kind in ("mod", "gain"):
                remainder(chunks(n) - 1)
            if kind == "post":
                residual(dve, n, src, chunks(n) - 1, factor, t0)

        def residual(dve, n, src, c, factor, t0):
            dve.wait_ge(n_t, t0 + c + 1)
            x = chunk_of(X, n, c)
            nc.vector.scalar_tensor_tensor(out=x, in0=src(c), scalar=factor, in1=x, op0=ALU.mult,
                                           op1=ALU.add).then_inc(n_x, 1)

        def x_chunk(n):
            return lambda c: chunk_of(X, n, c)

        def y_chunk(c):
            return yb[:, 2 * c:2 * c + 2, :]

        def mod_stripe(pe, batch, k):
            slot = k % 2
            if k == 0:
                need(pe, mod_ready, batch)
            w = mod_ring[:, slot, :]
            if isinstance(batch, int) and batch == 0:
                if 2 <= k < 6:
                    pe.wait_ge(mod_early[k - 2], 16)
                    w = mod_early_ring[:, k - 2, :]
                else:
                    pe.wait_ge(mod_in[slot], 16 if k < 2 else 32)
            else:
                pe.wait_ge(mod_in[slot], 64 * batch + 16 * (k // 2 - 1))
            for j in range(4):
                made = nc.tensor.matmul(psum[32 * j:32 * j + 32, 7, :], silu_all[:, 2 * k:2 * k + 32], w[:, TT * j:TT * (j + 1)],
                                        start=k == 0, stop=k == KD - 1, skip_group_check=True)
            made.then_inc(mod_stripes, 1)

        def mod_turn(pe, batch):
            pe.wait_ge(mod_rows_in, batch + 1)
            for q in range(4):
                made = nc.tensor.transpose(psum[:, 7, q * P:(q + 1) * P], mod_rows[:, q * P:(q + 1) * P], ident)
            made.then_inc(mod_turned, 1)

        def mod_copy(dve, batch):
            dve.wait_ge(mod_stripes, 8 * batch + 8)
            nc.vector.tensor_copy(mod_rows, psum[:, 7, :]).then_inc(mod_rows_in, 1)

        def mod_store(dve, layer, batch, at):
            dve.wait_ge(mod_turned, batch + 1)
            turned = psum[:, 7, :].rearrange("p (q j n) -> p j q n", q=4, j=4)
            b = par[:, 0, bass.ds(16 + 48 * layer + 16 * at, 16)].rearrange("p (j q) -> p j q", q=4)
            dst = mod[:, layer, bass.ds(16 * at, 16), :].rearrange("p (j q) s -> p j q s", q=4)
            for s in range(2):
                made = nc.vector.tensor_tensor(dst[:, :, :, s], turned[:, :, :, s], b, ALU.add)
            made.then_inc(mod_ready, 1)

        def mod_plus_one(dve, layer, which):
            at = 8 * (1, 4)[which]
            nc.vector.tensor_scalar(mod1[:, layer, which, :, :], mod[:, layer, at:at + 8, :], 1.0, None,
                                    ALU.add).then_inc(mod1_ready, 1)

        def mod_step(pe, batch, i):
            if i < KD:
                mod_stripe(pe, batch, i)
            else:
                mod_turn(pe, batch)

        MI = AT["mix_in"]
        MOD_AFTER = ([(1, 0), (1, 1)], [(1, 2)], [(1, 3), (1, 4)], [(1, 5)], [(1, 6), (1, 7)], [(1, 8)],
                     [(2, 0), (2, 1)], [(2, 2), (2, 3)], [(2, 4), (2, 5)], [(2, 6), (2, 7)])
        kr_raw = scr[64:96, 2, :]

        def mix_in_tensor(pe):
            for s in range(5):
                begin_stripe(pe, MI + s)
                if s == 0:
                    two_products(pe, (psum[:, 0, :], psum[:, 1, :]), MI, h_cols(0, TT), (mi_sums, mi_sums),
                                 h_ready(pe, 0))
                for t in range(2):
                    n = 2 * s + t
                    if s:
                        need(pe, mi_evac, n - 3)
                        product(pe, psum[:, n % 4, :], MI + s, 64 if n == 5 else t * P, h_cols(0, TT), t == 0,
                                mi_sums)
                    for batch, k in MOD_AFTER[n]:
                        mod_step(pe, batch, k)
                if s == 1:
                    for k in range(3):
                        pe.wait_ge(mi_sq, k + 1)
                        nc.tensor.matmul(psum[:, 4, :], ones, scr[:, 3 + k, :], start=k == 0,
                                         stop=k == 2).then_inc(mi_ss, 1)
                if s == 2:
                    for k in range(2):
                        pe.wait_ge(mi_sq, k + 4)
                        nc.tensor.matmul(psum[:, 5, :], ones, scr[:, 3 + k, :], start=k == 0,
                                         stop=k == 1).then_inc(mi_ss, 1)
                    pe.wait_ge(mi_evac, 6)
                    nc.tensor.matmul(psum[64:96, 6, 0:T], rot_mla[64:96, 64:96], kr_raw[:, T:TT],
                                     start=True, stop=True).then_inc(mi_rot, 1)

        def mix_in_scalar(act):
            for s in range(5):
                ahead_hi(act, MI + s)
                for n in (2 * s, 2 * s + 1):
                    act.wait_ge(mi_sums, n + 1)
                    bank = psum[:, n % 4, :]
                    if n < 5:
                        need(act, mi_ss, n - 2)
                        nc.scalar.activation(scr[:, 3 + n % 3, :], bank, ACT.Square).then_inc(mi_sq, 1)
                        dst = cq[:, n, :] if n < 3 else ckv[:, n - 3, :]
                        nc.scalar.activation(dst, bank, ACT.Copy,
                                             scale=par[:, 1, 88 + n:89 + n]).then_inc(mi_evac, 1)
                    elif n == 5:
                        nc.scalar.activation(kr_raw, psum[64:96, n % 4, :], ACT.Copy).then_inc(mi_evac, 1)
                    else:
                        nc.scalar.activation(pool_p[:, n - 6, :, PAD:PAD + T], bank2(n % 4),
                                             ACT.Copy).then_inc(mi_evac, 1)
                if s == 1:
                    act.wait_ge(mi_ss, 3)
                    act.wait_ge(n_rinv, 1)
                    nc.scalar.activation(std[:, :], psum[:, 4, :], ACT.Sqrt, bias=eps,
                                         scale=1.0 / QR).then_inc(mi_std, 1)
                if s == 2:
                    act.wait_ge(mi_ss, 5)
                    nc.scalar.activation(scr[:, 0, :], psum[:, 5, :], ACT.Sqrt, bias=eps,
                                         scale=1.0 / KVR).then_inc(mi_std, 1)
            for t in range(4):
                act.wait_ge(v_sums, t + 1)
                nc.scalar.activation(v_mla[:, t, :], psum[:, t, :], ACT.Copy).then_inc(v_evac, 1)

        def mix_in_vector(dve):
            def fix(inst, count):
                inst.then_inc(mi_fix, 1)
                dve.wait_ge(mi_fix, count)

            for s in range(5):
                ahead_lo(dve, MI + s)
                if s == 2:
                    dve.wait_ge(mi_std, 1)
                    fix(nc.vector.reciprocal(rinv[:, :], std[:, :]), 1)
                    for k in range(3):
                        dve.wait_ge(mi_evac, k + 1)
                        nc.vector.tensor_tensor(cq[:, k, :], cq[:, k, :], rinv[:, :], ALU.mult).then_inc(mi_fix, 1)
                if s == 3:
                    mod_store(dve, 0, 1, 1)
                    dve.wait_ge(mi_std, 2)
                    fix(nc.vector.reciprocal(scr[:, 1, :], scr[:, 0, :]), 5)
                    for k in range(2):
                        dve.wait_ge(mi_evac, k + 4)
                        nc.vector.tensor_tensor(ckv[:, k, :], ckv[:, k, :], scr[:, 1, :],
                                                ALU.mult).then_inc(mi_fix, 1)
                if s == 2:
                    mod_copy(dve, 1)
            mod_copy(dve, 2)
            mod_store(dve, 0, 2, 2)
            dve.wait_ge(mod_ready, 3)
            mod_plus_one(dve, 0, 1)
            dve.wait_ge(mi_rot, 1)
            dve.wait_ge(small_in, 80)
            k0, tmp = k_mla[64:96, 0, :], scr[64:96, 0, 0:T]
            nc.vector.tensor_copy(k0[:, 0:T], kr_raw[:, 0:T]).then_inc(mi_fix, 1)
            nc.vector.tensor_tensor(k0[:, T:TT], kr_raw[:, T:TT], tab_mla[64:96, 0, :], ALU.mult).then_inc(mi_fix, 1)
            fix(nc.vector.tensor_tensor(tmp, psum[64:96, 6, 0:T], tab_mla[64:96, 1, :], ALU.mult), 10)
            fix(nc.vector.tensor_tensor(k0[:, T:TT], k0[:, T:TT], tmp, ALU.add), 11)
            fix(nc.vector.tensor_copy(k_mla[64:96, 1, :], k0), 12)

        def values_tensor(pe):
            pe.wait_ge(small_in, 80)
            pe.wait_ge(mi_fix, 7)
            pe.wait_ge(mi_evac, 10)
            for t in range(4):
                for k in range(2):
                    made = nc.tensor.matmul(psum[:, t, :], ckv[:, k, t * P:(t + 1) * P], w_uv[:, k, :],
                                            start=k == 0, stop=k == 1)
                made.then_inc(v_sums, 1)

        def q_tensor(pe, h):
            if h == 0:
                pe.wait_ge(v_evac, 4)
                pe.wait_ge(mi_fix, 12)
            need(pe, q_roped, 3 * h)
            for k in range(3):
                made = nc.tensor.matmul(psum[0:MLA_QK, 0, :], w_uq[:, k, MLA_QK * h:MLA_QK * (h + 1)], cq[:, k, :],
                                        start=k == 0, stop=k == 2)
            made.then_inc(q_sums, 1)

        def k_tensor(pe, h):
            need(pe, k_copied, h)
            for k in range(2):
                made = nc.tensor.matmul(psum[0:NOPE, 1, :], w_uk[:, k, NOPE * h:NOPE * (h + 1)], ckv[:, k, :],
                                        start=k == 0, stop=k == 1)
            made.then_inc(k_sums, 1)

        def q_rotate_tensor(pe, h):
            pe.wait_ge(q_copied, h + 1)
            nc.tensor.matmul(psum[0:MLA_QK, 0, 0:T], rot_mla[0:MLA_QK, 0:MLA_QK], q_mla[0:MLA_QK, h % 2, T:TT],
                             start=True, stop=True).then_inc(q_rot, 1)

        def q_copy_scalar(act, h):
            act.wait_ge(q_sums, h + 1)
            need(act, at_s, 3 * (h - 1))
            nc.scalar.activation(q_mla[0:MLA_QK, h % 2, :], psum[0:MLA_QK, 0, :], ACT.Copy).then_inc(q_copied, 1)

        def k_copy_vector(dve, h):
            dve.wait_ge(k_sums, h + 1)
            need(dve, at_s, 3 * (h - 1))
            nc.vector.tensor_copy(k_mla[0:NOPE, h % 2, :], psum[0:NOPE, 1, :]).then_inc(k_copied, 1)

        def q_rope_vector(dve, h):
            dve.wait_ge(q_rot, h + 1)
            q, tmp = q_mla[0:MLA_QK, h % 2, T:TT], rinv[0:MLA_QK, 0:T]
            nc.vector.tensor_tensor(tmp, psum[0:MLA_QK, 0, 0:T], tab_mla[0:MLA_QK, 1, :], ALU.mult).then_inc(q_roped, 1)
            nc.vector.tensor_tensor(q, q, tab_mla[0:MLA_QK, 0, :], ALU.mult).then_inc(q_roped, 1)
            dve.wait_ge(q_roped, 3 * h + 2)
            nc.vector.tensor_tensor(q, q, tmp, ALU.add).then_inc(q_roped, 1)

        pt_l = pt_mla[:, 0:1024].rearrange("p (k q) -> p k q", k=4)
        pt_c = pt_mla[:, 1024:1536].rearrange("p (k q) -> p k q", k=2)
        pt_g = pt_gqa.rearrange("p (k q) -> p k q", k=4)
        MLA = dict(
            heads=8, scale=MLA_SCALE, base=0, apart=0, score_banks=((2, 1), (3, 1), (4, 2)),
            rows=((2, 0, 512, 0), (3, 0, 512, 1), (4, 0, 256, 2), (4, 256, 256, 2)),
            turns=((5, [(0, 128 * k, 128 * k) for k in range(4)], pt_l[:, :, 0:P], 1),
                   (6, [(1, 128 * k, 128 * k) for k in range(4)], pt_l[:, :, P:T], 2),
                   (1, [(2, 256 * q + 128 * k, 256 * k + 128 * q) for q in range(2) for k in range(2)],
                    pt_c[:, :, :], 4)))
        GQA = dict(
            heads=8, scale=GQA_SCALE, base=1, apart=6, score_banks=((0, 1), (1, 1)),
            rows=((0, 0, 512, 0), (1, 0, 512, 1)),
            turns=((2, [(0, 128 * k, 128 * k) for k in range(4)], pt_g[:, :, 0:P], 1),
                   (3, [(1, 128 * k, 128 * k) for k in range(4)], pt_g[:, :, P:T], 2)))

        def at_base(cfg, per):
            return cfg["base"] * MLA["heads"] * per(MLA)

        def n_rows(cfg):
            return len(cfg["rows"])

        def n_banks(cfg):
            return len(cfg["score_banks"])

        def n_turns(cfg):
            return len(cfg["turns"])

        def mla_scores(pe, h, b):
            q, k = q_mla[0:MLA_QK, h % 2, :], k_mla[0:MLA_QK, h % 2, :]
            if b < 2:
                return nc.tensor.matmul(psum[:, 2 + b, :], q[:, T + b * P:T + (b + 1) * P], k, start=True, stop=True)
            for t in range(2):
                made = nc.tensor.matmul(psum[:, 4, t * T:(t + 1) * T], q[:, t * P:(t + 1) * P], k[:, 0:T],
                                        start=True, stop=True)
            return made

        def gqa_scores(pe, h, b):
            return nc.tensor.matmul(psum[:, b + 6 * (h % 2), :], q_gqa[:, h, b * P:(b + 1) * P], k_gqa[:, h // 4, :],
                                    start=True, stop=True)

        def scores_tensor(pe, cfg, h, scores):
            before = h - 1 if cfg["apart"] else h
            need(pe, at_e, at_base(cfg, n_rows) + n_rows(cfg) * before if before > 0 or cfg["base"] else 0)
            for b in range(n_banks(cfg)):
                scores(pe, h, b).then_inc(at_s, 1)

        def turns_tensor(pe, cfg, h):
            done, turned = at_base(cfg, n_rows) + n_rows(cfg) * h, at_base(cfg, n_turns) + n_turns(cfg) * h
            banks = [b for b, *_ in cfg["turns"]]
            for g, (bank, pieces, _, rows) in enumerate(cfg["turns"]):
                pe.wait_ge(at_pn, done + rows)
                before = [x for x in range(g) if banks[x] == bank]
                last = max(x for x in range(len(banks)) if banks[x] == bank)
                need(pe, at_pt, turned + before[-1] + 1 if before else turned - n_turns(cfg) + last + 1)
                for slot, col, to in pieces:
                    made = nc.tensor.transpose(psum[:, bank, to:to + P], scr[:, 3 * (h % 2) + slot, col:col + P], ident)
                made.then_inc(at_t, 1)

        def mla_out_tensor(pe, h):
            pe.wait_ge(at_pt, 3 * (h + 1))
            need(pe, at_lo, h)
            r = slice(NOPE * (h % 2), NOPE * (h % 2) + NOPE)
            for t in range(2):
                nc.tensor.matmul(psum[r, 7, 0:T], v_mla[:, t, 64 * h:64 * (h + 1)], pt_c[:, t, :],
                                 start=t == 0, stop=t == 1)
            for t in range(4):
                made = nc.tensor.matmul(psum[r, 7, T:TT], v_mla[:, t, 64 * h:64 * (h + 1)], pt_l[:, t, :],
                                        start=t == 0, stop=t == 3)
            made.then_inc(at_o, 1)

        def gqa_out_tensor(pe, h):
            pe.wait_ge(at_pt, at_base(GQA, n_turns) + 2 * (h + 1))
            need(pe, at_lo, 8 + h - 1)
            for t in range(4):
                made = nc.tensor.matmul(psum[:, 4 + h % 2, 0:T], v_gqa[:, t, P * (h // 4):P * (h // 4 + 1)],
                                        pt_g[:, t, :], start=t == 0, stop=t == 3)
            made.then_inc(at_o, 1)

        def exp_scalar(act, cfg, h):
            n = at_base(cfg, lambda c: n_banks(c) + 1) + (n_banks(cfg) + 1) * (h + 1)
            act.wait_ge(at_mx, n)
            need(act, at_t, at_base(cfg, n_turns) + n_turns(cfg) * (h - 1))
            for r, (bank, lo, cols, slot) in enumerate(cfg["rows"]):
                bank += cfg["apart"] * (h % 2)
                nc.scalar.activation(scr[:, 3 * (h % 2) + slot, lo:lo + cols], psum[:, bank, lo:lo + cols], ACT.Exp,
                                     bias=row_neg[:, h % 2, r:r + 1], scale=cfg["scale"],
                                     accum_out=row_sum[:, h % 2, r:r + 1]).then_inc(at_e, 1)

        def turned_scalar(act, cfg, h):
            turned = at_base(cfg, n_turns) + n_turns(cfg) * h
            need(act, at_o, 8 * cfg["base"] + h)
            for g, (bank, _, dst, _) in enumerate(cfg["turns"]):
                act.wait_ge(at_t, turned + g + 1)
                k = dst.shape[1]
                nc.scalar.activation(dst, psum[:, bank, :].rearrange("p (k q) -> p k q", k=k),
                                     ACT.Copy).then_inc(at_pt, 1)

        def head_out(cfg, h):
            if cfg is MLA:
                r = slice(NOPE * (h % 2), NOPE * (h % 2) + NOPE)
                return psum[r, 7, :], h_hi[r, h // 2, :], h_lo[r, h // 2, :]
            return psum[:, 4 + h % 2, 0:T], h_hi[:, h, 0:T], h_lo[:, h, 0:T]

        def out_hi_scalar(act, cfg, h):
            act.wait_ge(at_o, 8 * cfg["base"] + h + 1)
            src, hi, _ = head_out(cfg, h)
            nc.scalar.activation(hi, src, ACT.Copy).then_inc(at_hi, 1)

        def out_lo_vector(dve, cfg, h):
            dve.wait_ge(at_hi, 8 * cfg["base"] + h + 1)
            src, hi, lo = head_out(cfg, h)
            nc.vector.tensor_tensor(lo, src, hi.bitcast(F32), ALU.subtract).then_inc(at_lo, 1)

        def max_vector(dve, cfg, h):
            scored = at_base(cfg, n_banks) + n_banks(cfg) * h
            n = at_base(cfg, lambda c: n_banks(c) + 1) + (n_banks(cfg) + 1) * h
            r = 0
            for b, (bank, blocks_) in enumerate(cfg["score_banks"]):
                dve.wait_ge(at_s, scored + b + 1)
                src = psum[:, bank + cfg["apart"] * (h % 2), :].rearrange("p (r k) -> p r k", r=blocks_)
                nc.vector.tensor_reduce(row_max[:, h % 2, r:r + blocks_], src, AX.X, ALU.max).then_inc(at_mx, 1)
                r += blocks_
            dve.wait_ge(at_mx, n + n_banks(cfg))
            nc.vector.tensor_scalar(row_neg[:, h % 2, 0:r], row_max[:, h % 2, 0:r], -cfg["scale"], None,
                                    ALU.mult).then_inc(at_mx, 1)

        def norm_rows_vector(dve, cfg, h):
            made = at_base(cfg, n_rows) + n_rows(cfg) * h
            R = n_rows(cfg)
            dve.wait_ge(at_e, made + R)
            nc.vector.reciprocal(row_inv[:, h % 2, 0:R], row_sum[:, h % 2, 0:R]).then_inc(at_rs, 1)
            dve.wait_ge(at_rs, 8 * cfg["base"] + h + 1)
            for r, (_, lo, cols, slot) in enumerate(cfg["rows"]):
                p = scr[:, 3 * (h % 2) + slot, lo:lo + cols]
                nc.vector.tensor_scalar(p, p, row_inv[:, h % 2, r:r + 1], None, ALU.mult).then_inc(at_pn, 1)

        def mla_tensor(pe):
            def turns(h):
                pe.wait_ge(k_copied, min(h + 3, MLA_H))
                turns_tensor(pe, MLA, h)

            q_tensor(pe, 0)
            k_tensor(pe, 0)
            q_rotate_tensor(pe, 0)
            q_tensor(pe, 1)
            for h in range(MLA_H):
                if h + 1 < MLA_H:
                    k_tensor(pe, h + 1)
                    q_rotate_tensor(pe, h + 1)
                pe.wait_ge(q_roped, 3 * (h + 1))
                pe.wait_ge(k_copied, h + 1)
                scores_tensor(pe, MLA, h, mla_scores)
                if h:
                    turns(h - 1)
                if h + 2 < MLA_H:
                    q_tensor(pe, h + 2)
                if h:
                    mla_out_tensor(pe, h - 1)
            turns(MLA_H - 1)
            mla_out_tensor(pe, MLA_H - 1)

        def mla_scalar(act):
            q_copy_scalar(act, 0)
            q_copy_scalar(act, 1)
            for h in range(MLA_H):
                if h:
                    turned_scalar(act, MLA, h - 1)
                exp_scalar(act, MLA, h)
                if h + 2 < MLA_H:
                    q_copy_scalar(act, h + 2)
                if h:
                    out_hi_scalar(act, MLA, h - 1)
            turned_scalar(act, MLA, MLA_H - 1)
            out_hi_scalar(act, MLA, MLA_H - 1)

        def mla_vector(dve):
            k_copy_vector(dve, 0)
            q_rope_vector(dve, 0)
            for h in range(MLA_H):
                if h + 1 < MLA_H:
                    k_copy_vector(dve, h + 1)
                    q_rope_vector(dve, h + 1)
                max_vector(dve, MLA, h)
                norm_rows_vector(dve, MLA, h)
                if h:
                    out_lo_vector(dve, MLA, h - 1)
            out_lo_vector(dve, MLA, MLA_H - 1)

        def pool_gpsimd(pool):
            seq = 0

            def then(inst):
                nonlocal seq
                seq += 1
                inst.then_inc(pool_seq, 1)
                pool.wait_ge(pool_seq, seq)

            pool.wait_ge(inv_in, 16)
            for g, w in enumerate(WINDOWS):
                pool.wait_ge(mi_evac, 7 + g)
                src, length, step = pool_p[:, g, :, :], T + 2 * PAD, 1
                while step < w:
                    dst = pool_b if src is pool_a else pool_a
                    length -= step
                    then(nc.gpsimd.tensor_tensor(dst[:, :, 0:length], src[:, :, 0:length],
                                                 src[:, :, step:step + length], ALU.add))
                    src, step = dst, 2 * step
                dst = pool_b if src is pool_a else pool_a
                inv = pool_inv[:, g, :]
                for s in range(2):
                    made = nc.gpsimd.tensor_tensor(dst[:, s, 0:T], src[:, s, PAD - w // 2:PAD - w // 2 + T], inv, ALU.mult)
                then(made)
                p = pool_p[:, g, :, PAD:PAD + T]
                nc.gpsimd.tensor_tensor(p, dst[:, :, 0:T], p, ALU.subtract).then_inc(pool_d, 1)
                pool.wait_ge(pool_d, g + 1)

        def pool_tensor(pe):
            for g in range(4):
                pe.wait_ge(pool_d, g + 1)
                if g == 0:
                    pe.wait_ge(at_e, 8 * n_rows(MLA))
                nc.tensor.matmul(psum[:, g, :], w_pool[:, g, :], pool_p[:, g, :, PAD:PAD + T], start=True,
                                 stop=True).then_inc(pool_sums, 1)

        def pool_scalar(act):
            for g in range(4):
                act.wait_ge(pool_sums, g + 1)
                nc.scalar.activation(h_hi[:, 4 + g, :], psum[:, g, :], ACT.Copy,
                                     scale=par[:, 1, 93 + g:94 + g]).then_inc(pool_hi, 1)

        def pool_vector(dve):
            for g in range(4):
                dve.wait_ge(pool_hi, g + 1)
                nc.vector.scalar_tensor_tensor(out=h_lo[:, 4 + g, :], in0=psum[:, g, :],
                                               scalar=par[:, 1, 93 + g:94 + g],
                                               in1=h_hi[:, 4 + g, :].bitcast(F32), op0=ALU.mult,
                                               op1=ALU.subtract).then_inc(pool_lo, 1)

        def double(x, n=2):
            return x.unsqueeze(1).broadcast_to([x.shape[0], n, x.shape[1]])

        MO, GO, WO = AT["mix_out"], AT["gqa_out"], AT["w_out"]

        def mix_out_tensor(pe):
            pe.wait_ge(at_lo, MLA_H)
            pe.wait_ge(pool_lo, 4)
            for m in range(KD):
                if m % 2 == 0:
                    begin_stripe(pe, MO + m // 2)
                need(pe, o_evac, m - 3)
                product(pe, psum[:, m % 4, :], MO + m // 2, m % 2 * P, h_cols(0, TT), m % 2 == 0, o_sums)

        def mix_out_vector(dve):
            for m in range(KD):
                if m % 2 == 0:
                    ahead_lo(dve, MO + m // 2)
                dve.wait_ge(o_sums, m + 1)
                for s in range(2):
                    x = X[:, m, block_cols(s)]
                    made = nc.vector.scalar_tensor_tensor(out=x, in0=psum[:, m % 4, block_cols(s)],
                                                          scalar=mod[:, 0, 16 + m, s:s + 1], in1=x,
                                                          op0=ALU.mult, op1=ALU.add)
                made.then_inc(o_evac, 1)

        def out_tensor(pe, i0, ready):
            for s in range(4):
                begin_stripe(pe, i0 + s)
                product(pe, psum[:, s, 0:T], i0 + s, 0, h_cols(0, T), True, ready=ready if s == 0 else None)
                product(pe, psum[:, s, T:TT], i0 + s, P, h_cols(0, T), False, o_sums)

        def ahead_scalar(act, i0, n):
            for i in range(i0, i0 + n):
                ahead_hi(act, i)

        def gqa_out_vector(dve):
            for s in range(4):
                ahead_lo(dve, GO + s)
                dve.wait_ge(o_sums, 8 + s + 1)
                for t in range(2):
                    x = X[:, 2 * s + t, T:TT]
                    made = nc.vector.scalar_tensor_tensor(out=x, in0=psum[:, s, block_cols(t)],
                                                          scalar=mod[:, 1, 16 + 2 * s + t, 1:2], in1=x,
                                                          op0=ALU.mult, op1=ALU.add)
                made.then_inc(o_evac, 1)

        def w_out_vector(dve):
            for s in range(4):
                ahead_lo(dve, WO + s)
                dve.wait_ge(o_sums, 12 + s + 1)
                dve.wait_ge(p_hi, s + 1)
                nc.vector.tensor_copy(yb[:, 2 * s:2 * s + 2, :], bank2(s)).then_inc(o_evac, 1)

        FFNS = [dict(wide=True, layer=0, norm=1), dict(wide=False, layer=1, norm=3),
                dict(wide=False, layer=None, norm=5), dict(wide=False, layer=None, norm=9)]

        def units(f):
            return 2 if FFNS[f]["wide"] else 1

        def unit_base(f):
            return sum(units(g) * PAIRS for g in range(f))

        def down_per(f):
            return KD if FFNS[f]["wide"] else 1

        def down_base(f):
            return sum(down_per(g) * PAIRS for g in range(f))

        def x_base(f):
            return (0, KD * PAIRS, KD * PAIRS + KD, KD * PAIRS + KD + 4)[f]

        def ffn_stripe(f, what, first):
            i0 = AT[f"ffn{f}"]
            return i0 + {"g": 0, "u": 1}[what] if first else i0 + {"g": 2, "u": 3, "d": 4}[what]

        def up_tensor(pe, f, what, i, n, j):
            U_, base = units(f), unit_base(f)
            begin_stripe(pe, i, n)
            freed = f_prod if what == "u" else f_conv
            need(pe, freed, base + U_ * j)
            done = f_g if what == "g" else f_u
            if what == "g" and isinstance(j, int) and j == 0:
                wide = FFNS[f]["wide"]
                two_products(pe, [psum[:, t, :] if wide else psum[:, 0, block_cols(t)] for t in range(2)], i,
                             h_cols(0, TT) if wide else h_cols(T, TT), (done, done) if wide else (done,),
                             h_ready(pe, FFNS[f]["norm"]))
                return
            for t in range(2):
                if FFNS[f]["wide"]:
                    product(pe, psum[:, t + (2 if what == "u" else 0), :], i, t * P, h_cols(0, TT), t == 0, done)
                else:
                    product(pe, psum[:, 1 if what == "u" else 0, block_cols(t)], i, t * P, h_cols(T, TT),
                            t == 0, done if t == 1 else None)

        def down_tensor(pe, f, i, n, j, last=False):
            begin_stripe(pe, i, n)
            pe.wait_ge(f_alo, unit_base(f) + units(f) * (j + 1))
            slot = i % RING
            started = False
            if FFNS[f]["wide"]:
                for m in range(KD):
                    need(pe, f_x, x_base(f) + KD * j + (m - 2 if m >= 3 else 0))
                    for k in range(2):
                        c = k * D + m * P
                        made = three(psum[:, 4 + m % 3, :], (w_hi[:, slot, c:c + P], w_lo[:, slot, c:c + P]),
                                     (a_hi[:, k, :], a_lo[:, k, :]), k == 0, k == 1)
                        if not started:
                            made[0].then_inc(stripe_started, 1)
                            started = True
                    made[-1].then_inc(f_d, 1)
                return
            for k in range(2):
                for m in range(KD):
                    c = k * D + m * P
                    begins = isinstance(j, int) and j == 0 and k == 0 and m % 2 == 0
                    made = three(psum[:, 4 + m // 2, block_cols(m % 2)],
                                 (w_hi[:, slot, c:c + P], w_lo[:, slot, c:c + P]),
                                 (a_hi[:, 0, block_cols(k)], a_lo[:, 0, block_cols(k)]), begins, last and k == 1)
                    if not started:
                        made[0].then_inc(stripe_started, 1)
                        started = True
            made[-1].then_inc(f_d, 1)

        def ffn_tensor(pe, f):
            i0 = AT[f"ffn{f}"]
            G, U_, D_ = (ffn_stripe(f, w, False) for w in "gud")
            up_tensor(pe, f, "g", i0, 0, 0)
            if FFNS[f]["layer"] is None:
                norm_tensor(pe, FFNS[f]["norm"])
            up_tensor(pe, f, "u", i0 + 1, 0, 0)

            def pair(n, between=lambda i: None):
                up_tensor(pe, f, "g", G, n, n + 1)
                between(0)
                up_tensor(pe, f, "u", U_, n, n + 1)
                between(1)
                down_tensor(pe, f, D_, n, n)
                between(2)

            pair(0)
            if f == 0:
                with pe.Fori(0, (PAIRS - 2) // 3) as r:
                    for c in range(3):
                        pair(3 * r + (c + 1), lambda i, c=c: mod_step(pe, r + 3, 3 * c + i))
            else:
                with pe.Fori(1, PAIRS - 1) as n:
                    pair(n)
            down_tensor(pe, f, i0 + 3 * PAIRS - 1, 0, PAIRS - 1, last=True)

        def u_bank(f, t):
            return psum[:, 2 + t, :] if FFNS[f]["wide"] else psum[:, 1, :]

        def ffn_act_hi(act, f, j):
            base = unit_base(f) + units(f) * j
            for t in range(units(f)):
                act.wait_ge(f_prod, base + t + 1)
                if not (isinstance(j, int) and j == 0):
                    act.wait_ge(f_d, down_base(f) + down_per(f) * j)
                nc.scalar.activation(a_hi[:, t, :], f_act[:, t, :], ACT.Copy).then_inc(f_ahi, 1)

        def conv_blocks(f, t, j):
            if FFNS[f]["wide"]:
                return [(bank2(t), f_act[:, t, :].rearrange("p (s t) -> p s t", s=2), 2 * j + t)]
            act2 = f_act[:, 0, :].rearrange("p (s t) -> p s t", s=2)
            return [(bank2(0)[:, q:q + 1, :], act2[:, q:q + 1, :], 2 * j + q) for q in range(2)]

        def ffn_mid_scalar(act, f, j):
            layer = FFNS[f]["layer"]
            base = unit_base(f) + units(f) * j
            for t in range(units(f)):
                act.wait_ge(f_g, base + t + 1)
                need(act, f_alo, unit_base(f) + units(f) * j)
                for src, dst, tile in conv_blocks(f, t, j):
                    made = nc.scalar.activation(dst, src, ACT.Identity,
                                                bias=par[:, 1 + layer, bass.ds(66 + tile, 1)],
                                                scale=par[:, 1 + layer, bass.ds(NFF + tile, 1)])
                made.then_inc(f_mid, 1)

        def ffn_silu_scalar(act, f, j):
            base = unit_base(f) + units(f) * j
            for t in range(units(f)):
                act.wait_ge(f_conv, base + t + 1)
                nc.scalar.activation(f_act[:, t, :], f_act[:, t, :], ACT.Silu).then_inc(f_silu, 1)

        def ffn_scalar(act, f):
            i0 = AT[f"ffn{f}"]
            G, U_, D_ = (ffn_stripe(f, w, False) for w in "gud")

            def gate(i, n, j):
                if FFNS[f]["layer"] is not None:
                    ffn_mid_scalar(act, f, j)
                ahead_hi(act, i, n)
                ffn_silu_scalar(act, f, j)

            ahead_hi(act, i0)
            gate(i0 + 1, 0, 0)

            def pair(n):
                ffn_act_hi(act, f, n)
                ahead_hi(act, G, n)
                gate(U_, n, n + 1)
                ahead_hi(act, D_, n)

            pair(0)
            if f == 2:
                tables_scalar(act)
            last = PAIRS - 2 if f == 3 else PAIRS - 1
            with act.Fori(1, last) as n:
                pair(n)
            for n in range(last, PAIRS - 1):
                pair(n)
            ffn_act_hi(act, f, PAIRS - 1)
            ahead_hi(act, i0 + 3 * PAIRS - 1)

        def ffn_act_lo(dve, f, j):
            base = unit_base(f) + units(f) * j
            for t in range(units(f)):
                dve.wait_ge(f_ahi, base + t + 1)
                nc.vector.tensor_tensor(a_lo[:, t, :], f_act[:, t, :], a_hi[:, t, :].bitcast(F32),
                                        ALU.subtract).then_inc(f_alo, 1)

        def ffn_conv_vector(dve, f, j):
            layer = FFNS[f]["layer"]
            base = unit_base(f) + units(f) * j
            for t in range(units(f)):
                dve.wait_ge(f_mid, base + t + 1)
                for tap, src_at, dst_at, done in ((0, 0, 1, f_left), (2, 1, 0, f_conv)):
                    for src, dst, tile in conv_blocks(f, t, j):
                        made = nc.vector.scalar_tensor_tensor(
                            out=dst[:, :, dst_at:dst_at + T - 1], in0=src[:, :, src_at:src_at + T - 1],
                            scalar=par[:, 1 + layer, bass.ds(NFF * tap + tile, 1)],
                            in1=dst[:, :, dst_at:dst_at + T - 1], op0=ALU.mult, op1=ALU.add)
                    made.then_inc(done, 1)
                    if tap == 0:
                        dve.wait_ge(f_left, base + t + 1)

        def ffn_scale_vector(dve, f, j):
            base = unit_base(f) + j
            dve.wait_ge(f_g, base + 1)
            need(dve, f_alo, base)
            nc.vector.tensor_tensor(f_act[:, 0, :].rearrange("p (s t) -> p s t", s=2), bank2(0), double(rinv[:, 0:T]),
                                    ALU.mult).then_inc(f_conv, 1)

        def ffn_prod_vector(dve, f, j):
            if FFNS[f]["layer"] is None:
                base = unit_base(f) + j
                dve.wait_ge(f_u, base + 1)
                nc.vector.tensor_tensor(f_act[:, 1, :].rearrange("p (s t) -> p s t", s=2), bank2(1),
                                        double(rinv[:, 0:T]), ALU.mult).then_inc(f_left, 1)
                dve.wait_ge(f_silu, base + 1)
                dve.wait_ge(f_left, base + 1)
                nc.vector.tensor_tensor(f_act[:, 0, :], f_act[:, 0, :], f_act[:, 1, :], ALU.mult).then_inc(f_prod, 1)
                return
            base = unit_base(f) + units(f) * j
            for t in range(units(f)):
                dve.wait_ge(f_u, base + t + 1)
                dve.wait_ge(f_silu, base + t + 1)
                nc.vector.tensor_tensor(f_act[:, t, :], f_act[:, t, :], u_bank(f, t), ALU.mult).then_inc(f_prod, 1)

        def ffn_down_vector(dve, f, j, tiles):
            for m in tiles:
                dve.wait_ge(f_d, down_base(f) + KD * j + m + 1)
                for s in range(2):
                    x = X[:, m, block_cols(s)]
                    made = nc.vector.scalar_tensor_tensor(out=x, in0=psum[:, 4 + m % 3, block_cols(s)],
                                                          scalar=mod[:, 0, 40 + m, s:s + 1], in1=x,
                                                          op0=ALU.mult, op1=ALU.add)
                made.then_inc(f_x, 1)

        def ffn_vector(dve, f):
            i0 = AT[f"ffn{f}"]
            wide = FFNS[f]["wide"]
            G, U_, D_ = (ffn_stripe(f, w, False) for w in "gud")

            def gate(i, n, j):
                if FFNS[f]["layer"] is not None:
                    ffn_conv_vector(dve, f, j)
                else:
                    ffn_scale_vector(dve, f, j)
                ahead_lo(dve, i, n)

            def store(i, n, j):
                if wide:
                    ffn_down_vector(dve, f, j, range(3))
                ahead_lo(dve, i, n)
                if wide:
                    ffn_down_vector(dve, f, j, range(3, KD))

            ahead_lo(dve, i0)
            gate(i0 + 1, 0, 0)
            ffn_prod_vector(dve, f, 0)

            def pair(n, batch=None):
                ffn_act_lo(dve, f, n)
                ahead_lo(dve, G, n)
                gate(U_, n, n + 1)
                ffn_prod_vector(dve, f, n + 1)
                if batch is not None:
                    mod_copy(dve, batch + 3)
                if wide:
                    dve.wait_ge(f_x, x_base(f) + KD * n) if not isinstance(n, int) else None
                store(D_, n, n)
                if batch is not None:
                    mod_store(dve, 1, batch + 3, batch)

            pair(0)
            if f == 2:
                tables_vector(dve)
            if f == 0:
                with dve.Fori(0, (PAIRS - 2) // 3) as r:
                    for c in range(3):
                        pair(3 * r + (c + 1), r if c == 2 else None)
            else:
                last = PAIRS - 2 if f == 3 else PAIRS - 1
                with dve.Fori(1, last) as n:
                    pair(n)
                for n in range(last, PAIRS - 1):
                    pair(n)
            ffn_act_lo(dve, f, PAIRS - 1)
            if wide:
                dve.wait_ge(f_x, x_base(f) + KD * (PAIRS - 1))
            store(i0 + 3 * PAIRS - 1, 0, PAIRS - 1)
            if f == 0:
                dve.wait_ge(mod_ready, 6)
                mod_plus_one(dve, 1, 0)
                mod_plus_one(dve, 1, 1)
                dve.wait_ge(mod1_ready, 4)
            if not wide:
                dve.wait_ge(f_d, down_base(f) + PAIRS)
                for b in range(4):
                    if FFNS[f]["layer"] is None:
                        nc.vector.tensor_copy(yb[:, 2 * b:2 * b + 2, :], bank2(4 + b)).then_inc(f_x, 1)
                        continue
                    for t in range(2):
                        m = 2 * b + t
                        x = X[:, m, T:TT]
                        nc.vector.scalar_tensor_tensor(out=x, in0=bank2(4 + b)[:, t, :],
                                                       scalar=mod[:, 1, 40 + m, 1:2], in1=x, op0=ALU.mult,
                                                       op1=ALU.add).then_inc(f_x, 1)

        GI = AT["gqa_in"]

        def gqa_in_tensor(pe):
            def turn(v):
                pe.wait_ge(gi_evac, v + 1)
                need(pe, gi_fix, 5 * (v - 1))
                nc.tensor.matmul(psum[:, 4 + v % 2, :], rot_gqa, g_tmp[:, v % 2, :], start=True,
                                 stop=True).then_inc(gi_rot, 1)
                nc.tensor.matmul(psum[:, 6 + v % 2, :], ones, scr[:, 3 + v % 3, :], start=True,
                                 stop=True).then_inc(gi_rot, 1)

            for s in range(6):
                begin_stripe(pe, GI + s)
                if s == 0:
                    two_products(pe, [psum[:, 0, block_cols(t)] for t in range(2)], GI, h_cols(T, TT), (gi_sums,),
                                 h_ready(pe, 2))
                    continue
                for t in range(2):
                    u = s if s < 4 else 2 * s - 4 + t
                    if s >= 4 or t == 0:
                        need(pe, gi_evac, u - 3)
                    if s < 4:
                        product(pe, psum[:, u, block_cols(t)], GI + s, t * P, h_cols(T, TT), t == 0,
                                gi_sums if t else None)
                    elif s == 4:
                        product(pe, psum[:, u % 4, :], GI + s, t * P, h_cols(0, TT), t == 0, gi_sums)
                    else:
                        for q in range(2):
                            c = (2 * t + q) * P
                            product_rows(pe, psum[:, u % 4, block_cols(q)], GI + s, h_cols(c, c + P),
                                         t == q == 0, True, gi_sums if q else None)
                    if (s < 4 and t == 0) or s == 5:
                        continue
                    if u >= 1:
                        turn(u - 1)
                if s == 4:
                    turn(5)

        def gqa_in_scalar(act):
            def deviation(v):
                act.wait_ge(gi_rot, 2 * v + 2)
                need(act, gi_fix, 5 * (v - 1) + 1)
                nc.scalar.activation(std[:, :], psum[:, 6 + v % 2, :], ACT.Sqrt, bias=eps,
                                     scale=1.0 / P).then_inc(gi_std, 1)

            act.wait_ge(n_rinv, 3)
            for s in range(6):
                ahead_hi(act, GI + s)
                if s == 5:
                    deviation(5)
                for u in ((s,) if s < 4 else (2 * s - 4, 2 * s - 3)):
                    act.wait_ge(gi_sums, u + 1)
                    if u < 6:
                        need(act, gi_rot, 2 * (u - 2))
                        nc.scalar.activation(scr[:, 3 + u % 3, :], psum[:, u % 4, :], ACT.Square)
                        need(act, gi_fix, 5 * (u - 1))
                        nc.scalar.activation(g_tmp[:, u % 2, :], psum[:, u % 4, :], ACT.Copy,
                                             scale=par[:, 1, 97:98] if u < 4 else par[:, 1, 98:99]).then_inc(gi_evac, 1)
                        if u >= 1:
                            deviation(u - 1)
                    else:
                        nc.scalar.activation(v_gqa[:, 2 * (u - 6):2 * (u - 6) + 2, :], bank2(u % 4),
                                             ACT.Copy).then_inc(gi_evac, 1)

        def gqa_in_vector(dve):
            def rope(v):
                f0 = 5 * v
                dve.wait_ge(gi_std, v + 1)
                need(dve, gi_fix, f0)
                nc.vector.reciprocal(rinv[:, :], std[:, :]).then_inc(gi_fix, 1)
                g = g_tmp[:, v % 2, :].rearrange("p (s t) -> p s t", s=2)
                r = bank2(4 + v % 2)
                tmp = scr[:, v % 2, :].rearrange("p (s t) -> p s t", s=2)
                if v < 4:
                    cos, sin = double(tab_gqa[:, 0, :]), double(tab_gqa[:, 1, :])
                    dst = q_gqa[:, 2 * v:2 * v + 2, :]
                    gr = g
                else:
                    cos, sin = tab_gqa[:, 0:1, :], tab_gqa[:, 1:2, :]
                    dst = k_gqa[:, v - 4, :].rearrange("p (s t) -> p s t", s=2)
                    gr, r, tmp = g[:, 1:2, :], r[:, 1:2, :], tmp[:, 1:2, :]
                nc.vector.tensor_tensor(tmp, r, sin, ALU.mult).then_inc(gi_fix, 1)
                nc.vector.tensor_tensor(gr, gr, cos, ALU.mult).then_inc(gi_fix, 1)
                dve.wait_ge(gi_fix, f0 + 3)
                nc.vector.tensor_tensor(gr, gr, tmp, ALU.add).then_inc(gi_fix, 1)
                dve.wait_ge(gi_fix, f0 + 4)
                nc.vector.tensor_tensor(dst, g, rinv[:, :].rearrange("p (s t) -> p s t", s=2),
                                        ALU.mult).then_inc(gi_fix, 1)

            dve.wait_ge(tab_in, 16)
            for s in range(6):
                ahead_lo(dve, GI + s)
                if 1 <= s < 5:
                    rope(s - 1)
            rope(4)
            rope(5)

        def gqa_tensor(pe):
            pe.wait_ge(gi_fix, 30)
            pe.wait_ge(gi_evac, 8)
            scores_tensor(pe, GQA, 0, gqa_scores)
            scores_tensor(pe, GQA, 1, gqa_scores)
            for h in range(8):
                turns_tensor(pe, GQA, h)
                if h + 2 < 8:
                    scores_tensor(pe, GQA, h + 2, gqa_scores)
                gqa_out_tensor(pe, h)

        def gqa_scalar(act):
            exp_scalar(act, GQA, 0)
            for h in range(8):
                if h + 1 < 8:
                    exp_scalar(act, GQA, h + 1)
                turned_scalar(act, GQA, h)
                out_hi_scalar(act, GQA, h)

        def gqa_vector(dve):
            max_vector(dve, GQA, 0)
            max_vector(dve, GQA, 1)
            norm_rows_vector(dve, GQA, 0)
            for h in range(8):
                if h + 1 < 8:
                    norm_rows_vector(dve, GQA, h + 1)
                if h + 2 < 8:
                    max_vector(dve, GQA, h + 2)
                out_lo_vector(dve, GQA, h)

        TWO_PI = 6.283185307179586
        PI_1, PI_2, PI_3 = 6.28125, 0.0019350051879882812, 3.0199159819e-07
        ROUND = 12582912.0
        PI_TOP = 3.1415925

        def tables_vector(dve):
            seq = 0

            def then(inst):
                nonlocal seq
                seq += 1
                inst.then_inc(tb_seq, 1)
                dve.wait_ge(tb_seq, seq)

            ang, turns, red = scr[:, 3, 0:T], scr[:, 3, T:TT], scr[:, 4, :]
            dve.wait_ge(b2_in, 80)
            then(nc.vector.tensor_copy(turns, pos_i.bitcast(I32)))
            then(nc.vector.tensor_scalar(ang, turns, inv_freq, None, ALU.mult))
            then(nc.vector.tensor_scalar(turns, ang, 1.0 / TWO_PI, ROUND, ALU.mult, ALU.add))
            then(nc.vector.tensor_scalar(turns, turns, ROUND, None, ALU.subtract))
            for part in (PI_1, PI_2, PI_3):
                then(nc.vector.scalar_tensor_tensor(out=ang, in0=turns, scalar=-part, in1=ang, op0=ALU.mult,
                                                    op1=ALU.add))
            then(nc.vector.tensor_scalar(red[:, 0:T], ang, TWO_PI / 4, None, ALU.add))
            then(nc.vector.tensor_scalar(turns, red[:, 0:T], TWO_PI / 2, -TWO_PI, ALU.is_gt, ALU.mult))
            then(nc.vector.tensor_tensor(red[:, 0:T], red[:, 0:T], turns, ALU.add))
            then(nc.vector.tensor_copy(red[:, T:TT], ang))
            then(nc.vector.tensor_scalar(red, red, PI_TOP, -PI_TOP, ALU.min, ALU.max))
            pairs = scr[:, 5, 0:P].rearrange("p (i n) -> p i n", i=2)
            then(nc.vector.tensor_tensor(pairs, lam_rows[:, 0:4:2, :], lam_rows[:, 1:4:2, :], ALU.mult))
            nc.vector.tensor_reduce(lam[:, 0:2], pairs, AX.X, ALU.add).then_inc(tb_ang, 1)
            dve.wait_ge(tb_sin, 2)
            then(nc.vector.tensor_tensor(lam[:, 4:5], lam[:, 2:3], lam[:, 3:4], ALU.subtract))
            then(nc.vector.tensor_scalar(lam[:, 5:6], lam[:, 4:5], LAMBDA_INIT, None, ALU.add))
            then(nc.vector.tensor_scalar(g_sub, par[:, 2, 88:89], 1.0 - LAMBDA_INIT, None, ALU.mult))

        def tables_scalar(act):
            act.wait_ge(tb_ang, 1)
            nc.scalar.activation(tab_b2, scr[:, 4, :].rearrange("p (s t) -> p s t", s=2),
                                 ACT.Sin).then_inc(tb_sin, 1)
            nc.scalar.activation(lam[:, 2:4], lam[:, 0:2], ACT.Exp).then_inc(tb_sin, 1)

        QK = AT["qkv"]
        N_ROT = 14

        def qkv_dst(u):
            if u < 4:
                return qa[:, 2 * u:2 * u + 2, :]
            if u < 8:
                return ka[:, 2 * (u - 4):2 * (u - 4) + 2, :]
            if u < 11:
                return qd[:, 2 * (u - 8):2 * (u - 8) + 2, :]
            if u < N_ROT:
                return kd[:, 2 * (u - 11):2 * (u - 11) + 2, :]
            if u < 18:
                return va[:, :, 256 * (u - 14):256 * (u - 13)]
            return vd[:, :, 256 * (u - 18):256 * (u - 17)]

        def qkv_tensor(pe):
            def turn(v):
                pe.wait_ge(r_evac, v + 1)
                need(pe, r_fix, 3 * (v - 1))
                nc.tensor.matmul(psum[:, 4 + v % 2, :], rot_b2, t_rope[:, v % 2, :], start=True,
                                 stop=True).then_inc(r_rot, 1)

            for u in range(21):
                begin_stripe(pe, QK + u)
                if u == 0:
                    two_products(pe, [psum[:, 0, block_cols(t)] for t in range(2)], QK, h_cols(T, TT), (r_sums,),
                                 h_ready(pe, 7))
                    continue
                need(pe, r_evac, u - 3)
                for t in range(2):
                    dst, done = psum[:, u % 4, block_cols(t)], r_sums if t else None
                    if u < N_ROT:
                        product(pe, dst, QK + u, t * P, h_cols(T, TT), t == 0, done)
                    else:
                        product_rows(pe, dst, QK + u, h_cols(T + t * P, T + (t + 1) * P), t == 0, True, done)
                if 1 <= u <= N_ROT:
                    turn(u - 1)

        def qkv_scalar(act):
            for u in range(21):
                ahead_hi(act, QK + u)
                act.wait_ge(r_sums, u + 1)
                if u < N_ROT:
                    need(act, r_fix, 3 * (u - 1))
                    nc.scalar.activation(t_rope[:, u % 2, :], psum[:, u % 4, :], ACT.Copy).then_inc(r_evac, 1)
                else:
                    nc.scalar.activation(qkv_dst(u), bank2(u % 4), ACT.Copy).then_inc(r_evac, 1)

        def qkv_vector(dve):
            for u in range(21):
                ahead_lo(dve, QK + u)
                if not 1 <= u <= N_ROT:
                    continue
                v = u - 1
                dve.wait_ge(r_rot, v + 1)
                need(dve, r_fix, 3 * v - 3)
                x = t_rope[:, v % 2, :].rearrange("p (s t) -> p s t", s=2)
                tmp = scr[:, v % 2, :].rearrange("p (s t) -> p s t", s=2)
                nc.vector.tensor_tensor(tmp, bank2(4 + v % 2), double(tab_b2[:, 1, :]), ALU.mult).then_inc(r_fix, 1)
                nc.vector.tensor_tensor(x, x, double(tab_b2[:, 0, :]), ALU.mult).then_inc(r_fix, 1)
                dve.wait_ge(r_fix, 3 * v + 2)
                nc.vector.tensor_tensor(qkv_dst(v), x, tmp, ALU.add).then_inc(r_fix, 1)

        B_S, B_MX, B_E, B_RS, B_PN, B_T, B_PT, B_O = 40, 56, 48, 16, 48, 40, 40, 16
        C_S, C_MX, C_E, C_RS, C_PN, C_T, C_PT, C_O = 56, 80, 80, 32, 80, 48, 48, 24

        DOWN, CLIP, OVERFLOW = 2.0 ** -20, 2.0 ** 78, 2.0 ** 88

        def diff_probs(h, c):
            return scr[:, 3 * (h % 2) + c, :].rearrange("p (q k) -> p q k", q=2)

        def diff_tensor(pe):
            pe.wait_ge(r_fix, 3 * N_ROT)
            pe.wait_ge(r_evac, 21)

            def turns(h):
                pe.wait_ge(at_pn, B_PN + 4 * (h + 1))
                need(pe, at_pt, B_PT + h)
                for q in range(2):
                    for k in range(2):
                        made = nc.tensor.transpose(psum[:, 4, k * T + q * P:k * T + (q + 1) * P],
                                                   diff_probs(h, 0)[:, q, k * P:(k + 1) * P], ident)
                made.then_inc(at_t, 1)

            def outputs(h):
                pe.wait_ge(at_pt, B_PT + h + 1)
                need(pe, d_copied, h - 1)
                for k in range(2):
                    made = nc.tensor.matmul(psum[:, 5 + h % 2, 0:T], va[:, k, h * P:(h + 1) * P],
                                            pt_b2[:, k * T:(k + 1) * T], start=k == 0, stop=k == 1)
                made.then_inc(at_o, 1)

            def scores(h):
                need(pe, at_e, B_E + 4 * (h - 1))
                for q in range(2):
                    for c in range(2):
                        r = slice(64 * c, 64 * (c + 1))
                        made = nc.tensor.matmul(psum[:, 2 * (h % 2) + c, block_cols(q)],
                                                qa[r, h, q * P:(q + 1) * P], ka[r, h, :], start=True, stop=True)
                        if q:
                            made.then_inc(at_s, 1)

            scores(0)
            scores(1)
            for h in range(8):
                turns(h)
                if h + 2 < 8:
                    scores(h + 2)
                gate_a_tensor(pe, h)
                outputs(h)
            dil_scores(pe, 0)
            for p in range(4):
                pe.wait_ge(d_sq, p + 1)
                nc.tensor.matmul(psum[32 * p:32 * p + 32, 4, :], ones[:, 0:32], scr[:, 3 + p % 3, :], start=True,
                                 stop=True).then_inc(d_ss, 1)
            gate_tensor(pe, GB01, 3, gb_sums)
            pe.wait_ge(d_rinv, 3)
            pe.wait_ge(ga_kept, 4)
            for p in range(4):
                nc.tensor.matmul(psum[:, 4 + p, :], ones[32 * p:32 * p + 1, :], rinv[32 * p:32 * p + 1, :], start=True,
                                 stop=True).then_inc(d_wide, 1)
            pe.wait_ge(d_t, 1)
            gate_tensor(pe, GB01 + 1, 4, gb_sums)

        GA, GB01, PA, GB2, PB, GB3 = (AT[n] for n in ("gate_a", "gate_b01", "proj_a", "gate_b2", "proj_b", "gate_b3"))

        def gate_tensor(pe, i, bank, done, acts=(T, TT)):
            begin_stripe(pe, i)
            for t in range(2):
                product(pe, psum[:, bank, block_cols(t)], i, t * P, h_cols(*acts), t == 0, done if t else None)

        def gate_a_tensor(pe, h):
            s, t = divmod(h, 2)
            if t == 0:
                begin_stripe(pe, GA + s)
                need(pe, ga_kept, s)
            product(pe, psum[:, 7, block_cols(t)], GA + s, t * P, h_cols(T, TT), t == 0, ga_sums if t else None)

        def diff_scalar(act):
            def finish(h):
                act.wait_ge(at_t, B_T + h + 1)
                act.wait_ge(at_o, B_O + h)
                nc.scalar.activation(pt_b2[:, 0:TT], psum[:, 4, :], ACT.Copy).then_inc(at_pt, 1)
                if h % 2 == 0:
                    ahead_hi(act, GA + h // 2)
                act.wait_ge(at_o, B_O + h + 1)
                nc.scalar.activation(qa[:, h, :], psum[:, 5 + h % 2, 0:T], ACT.Copy).then_inc(d_copied, 1)

            def exponentials(h):
                act.wait_ge(at_mx, B_MX + 3 * (h + 1))
                need(act, at_t, B_T + h - 1)
                for c in range(2):
                    for q in range(2):
                        nc.scalar.activation(diff_probs(h, c)[:, q, :], psum[:, 2 * (h % 2) + c, block_cols(q)],
                                             ACT.Exp, bias=row_neg[:, h % 2, 2 * c + q:2 * c + q + 1], scale=B2_SCALE,
                                             accum_out=row_sum[:, h % 2, 2 * c + q:2 * c + q + 1]).then_inc(at_e, 1)

            exponentials(0)
            for h in range(8):
                if h + 1 < 8:
                    exponentials(h + 1)
                finish(h)
                if h % 2:
                    s = h // 2
                    act.wait_ge(ga_sums, s + 1)
                    nc.scalar.activation(gate_a[s], psum[:, 7, :], ACT.Copy).then_inc(ga_kept, 1)
            for p in range(4):
                act.wait_ge(d_clip, p + 1)
                nc.scalar.activation(scr[:, 3 + p % 3, :], scr[:, 3 + p % 3, :], ACT.Square,
                                     scale=DOWN).then_inc(d_sq, 1)
            act.wait_ge(d_ss, 4)
            nc.scalar.activation(std[:, :], psum[:, 4, :], ACT.Sqrt, bias=eps_down, scale=1.0 / P).then_inc(d_std, 1)
            ahead_hi(act, GB01)
            for p in range(4):
                diff_hi(act, p)
            act.wait_ge(ga_kept, 4)
            for s in range(4):
                nc.scalar.activation(gate_a[s], gate_a[s], ACT.Sigmoid).then_inc(ga_sig, 1)
            for s in range(2):
                act.wait_ge(gb_sums, s + 1)
                nc.scalar.activation(gate_b[:, s, :], psum[:, 3 + s, :], ACT.Sigmoid).then_inc(gb_sig, 1)
            ahead_hi(act, GB01 + 1)

        def diff_hi(act, p):
            act.wait_ge(d_t, p + 1)
            nc.scalar.activation(h_hi[:, 2 * p:2 * p + 2, 0:T], scr[:, p % 3, :].rearrange("p (s t) -> p s t", s=2),
                                 ACT.Copy).then_inc(d_hi, 1)

        def diff_lo(dve, p):
            dve.wait_ge(d_hi, p + 1)
            nc.vector.tensor_tensor(h_lo[:, 2 * p:2 * p + 2, 0:T],
                                    scr[:, p % 3, :].rearrange("p (s t) -> p s t", s=2),
                                    h_hi[:, 2 * p:2 * p + 2, 0:T].bitcast(F32), ALU.subtract).then_inc(d_lo, 1)

        def diff_vector(dve):
            def maxima(h):
                par_ = h % 2
                for c in range(2):
                    dve.wait_ge(at_s, B_S + 2 * h + c + 1)
                    nc.vector.tensor_reduce(row_max[:, par_, 2 * c:2 * c + 2], bank2(2 * par_ + c), AX.X,
                                            ALU.max).then_inc(at_mx, 1)
                dve.wait_ge(at_mx, B_MX + 3 * h + 2)
                nc.vector.tensor_scalar(row_neg[:, par_, :], row_max[:, par_, :], -B2_SCALE, None,
                                        ALU.mult).then_inc(at_mx, 1)

            maxima(0)
            for h in range(8):
                par_ = h % 2
                if h + 1 < 8:
                    maxima(h + 1)
                dve.wait_ge(at_e, B_E + 4 * (h + 1))
                nc.vector.reciprocal(row_inv[:, par_, :], row_sum[:, par_, :]).then_inc(at_rs, 1)
                dve.wait_ge(at_rs, B_RS + 2 * h + 1)
                nc.vector.tensor_scalar(row_inv[:, par_, 2:4], row_inv[:, par_, 2:4], lam[:, 5:6], None,
                                        ALU.mult).then_inc(at_rs, 1)
                dve.wait_ge(at_rs, B_RS + 2 * h + 2)
                p0, p1 = diff_probs(h, 0), diff_probs(h, 1)
                for q in range(2):
                    nc.vector.tensor_scalar(p1[:, q, :], p1[:, q, :], row_inv[:, par_, 2 + q:3 + q], None,
                                            ALU.mult).then_inc(at_pn, 1)
                for q in range(2):
                    dve.wait_ge(at_pn, B_PN + 4 * h + q + 1)
                    nc.vector.scalar_tensor_tensor(out=p0[:, q, :], in0=p0[:, q, :], scalar=row_inv[:, par_, q:q + 1],
                                                   in1=p1[:, q, :], op0=ALU.mult, op1=ALU.subtract).then_inc(at_pn, 1)
                if h % 2:
                    ahead_lo(dve, GA + h // 2)
            for p in range(4):
                dve.wait_ge(d_copied, 8)
                need(dve, d_ss, p - 2)
                nc.vector.tensor_scalar(scr[:, 3 + p % 3, :].rearrange("p (s t) -> p s t", s=2),
                                        qa[:, 2 * p:2 * p + 2, :], CLIP, -CLIP, ALU.min,
                                        ALU.max).then_inc(d_clip, 1)
            dve.wait_ge(d_std, 1)
            nc.vector.reciprocal(rinv[:, :], std[:, :]).then_inc(d_rinv, 1)
            nc.vector.tensor_scalar(scr[:, 0, :], psum[:, 4, :], OVERFLOW, DOWN, ALU.is_lt, ALU.mult).then_inc(d_rinv, 1)
            dve.wait_ge(d_rinv, 2)
            nc.vector.tensor_tensor(rinv[:, :], rinv[:, :], scr[:, 0, :], ALU.mult).then_inc(d_rinv, 1)
            for p in range(4):
                dve.wait_ge(d_wide, p + 1)
                if p == 0:
                    dve.wait_ge(d_rinv, 3)
                if p >= 3:
                    dve.wait_ge(d_lo, p - 2)
                nc.vector.scalar_tensor_tensor(out=scr[:, p % 3, :], in0=qa[:, 2 * p:2 * p + 2, :].rearrange("p s t -> p (s t)"),
                                               scalar=g_sub, in1=psum[:, 4 + p, :], op0=ALU.mult,
                                               op1=ALU.mult).then_inc(d_t, 1)
                if p:
                    diff_lo(dve, p - 1)
            diff_lo(dve, 3)
            ahead_lo(dve, GB01)

        def dil_scores(pe, j):
            need(pe, at_mx, C_MX + 5 * (j - 1) + 3) if j else None
            for g in range(3):
                hd = 4 * g + j
                r = slice(64 * (hd % 2), 64 * (hd % 2) + 64)
                for q in range(2):
                    made = nc.tensor.matmul(psum[:, g, block_cols(q)], qd[r, hd // 2, q * P:(q + 1) * P],
                                            kd[r, hd // 2, :], start=True, stop=True)
                made.then_inc(at_s, 1)

        def dil_tensor(pe):
            def turns(j):
                pe.wait_ge(at_pn, C_PN + 2 * (j + 1))
                need(pe, at_pt, C_PT + 3 * j)
                for g in range(3):
                    for q in range(2):
                        for k in range(2):
                            made = nc.tensor.transpose(psum[:, 3 + g, k * T + q * P:k * T + (q + 1) * P],
                                                       scr[:, 3 * (j % 2) + g, q * T + k * P:q * T + (k + 1) * P], ident)
                    made.then_inc(at_t, 1)

            def outputs(j):
                pe.wait_ge(at_pt, C_PT + 3 * (j + 1))
                r = slice(64 * (j % 2), 64 * (j % 2) + 64)
                for g in range(3):
                    for k in range(2):
                        c = 64 * (4 * g + j)
                        made = nc.tensor.matmul(psum[r, 6, block_cols(j // 2)], vd[:, k, c:c + 64],
                                                pt_b2[:, g * TT + k * T:g * TT + (k + 1) * T],
                                                start=g == k == 0, stop=g == 2 and k == 1)
                made.then_inc(at_o, 1)

            for j in range(DIL_OUT):
                if j == 0:
                    pe.wait_ge(d_lo, 4)
                need(pe, p_m, j)
                gate_tensor(pe, PA + j, 7, pa_sums, (0, T))
                if j == 0:
                    pe.wait_ge(gb_sig, 2)
                else:
                    outputs(j - 1)
                if j + 1 < DIL_OUT:
                    dil_scores(pe, j + 1)
                turns(j)
            outputs(DIL_OUT - 1)

        def dil_scalar(act):
            def finish(j):
                need(act, at_o, C_O + j)
                for g in range(3):
                    act.wait_ge(at_t, C_T + 3 * j + g + 1)
                    nc.scalar.activation(pt_b2[:, g * TT:(g + 1) * TT], psum[:, 3 + g, :], ACT.Copy).then_inc(at_pt, 1)
                if j == DIL_OUT - 1:
                    act.wait_ge(at_o, C_O + DIL_OUT)
                    nc.scalar.activation(a_hi[:, 0, :], psum[:, 6, :], ACT.Copy).then_inc(d_hi, 1)

            def exponentials(j):
                act.wait_ge(at_mx, C_MX + 5 * (j + 1))
                for q in range(2):
                    rows = scr[:, 3 * (j % 2):3 * (j % 2) + 3, block_cols(q)]
                    nc.scalar.activation(rows, rows, ACT.Exp, bias=row_neg[:, j % 2, q:q + 1], scale=B2_SCALE,
                                         accum_out=row_sum[:, j % 2, q:q + 1]).then_inc(at_e, 1)

            exponentials(0)
            for j in range(DIL_OUT):
                if j + 1 < DIL_OUT:
                    exponentials(j + 1)
                ahead_hi(act, PA + j)
                finish(j)

        def dil_vector(dve):
            dve.wait_ge(tab_in, 32)
            masks = (dil_mask[:, 0:2, :], double(dil_mask[:, 2, :]), double(dil_mask[:, 3, :]))
            def maxima(j):
                par_ = j % 2
                if j == 0:
                    dve.wait_ge(d_lo, 4)
                if j == 1:
                    dve.wait_ge(d_ss, 4)
                need(dve, at_t, C_T + 3 * (j - 1))
                for g in range(3):
                    dve.wait_ge(at_s, C_S + 3 * j + g + 1)
                    nc.vector.tensor_tensor(scr[:, 3 * par_ + g, :].rearrange("p (q k) -> p q k", q=2), bank2(g),
                                            masks[g], ALU.add).then_inc(at_mx, 1)
                dve.wait_ge(at_mx, C_MX + 5 * j + 3)
                for q in range(2):
                    made = nc.vector.tensor_reduce(row_max[:, par_, q:q + 1],
                                                   scr[:, 3 * par_:3 * par_ + 3, block_cols(q)], AX.XY, ALU.max)
                made.then_inc(at_mx, 1)
                dve.wait_ge(at_mx, C_MX + 5 * j + 4)
                nc.vector.tensor_scalar(row_neg[:, par_, 0:2], row_max[:, par_, 0:2], -B2_SCALE, None,
                                        ALU.mult).then_inc(at_mx, 1)

            maxima(0)
            ahead_lo(dve, GB01 + 1)
            for j in range(DIL_OUT):
                par_ = j % 2
                dve.wait_ge(at_e, C_E + 2 * (j + 1))
                nc.vector.reciprocal(row_inv[:, par_, 0:2], row_sum[:, par_, 0:2]).then_inc(at_rs, 1)
                dve.wait_ge(at_rs, C_RS + j + 1)
                for q in range(2):
                    rows = scr[:, 3 * par_:3 * par_ + 3, block_cols(q)]
                    nc.vector.tensor_scalar(rows, rows, row_inv[:, par_, q:q + 1], None, ALU.mult).then_inc(at_pn, 1)
                dve.wait_ge(ga_sig, j + 1)
                dve.wait_ge(pa_sums, j + 1)
                nc.vector.tensor_tensor(yb[:, 2 * j:2 * j + 2, :], gate_a[j].rearrange("p (s t) -> p s t", s=2),
                                        bank2(7), ALU.mult).then_inc(p_m, 1)
                if j + 1 < DIL_OUT:
                    maxima(j + 1)
                ahead_lo(dve, PA + j)
            dve.wait_ge(d_hi, 5)
            nc.vector.tensor_tensor(a_lo[:, 0, :], psum[:, 6, :], a_hi[:, 0, :].bitcast(F32),
                                    ALU.subtract).then_inc(d_lo, 1)

        def proj_tensor(pe):
            pe.wait_ge(at_mx, C_MX + 5 * DIL_OUT)
            gate_tensor(pe, GB2, 0, gb_sums)
            begin_stripe(pe, PB)
            pe.wait_ge(d_lo, 5)
            for m in range(KD):
                product(pe, psum[:, 2 + m // 2, block_cols(m % 2)], PB, m * P,
                        lambda k: (a_hi[:, 0, block_cols(k)], a_lo[:, 0, block_cols(k)]), m == 0,
                        pb_sums if m == KD - 1 else None, tiles=2, pitch=D)
            gate_tensor(pe, GB3, 1, gb_sums)

        def proj_scalar(act):
            for s, i in ((2, GB2), (3, GB3)):
                ahead_hi(act, i)
                if s == 2:
                    ahead_hi(act, PB)
                act.wait_ge(gb_sums, s + 1)
                nc.scalar.activation(gate_b[:, s, :], psum[:, s - 2, :], ACT.Sigmoid).then_inc(gb_sig, 1)
                if s == 2:
                    for m in range(3):
                        merged_hi(act, m)
            merged_hi(act, 3)

        def merged_hi(act, s):
            act.wait_ge(p_m, 4 + 2 * (s + 1))
            nc.scalar.activation(h_hi[:, 2 * s:2 * s + 2, 0:T], yb[:, 2 * s:2 * s + 2, :], ACT.Copy).then_inc(p_hi, 1)

        def merged_lo(dve, s):
            dve.wait_ge(p_hi, s + 1)
            nc.vector.tensor_tensor(h_lo[:, 2 * s:2 * s + 2, 0:T], yb[:, 2 * s:2 * s + 2, :],
                                    h_hi[:, 2 * s:2 * s + 2, 0:T].bitcast(F32), ALU.subtract).then_inc(p_lo, 1)

        def proj_vector(dve):
            ahead_lo(dve, GB2)
            ahead_lo(dve, PB)
            dve.wait_ge(pb_sums, 1)
            for s in range(4):
                if s == 3:
                    ahead_lo(dve, GB3)
                dve.wait_ge(gb_sig, s + 1)
                g = gate_b[:, s, :].rearrange("p (s t) -> p s t", s=2)
                y = yb[:, 2 * s:2 * s + 2, :]
                nc.vector.tensor_tensor(g, g, bank2(2 + s), ALU.mult).then_inc(p_m, 1)
                dve.wait_ge(p_m, 4 + 2 * s + 1)
                nc.vector.tensor_tensor(y, y, g, ALU.add).then_inc(p_m, 1)
                if s:
                    merged_lo(dve, s - 1)
            merged_lo(dve, 3)

        PAR_ROWS = (112, 99, 89, 56)

        block = ctx.enter_context(nc.Block())

        @block.sync
        def _(sp):
            sp.dma_start(const[:, 0:5 * P + 1], a["const_base"]).then_inc(base_in, 16)
            rows = par_rows
            packs = [
                (0, [(a["c"], 8), (a["c_ctx"].unsqueeze(0), 8), (a["b_mod"], 96)]),
                (1, [(a["ffn_conv_w"][0], 66), (a["ffn_conv_b"][0:1], 22), (a["mla_g_q"], 3), (a["mla_g_kv"], 2),
                     (a["pool_scale"], 4), (a["gqa_g_q"], 1), (a["gqa_g_k"], 1)]),
                (2, [(a["ffn_conv_w"][1], 66), (a["ffn_conv_b"][1:2], 22), (a["g_subln_2"], 1)]),
                (3, [(a["g_final"].unsqueeze(0), 8)] + [(a[n], 8) for n in (
                    "g_pre_ffn1_2", "g_post_ffn1_2", "g_pre_mix_2", "g_post_mix_2", "g_pre_ffn2_2", "g_post_ffn2_2")]),
            ]
            count = 0
            for p, parts in packs:
                at = 0
                for src, n in parts:
                    sp.dma_start(rows[at:at + n, p, :], src.rearrange("l (t q) -> (l t) q", q=P)).then_inc(par_in, 16)
                    at += n
                    count += 1
                assert at == PAR_ROWS[p]
            assert count == 20
            sp.dma_start(ctx_rows, a["ctx"][0].rearrange("(t p) n -> p t n", p=P)).then_inc(rows_in, 16)
            sp.dma_start(lat_rows, a["x"][0].rearrange("(t p) n -> p t n", p=P)).then_inc(rows_in, 16)
            sp.wait_ge(mod_early[3], 16)
            for i in range(3):
                load(sp, i, stripe_source(i))
            for dst, src in ((w_uq, a["mla_w_uq"]), (w_uk, a["mla_w_uk"]), (w_uv, a["mla_w_uv"])):
                sp.dma_start(dst, src[0].rearrange("(k p) n -> p k n", p=P)).then_inc(small_in, 16)
            sp.dma_start(w_pool, a["pool_w"][0].rearrange("g p n -> p g n")).then_inc(small_in, 16)
            sp.dma_start(tab_mla, a["rope_mla"].rearrange("p (s t) -> p s t", s=2)).then_inc(small_in, 16)
            for i in range(3, AT["ffn0"]):
                load(sp, i, stripe_source(i))

            def ffn_loads(f):
                i0 = AT[f"ffn{f}"]
                up_name, layer, _, _ = STRIPES[i0]
                down_name = STRIPES[i0 + 4][0]
                up = a[up_name][layer].rearrange("(k p) n -> p k n", p=P)
                down = a[down_name][layer].rearrange("(k p) n -> p k n", p=P)
                load(sp, i0, stripe_source(i0))
                load(sp, i0 + 1, stripe_source(i0 + 1))
                if f == 0:
                    sp.wait_ge(pool_sums, 4)
                    sp.wait_ge(at_o, 8)
                    sp.dma_start(tab_gqa, a["rope_gqa"].rearrange("p (s t) -> p s t", s=2)).then_inc(tab_in, 16)
                if f == 2:
                    sp.dma_start(dil_mask, a["dil_mask"].rearrange("p (g t) -> p g t", g=4)).then_inc(tab_in, 16)
                with sp.Fori(0, PAIRS - 1) as n:
                    load(sp, i0 + 2, up[:, :, bass.ds(256 * n + 256, 256)], n)
                    load(sp, i0 + 3, up[:, :, bass.ds(256 * n + FF + 256, 256)], n)
                    load(sp, i0 + 4, down[:, bass.ds(2 * n, 2), :], n)
                load(sp, i0 + 3 * PAIRS - 1, stripe_source(i0 + 3 * PAIRS - 1))

            ffn_loads(0)
            for i in range(AT["gqa_in"], AT["ffn1"]):
                load(sp, i, stripe_source(i))
            ffn_loads(1)
            ffn_loads(2)
            for i in range(AT["qkv"], AT["ffn3"]):
                load(sp, i, stripe_source(i))
            ffn_loads(3)
            for t in range(2):
                sp.wait_ge(y_rows, 2 * t + 2)
                sp.dma_start(out[0, t * P:(t + 1) * P, :], out_rows[:, t, :]).then_inc(stored, 16)
            sp.wait_ge(stored, 32)

        @block.gpsimd
        def _(pool):
            nc.gpsimd.memset(small_w[:, 0:1], EPS)
            nc.gpsimd.memset(silu_all[:, 2 * KD:], 0.0)
            nc.gpsimd.memset(small_w[:, 1:2], EPS * 2.0 ** -40).then_inc(fill, 1)
            def mod_load(batch, k, layer, at):
                src = a["w_mod"][layer][k * P:(k + 1) * P, bass.ds(STRIPE * at, STRIPE)]
                slot = k % 2
                if isinstance(batch, int) and batch == 0:
                    if 2 <= k < 6:
                        pool.dma_start(mod_early_ring[:, k - 2, :], src).then_inc(mod_early[k - 2], 16)
                        return
                    if k >= 6:
                        pool.wait_ge(mod_stripes, k - 5)
                else:
                    pool.wait_ge(mod_stripes, 8 * batch + k - 1)
                pool.dma_start(mod_ring[:, slot, :], src).then_inc(mod_in[slot], 16)

            pool.wait_ge(par_in, 320)
            for k in range(KD):
                mod_load(0, k, 0, 0)
            pool.wait_ge(x_turned, KD)
            pool.dma_start(pool_inv, a["pool_inv"].rearrange("p (g t) -> p g t", g=4)).then_inc(inv_in, 16)
            for g in range(4):
                for s in range(2):
                    for c in (0, PAD + T):
                        made = nc.gpsimd.memset(pool_p[:, g, s, c:c + PAD], 0.0)
            made.then_inc(pool_pads, 1)
            with pool.Fori(1, 3) as batch:
                for k in range(KD):
                    mod_load(batch, k, 0, batch)
            pool.wait_ge(pool_pads, 1)
            pool_gpsimd(pool)
            pool.wait_ge(o_sums, 1)
            with pool.Fori(3, 6) as batch:
                for k in range(KD):
                    mod_load(batch, k, 1, batch - 3)
            pool.wait_ge(f_x, x_base(2))
            pool.dma_start(pos_i.bitcast(I32), a["positions_2"].broadcast_to([P, T])).then_inc(b2_in, 16)
            for i, name in enumerate(("lambda_q1_2", "lambda_k1_2", "lambda_q2_2", "lambda_k2_2")):
                pool.dma_start(lam_rows[:, i, :], a[name].broadcast_to([P, 64])).then_inc(b2_in, 16)

        @block.tensor
        def _(pe):
            pe.wait_ge(base_in, 16)
            pe.wait_ge(par_in, 320)
            for p, n in enumerate(PAR_ROWS):
                nc.tensor.transpose(psum[:, 4 + p, 0:n], par_rows[0:n, p, :], ident[0:n, 0:n]).then_inc(par_turned, 1)
            pe.wait_ge(rows_in, 32)
            for m in range(KD):
                need(pe, x_in, m - 3)
                for t in range(4):
                    src = (ctx_rows if t < 2 else lat_rows)[:, t % 2, m * P:(m + 1) * P]
                    made = nc.tensor.transpose(psum[:, m % 4, t * P:(t + 1) * P], src, ident)
                made.then_inc(x_turned, 1)
            norm_tensor(pe, 0)
            pe.wait_ge(c_ready, 1)
            pe.wait_ge(fill, 1)
            pe.wait_ge(par_ready, 4)
            for i in range(KD + 1):
                mod_step(pe, 0, i)
            pe.wait_ge(x_in, KD)
            mix_in_tensor(pe)
            values_tensor(pe)
            mod_turn(pe, 2)
            mla_tensor(pe)
            pool_tensor(pe)
            mix_out_tensor(pe)
            norm_tensor(pe, 1)
            ffn_tensor(pe, 0)
            norm_tensor(pe, 2)
            gqa_in_tensor(pe)
            gqa_tensor(pe)
            out_tensor(pe, GO, lambda k: pe.wait_ge(at_lo, 8 + k + 1))
            norm_tensor(pe, 3)
            ffn_tensor(pe, 1)
            norm_tensor(pe, 4)
            ffn_tensor(pe, 2)
            norm_tensor(pe, 6)
            norm_tensor(pe, 7)
            qkv_tensor(pe)
            diff_tensor(pe)
            dil_tensor(pe)
            proj_tensor(pe)
            out_tensor(pe, WO, lambda k: pe.wait_ge(p_lo, k // 2 + 1))
            norm_tensor(pe, 8)
            ffn_tensor(pe, 3)
            norm_tensor(pe, 10)
            for t in range(2):
                for m in range(KD):
                    pe.wait_ge(n_x, 8 + m // 2 + 1)
                    made = nc.tensor.transpose(psum[:, 2 * t + m // 4, (m % 4) * P:(m % 4 + 1) * P],
                                               X[:, m, T + t * P:T + (t + 1) * P], ident)
                    if m % 4 == 3:
                        made.then_inc(y_turned, 1)

        @block.scalar
        def _(act):
            act.wait_ge(par_ready, 1)
            nc.scalar.activation(silu_c[:, :, 1], par[:, 0, 0:8], ACT.Silu)
            nc.scalar.activation(silu_c[:, :, 0], par[:, 0, 8:16], ACT.Silu).then_inc(c_ready, 1)
            act.wait_ge(fill, 1)
            act.wait_ge(par_ready, 4)
            norm_scalar(act, 0, x_chunk(0), lambda c: (x_in, c + 1), lambda: split_hi(act, 0))
            split_hi(act, 1)
            mix_in_scalar(act)
            mla_scalar(act)
            pool_scalar(act)
            ahead_scalar(act, MO, 4)
            norm_scalar(act, 1, x_chunk(1), lambda c: (o_evac, c + 1))
            ffn_scalar(act, 0)
            norm_scalar(act, 2, x_chunk(2), lambda c: (f_x, x_base(1) - 7 + c))
            gqa_in_scalar(act)
            gqa_scalar(act)
            ahead_scalar(act, GO, 4)
            norm_scalar(act, 3, x_chunk(3), lambda c: (o_evac, 8 + c + 1))
            ffn_scalar(act, 1)
            norm_scalar(act, 4, x_chunk(4), lambda c: (f_x, x_base(1) + 2 * c + 2))
            norm_scalar(act, 5, x_chunk(5), lambda c: (n_t, chunks_before(4) + c + 1))
            ffn_scalar(act, 2)
            norm_scalar(act, 6, y_chunk, lambda c: (f_x, x_base(2) + c + 1))
            norm_scalar(act, 7, x_chunk(7), lambda c: (n_x, c + 1))
            qkv_scalar(act)
            diff_scalar(act)
            dil_scalar(act)
            proj_scalar(act)
            ahead_scalar(act, WO, 4)
            norm_scalar(act, 8, y_chunk, lambda c: (o_evac, 12 + c + 1))
            norm_scalar(act, 9, x_chunk(9), lambda c: (n_x, 4 + c + 1))
            ffn_scalar(act, 3)
            norm_scalar(act, 10, y_chunk, lambda c: (f_x, x_base(3) + c + 1))

        @block.vector
        def _(dve):
            for p, n in enumerate(PAR_ROWS):
                dve.wait_ge(par_turned, p + 1)
                nc.vector.tensor_copy(par[:, p, 0:n], psum[:, 4 + p, 0:n]).then_inc(par_ready, 1)
            for m in range(KD):
                dve.wait_ge(x_turned, m + 1)
                nc.vector.tensor_copy(X[:, m, :], psum[:, m % 4, :]).then_inc(x_in, 1)
            dve.wait_ge(par_ready, 4)

            def first_modulation():
                mod_copy(dve, 0)
                mod_store(dve, 0, 0, 0)
                dve.wait_ge(mod_ready, 1)
                mod_plus_one(dve, 0, 0)
                dve.wait_ge(mod1_ready, 1)
                split_lo(dve, 0)

            norm_vector(dve, 0, x_chunk(0), between=first_modulation)
            split_lo(dve, 1)
            mix_in_vector(dve)
            mla_vector(dve)
            pool_vector(dve)
            mix_out_vector(dve)
            norm_vector(dve, 1, x_chunk(1))
            ffn_vector(dve, 0)
            norm_vector(dve, 2, x_chunk(2))
            gqa_in_vector(dve)
            gqa_vector(dve)
            gqa_out_vector(dve)
            norm_vector(dve, 3, x_chunk(3))
            ffn_vector(dve, 1)
            norm_vector(dve, 4, x_chunk(4))
            norm_vector(dve, 5, x_chunk(5))
            ffn_vector(dve, 2)
            norm_vector(dve, 6, y_chunk, 0.5)
            norm_vector(dve, 7, x_chunk(7))
            qkv_vector(dve)
            diff_vector(dve)
            dil_vector(dve)
            proj_vector(dve)
            w_out_vector(dve)
            norm_vector(dve, 8, y_chunk, 1.0)
            norm_vector(dve, 9, x_chunk(9))
            ffn_vector(dve, 3)
            norm_vector(dve, 10, y_chunk, 0.5)
            for b in range(4):
                dve.wait_ge(y_turned, b + 1)
                nc.vector.tensor_copy(out_rows[:, b // 2, (b % 2) * TT:(b % 2 + 1) * TT], psum[:, b, :]).then_inc(y_rows, 1)


def shape_constants():
    f = np.float32
    base = np.zeros((P, 5 * P + 1), f)
    base[:, 0:P] = np.eye(P)
    base[:, P:2 * P] = 1
    rot = np.zeros((3, P, P), f)
    for which, rows in ((0, range(NOPE, MLA_QK, 2)), (1, range(0, P, 2))):
        for r in rows:
            rot[which, r + 1, r], rot[which, r, r + 1] = -1, 1
    for r in range(P):
        if r % 64 < 8:
            rot[2, r + 8, r], rot[2, r, r + 8] = -1, 1
    base[:, 2 * P:5 * P] = rot.transpose(1, 0, 2).reshape(P, 3 * P)
    inv = f(500000.0) ** (-(np.arange(0, 16, 2, dtype=f) / f(16)))
    for r in range(P):
        if r % 64 < 16:
            base[r, 5 * P] = inv[r % 8]

    def tables(dim, first, rows):
        n = dim // 4
        freq = f(10000.0) ** (-np.arange(n, dtype=f) / f(n))
        row = np.repeat(np.arange(T // 64, dtype=f), 64)
        col = np.tile(np.arange(64, dtype=f), T // 64)
        ang = np.concatenate([row[:, None] * freq, col[:, None] * freq], -1)
        out = np.zeros((P, 2, T), f)
        out[:, 0] = 1
        for r in range(first, rows):
            out[r, 0], out[r, 1] = np.cos(ang[:, (r - first) // 2]), np.sin(ang[:, (r - first) // 2])
        return out.reshape(P, 2 * T)

    t = np.arange(T)
    inverse = np.stack([1 / (np.minimum(t - w // 2 + w, T) - np.maximum(t - w // 2, 0)).astype(f) for w in WINDOWS])
    i, j = np.arange(T)[:, None], np.arange(T)[None, :]
    near = np.where(abs(i - j) <= 64, 0, NEG).reshape(2, P, T).transpose(1, 0, 2)
    apart = [np.where((i[:P] - j) % d == 0, 0, NEG)[:, None] for d in (4, 16)]
    return {
        "const_base": base,
        "rope_mla": tables(ROPE, NOPE, MLA_QK),
        "rope_gqa": tables(P, 0, P),
        "pool_inv": np.broadcast_to(inverse.astype(f).reshape(1, -1), (P, 4 * T)).copy(),
        "dil_mask": np.concatenate([near, *apart], 1).astype(f).reshape(P, 4 * T),
    }


INPUTS = ["x", "c", "ctx", "c_ctx", "w_mod", "b_mod", "mix0_w_in", "mla_g_q", "mla_w_uq", "mla_g_kv", "mla_w_uk",
          "mla_w_uv", "pool_w", "pool_scale", "mix0_w_out", "gqa_w_in", "gqa_g_q", "gqa_g_k", "gqa_w_out",
          "ffn_w_up", "ffn_conv_w", "ffn_conv_b", "ffn_w_down", "g_final", "positions_2", "w_in_2",
          "lambda_q1_2", "lambda_k1_2", "lambda_q2_2", "lambda_k2_2", "g_subln_2", "w_proj_a_2", "w_proj_b_2",
          "w_out_2", "w_gu1_2", "w_down1_2", "w_gu2_2", "w_down2_2", "g_pre_ffn1_2", "g_post_ffn1_2",
          "g_pre_mix_2", "g_post_mix_2", "g_pre_ffn2_2", "g_post_ffn2_2"]


def kernel(**inputs):
    import concourse.bacc as bacc
    from concourse.bass_utils import run_bass_kernel_spmd

    nc = bacc.Bacc("TRN2", target_bir_lowering=False, num_devices=1)
    arrays, aps = {}, {}
    for name, value in [(n, inputs[n]) for n in INPUTS] + list(shape_constants().items()):
        value = np.ascontiguousarray(value)
        if name == "ffn_conv_w":
            value = value.reshape(value.shape[0], 1, -1)
        arrays[f"in_{name}"] = value
        aps[name] = nc.dram_tensor(f"in_{name}", value.shape, mybir.dt.from_np(value.dtype),
                                   kind="ExternalInput").ap()
    out = nc.dram_tensor("out", (1, T, D), F32, kind="ExternalOutput").ap()
    build(nc, aps, out)
    result = run_bass_kernel_spmd(nc, [arrays], core_ids=[0])
    return result.results[0]["out"]
```
